# Optimizing a Trainium2 kernel written in Bass

```python
import jax, jax.numpy as jnp
from jax import lax
import numpy as np
import math

D_MODEL = 1024
BATCH = 1
SEQ = 512
DEPTH = 1

CHUNK = 64
Q_BLOCK = 128
CONV_DIM = D_MODEL // 2
CONV_WIDTH = 3
N_HEADS = 8
NOPE_DIM = 64
ROPE_DIM = 32
V_DIM = 64
Q_LORA = 384
KV_LORA = 256
ROPE_THETA = 10000.0
D_FF = 2816
PLE_DIM = 256
EPS = 1e-6

QK_DIM = NOPE_DIM + ROPE_DIM
SPLIT_SIZES = (CONV_DIM, CONV_DIM, CONV_DIM, Q_LORA, KV_LORA, ROPE_DIM, D_MODEL, D_MODEL)
N_IN = CONV_DIM * 3 + Q_LORA + KV_LORA + ROPE_DIM + 2 * D_MODEL


def _rmsnorm(x, g):
    xf = x.astype(jnp.float32)
    y = xf * lax.rsqrt(jnp.mean(xf * xf, axis=-1, keepdims=True) + EPS)
    return (y * g.astype(jnp.float32)).astype(x.dtype)

def _causal_dwconv3(x, w):
    s = x.shape[1]
    xp = jnp.pad(x, ((0, 0), (CONV_WIDTH - 1, 0), (0, 0)))
    return xp[:, 0:s] * w[0] + xp[:, 1:s + 1] * w[1] + xp[:, 2:s + 2] * w[2]

def _rope(x, positions):
    half = ROPE_DIM // 2
    inv = 1.0 / (ROPE_THETA ** (jnp.arange(half, dtype=jnp.float32) * (2.0 / ROPE_DIM)))
    ang = positions.astype(jnp.float32)[..., None] * inv
    cos = jnp.cos(ang)[:, :, None, :]
    sin = jnp.sin(ang)[:, :, None, :]
    xf = x.astype(jnp.float32)
    x1, x2 = xf[..., :half], xf[..., half:]
    return jnp.concatenate([x1 * cos - x2 * sin, x2 * cos + x1 * sin], axis=-1).astype(x.dtype)

def _chunk_causal_attention(q, k, v):
    bsz, s, h, dqk = q.shape
    nblk = s // Q_BLOCK
    scale = dqk ** -0.5
    k_chunk = jnp.arange(s) // CHUNK
    qb = q.reshape(bsz, nblk, Q_BLOCK, h, dqk).transpose(1, 0, 2, 3, 4)
    kf = k.astype(jnp.float32)
    vf = v.astype(jnp.float32)
    neg = jnp.finfo(jnp.float32).min

    def one_block(args):
        qi, bi = args
        q_chunk = (bi * Q_BLOCK + jnp.arange(Q_BLOCK)) // CHUNK
        mask = k_chunk[None, :] <= q_chunk[:, None]
        sc = jnp.einsum('bqhd,bkhd->bhqk', qi.astype(jnp.float32), kf) * scale
        sc = jnp.where(mask[None, None], sc, neg)
        pr = jax.nn.softmax(sc, axis=-1)
        return jnp.einsum('bhqk,bkhd->bqhd', pr, vf)

    out = lax.map(one_block, (qb, jnp.arange(nblk)))
    return out.transpose(1, 0, 2, 3, 4).reshape(bsz, s, h, v.shape[-1]).astype(v.dtype)

def first_inputs(seed: int = 0) -> dict:
    key = jax.random.key(seed)
    ks = jax.random.split(key, 32)
    L = DEPTH
    f32 = jnp.float32

    def w(k, shape, fan_in):
        return jax.random.normal(k, shape, f32) * (fan_in ** -0.5)

    def gain(k, shape):
        return 1.0 + 0.05 * jax.random.normal(k, shape, f32)

    x = jax.random.normal(ks[0], (BATCH, SEQ, D_MODEL), f32)
    p = jax.random.normal(ks[1], (DEPTH, BATCH, SEQ, PLE_DIM), f32)
    offset = jax.random.randint(ks[2], (BATCH, 1), 0, 4096, dtype=jnp.int32)
    positions = offset + jnp.arange(SEQ, dtype=jnp.int32)[None, :]
    return {
        "x": x,
        "p": p,
        "positions": positions,
        "g_mix_pre": gain(ks[3], (L, D_MODEL)),
        "w_in": w(ks[4], (L, D_MODEL, N_IN), D_MODEL),
        "conv_a_w": w(ks[5], (L, CONV_WIDTH, CONV_DIM), CONV_WIDTH),
        "w_a_out": w(ks[6], (L, CONV_DIM, D_MODEL), CONV_DIM),
        "g_q_lat": gain(ks[7], (L, Q_LORA)),
        "w_q_up": w(ks[8], (L, Q_LORA, N_HEADS * QK_DIM), Q_LORA),
        "g_kv_lat": gain(ks[9], (L, KV_LORA)),
        "w_kv_up": w(ks[10], (L, KV_LORA, N_HEADS * (NOPE_DIM + V_DIM)), KV_LORA),
        "w_b_out": w(ks[11], (L, N_HEADS * V_DIM, D_MODEL), N_HEADS * V_DIM),
        "w_o": w(ks[12], (L, D_MODEL, D_MODEL), D_MODEL),
        "g_mix_post": gain(ks[13], (L, D_MODEL)),
        "g_ffn_pre": gain(ks[14], (L, D_MODEL)),
        "w_ffn_up": w(ks[15], (L, D_MODEL, 2 * D_FF), D_MODEL),
        "conv_ffn_w": w(ks[16], (L, CONV_WIDTH, 2 * D_FF), CONV_WIDTH),
        "b_ffn_conv": 0.01 * jax.random.normal(ks[17], (L, 2 * D_FF), f32),
        "w_ffn_down": w(ks[18], (L, D_FF, D_MODEL), D_FF),
        "g_ffn_post": gain(ks[19], (L, D_MODEL)),
        "w_ple_proj": w(ks[20], (L, PLE_DIM, D_MODEL), PLE_DIM),
        "w_ple_gate": w(ks[21], (L, D_MODEL, D_MODEL), D_MODEL),
        "g_ple_post": gain(ks[22], (L, D_MODEL)),
    }

def first_block(x, p, positions, g_mix_pre, w_in, conv_a_w, w_a_out, g_q_lat, w_q_up,
              g_kv_lat, w_kv_up, w_b_out, w_o, g_mix_post, g_ffn_pre, w_ffn_up,
              conv_ffn_w, b_ffn_conv, w_ffn_down, g_ffn_post, w_ple_proj, w_ple_gate,
              g_ple_post):
    bsz, s, _ = x.shape
    split_pts = list(np.cumsum(SPLIT_SIZES)[:-1])
    h = x
    for i in range(DEPTH):
        u = _rmsnorm(h, g_mix_pre[i])
        z = u @ w_in[i]
        a_b, a_c, a_x, q_lat, kv_lat, k_rope, gate_a, gate_b = jnp.split(z, split_pts, axis=-1)

        ya = a_b * _causal_dwconv3(a_c * a_x, conv_a_w[i])
        ya = ya @ w_a_out[i]

        q = (_rmsnorm(q_lat, g_q_lat[i]) @ w_q_up[i]).reshape(bsz, s, N_HEADS, QK_DIM)
        kv = (_rmsnorm(kv_lat, g_kv_lat[i]) @ w_kv_up[i]).reshape(bsz, s, N_HEADS, NOPE_DIM + V_DIM)
        q_nope, q_pe = q[..., :NOPE_DIM], q[..., NOPE_DIM:]
        k_nope, v = kv[..., :NOPE_DIM], kv[..., NOPE_DIM:]
        q_pe = _rope(q_pe, positions)
        k_pe = _rope(k_rope[:, :, None, :], positions)
        q_full = jnp.concatenate([q_nope, q_pe], axis=-1)
        k_full = jnp.concatenate(
            [k_nope, jnp.broadcast_to(k_pe, (bsz, s, N_HEADS, ROPE_DIM))], axis=-1)
        ob = _chunk_causal_attention(q_full, k_full, v).reshape(bsz, s, N_HEADS * V_DIM)
        yb = ob @ w_b_out[i]

        mixed = jax.nn.sigmoid(gate_a) * ya + jax.nn.sigmoid(gate_b) * yb
        h = h + _rmsnorm(mixed @ w_o[i], g_mix_post[i])

        u2 = _rmsnorm(h, g_ffn_pre[i])
        up = _causal_dwconv3(u2 @ w_ffn_up[i], conv_ffn_w[i]) + b_ffn_conv[i]
        f_gate, f_val = up[..., :D_FF], up[..., D_FF:]
        f = (jax.nn.gelu(f_gate, approximate=True) * f_val) @ w_ffn_down[i]
        h = h + _rmsnorm(f, g_ffn_post[i])

        e = p[i] @ w_ple_proj[i]
        g = jax.nn.sigmoid(h @ w_ple_gate[i])
        h = h + _rmsnorm(e * g, g_ple_post[i])
    return h


DEPTH_2 = 2

N_MIXERS = 3
EXPAND = 2
D_INNER = EXPAND * D_MODEL
GLA_HEADS = 4
GLA_DK = D_MODEL // GLA_HEADS
GLA_DV = D_INNER // GLA_HEADS
GLA_RANK = 16
GLA_GATE_NORM = 16.0
GLA_CHUNK = 64
DSA_HEADS = 16
DSA_HEAD_DIM = D_INNER // DSA_HEADS
IDX_HEADS = 8
IDX_DIM = 64
TOPK_MAX = 256
ATTN_SCALE = DSA_HEAD_DIM ** -0.5
INDEX_SCALE = (IDX_HEADS ** -0.5) * (IDX_DIM ** -0.5)
CONV_WIDTH_2 = 31
ROPE_THETA_2 = 500000.0
DSA_ROT_DIM = DSA_HEAD_DIM // 4
IDX_ROT_DIM = IDX_DIM // 4
ALPHA = (2 * DEPTH_2) ** 0.25
BETA = (8 * DEPTH_2) ** -0.25
NORM_EPS = 1e-5

GLA_IN = 2 * GLA_HEADS * GLA_DK + 2 * D_INNER + GLA_RANK
DSA_IN = 2 * D_INNER + 2 * DSA_HEAD_DIM + IDX_HEADS * IDX_DIM + IDX_DIM + IDX_HEADS
CONV_IN = 3 * D_INNER


def layer_norm(x, g, b):
    xf = x.astype(jnp.float32)
    mu = jnp.mean(xf, axis=-1, keepdims=True)
    var = jnp.mean(jnp.square(xf - mu), axis=-1, keepdims=True)
    return ((xf - mu) * lax.rsqrt(var + NORM_EPS) * g + b).astype(x.dtype)

def rope_tables(positions, rot_dim):
    inv_freq = ROPE_THETA_2 ** (-jnp.arange(0, rot_dim, 2, dtype=jnp.float32) / rot_dim)
    ang = positions.astype(jnp.float32)[..., None] * inv_freq
    return jnp.cos(ang), jnp.sin(ang)

def apply_partial_rope(x, cos, sin):
    half = cos.shape[-1]
    rot = 2 * half
    bshape = cos.shape[:2] + (1,) * (x.ndim - 3) + (half,)
    c = cos.reshape(bshape)
    s = sin.reshape(bshape)
    x1 = x[..., :half].astype(jnp.float32)
    x2 = x[..., half:rot].astype(jnp.float32)
    rotated = jnp.concatenate([x1 * c - x2 * s, x2 * c + x1 * s], axis=-1).astype(x.dtype)
    return jnp.concatenate([rotated, x[..., rot:]], axis=-1)

def gla_mixer(x, w_in, w_a2, b_a, gn_g, w_out):
    B, L, _ = x.shape
    n = L // GLA_CHUNK
    qk = GLA_HEADS * GLA_DK
    h = x @ w_in
    q = h[..., :qk]
    k = h[..., qk:2 * qk]
    v = h[..., 2 * qk:2 * qk + D_INNER]
    z = h[..., 2 * qk + D_INNER:2 * qk + 2 * D_INNER]
    a = h[..., 2 * qk + 2 * D_INNER:]
    g = jax.nn.log_sigmoid((a @ w_a2 + b_a).astype(jnp.float32)) / GLA_GATE_NORM

    def chunk(t, d):
        return t.astype(jnp.float32).reshape(B, n, GLA_CHUNK, GLA_HEADS, d)

    q, k, g, v = chunk(q, GLA_DK), chunk(k, GLA_DK), chunk(g, GLA_DK), chunk(v, GLA_DV)
    G = jnp.cumsum(g, axis=2)
    G_last = G[:, :, -1:]
    q_t = q * (GLA_DK ** -0.5) * jnp.exp(G)
    k_t = k * jnp.exp(-G)
    k_s = k * jnp.exp(G_last - G)
    pos = jnp.arange(GLA_CHUNK)
    tril = pos[:, None] >= pos[None, :]
    A = jnp.where(tril, jnp.einsum('bnihd,bnjhd->bnhij', q_t, k_t), 0.0)
    o_intra = jnp.einsum('bnhij,bnjhv->bnihv', A, v)

    def step(S, inp):
        q_c, k_c, v_c, decay = inp
        o_c = jnp.einsum('bihd,bhdv->bihv', q_c, S)
        S = S * decay[..., None] + jnp.einsum('bjhd,bjhv->bhdv', k_c, v_c)
        return S, o_c

    S0 = jnp.zeros((B, GLA_HEADS, GLA_DK, GLA_DV), jnp.float32)
    xs = (jnp.moveaxis(q_t, 1, 0), jnp.moveaxis(k_s, 1, 0), jnp.moveaxis(v, 1, 0),
          jnp.moveaxis(jnp.exp(G_last[:, :, 0]), 1, 0))
    _, o_inter = lax.scan(step, S0, xs)
    o = o_intra + jnp.moveaxis(o_inter, 0, 1)
    o = o * lax.rsqrt(jnp.mean(o * o, axis=-1, keepdims=True) + NORM_EPS)
    o = o.reshape(B, L, D_INNER) * gn_g
    return (o.astype(x.dtype) * jax.nn.silu(z)) @ w_out

def dsa_mixer(x, cos_h, sin_h, cos_i, sin_i, w_in, w_out):
    B, L, _ = x.shape
    topk = min(TOPK_MAX, L // 4)
    nb = L // Q_BLOCK
    h = x @ w_in
    o1 = D_INNER
    o2 = o1 + DSA_HEAD_DIM
    o3 = o2 + DSA_HEAD_DIM
    o4 = o3 + D_INNER
    o5 = o4 + IDX_HEADS * IDX_DIM
    o6 = o5 + IDX_DIM
    q = apply_partial_rope(h[..., :o1].reshape(B, L, DSA_HEADS, DSA_HEAD_DIM), cos_h, sin_h)
    k = apply_partial_rope(h[..., o1:o2], cos_h, sin_h)
    v = h[..., o2:o3]
    z = h[..., o3:o4]
    qi = apply_partial_rope(h[..., o4:o5].reshape(B, L, IDX_HEADS, IDX_DIM), cos_i, sin_i)
    ki = apply_partial_rope(h[..., o5:o6], cos_i, sin_i)
    wi = h[..., o6:]
    gather = jax.vmap(lambda arr, ids: arr[ids])
    s_pos = jnp.arange(L, dtype=jnp.int32)

    def to_blocks(t):
        return jnp.moveaxis(t.reshape((B, nb, Q_BLOCK) + t.shape[2:]), 1, 0)

    def attend_block(args):
        q_b, qi_b, wi_b, start = args
        t_pos = start + jnp.arange(Q_BLOCK, dtype=jnp.int32)
        rel = jax.nn.relu(jnp.einsum('bthd,bsd->bths', qi_b, ki).astype(jnp.float32))
        score = jnp.einsum('bths,bth->bts', rel, wi_b.astype(jnp.float32)) * INDEX_SCALE
        causal = s_pos[None, :] <= t_pos[:, None]
        score = jnp.where(causal[None], score, -jnp.inf)
        _, idx = lax.top_k(score, topk)
        valid = idx <= t_pos[None, :, None]
        k_sel = gather(k, idx)
        v_sel = gather(v, idx)
        logits = jnp.einsum('bthd,btjd->bthj', q_b, k_sel).astype(jnp.float32) * ATTN_SCALE
        logits = jnp.where(valid[:, :, None, :], logits, -jnp.inf)
        probs = jax.nn.softmax(logits, axis=-1).astype(v.dtype)
        return jnp.einsum('bthj,btjd->bthd', probs, v_sel)

    starts = jnp.arange(nb, dtype=jnp.int32) * Q_BLOCK
    o = lax.map(attend_block, (to_blocks(q), to_blocks(qi), to_blocks(wi), starts))
    o = jnp.moveaxis(o, 0, 1).reshape(B, L, D_INNER)
    return (o * jax.nn.silu(z)) @ w_out

def conformer_conv_mixer(x, w_in, dw_w, dw_b, ln_g, ln_b, w_out):
    h = x @ w_in
    a, gate, z = jnp.split(h, 3, axis=-1)
    u = a * jax.nn.sigmoid(gate)
    u = lax.conv_general_dilated(u, dw_w[:, None, :], window_strides=(1,),
                                 padding=[(CONV_WIDTH_2 - 1, 0)],
                                 dimension_numbers=('NWC', 'WIO', 'NWC'),
                                 feature_group_count=D_INNER) + dw_b
    u = jax.nn.silu(layer_norm(u, ln_g, ln_b))
    return (u * jax.nn.silu(z)) @ w_out

def second_inputs(seed: int = 0) -> dict:
    key = jax.random.key(seed)
    ks = jax.random.split(key, 24)
    n_gla = len(range(0, DEPTH_2, N_MIXERS))
    n_dsa = len(range(1, DEPTH_2, N_MIXERS))
    n_conv = len(range(2, DEPTH_2, N_MIXERS))

    def normal(k, shape, scale):
        return jax.random.normal(k, shape, jnp.float32) * scale

    x = normal(ks[0], (BATCH, SEQ, D_MODEL), 1.0)
    p = normal(ks[1], (DEPTH_2, BATCH, SEQ, PLE_DIM), 1.0)
    offsets = jax.random.randint(ks[2], (BATCH, 1), 0, 1024, dtype=jnp.int32)
    positions = offsets + jnp.arange(SEQ, dtype=jnp.int32)[None, :]
    return {
        'x': x,
        'p': p,
        'positions': positions,
        'gla_w_in': normal(ks[3], (n_gla, D_MODEL, GLA_IN), D_MODEL ** -0.5),
        'gla_w_a2': normal(ks[4], (n_gla, GLA_RANK, GLA_HEADS * GLA_DK), GLA_RANK ** -0.5),
        'gla_b_a': normal(ks[5], (n_gla, GLA_HEADS * GLA_DK), 0.1),
        'gla_gn_g': 1.0 + normal(ks[6], (n_gla, D_INNER), 0.02),
        'gla_w_out': normal(ks[7], (n_gla, D_INNER, D_MODEL), BETA * D_INNER ** -0.5),
        'dsa_w_in': normal(ks[8], (n_dsa, D_MODEL, DSA_IN), D_MODEL ** -0.5),
        'dsa_w_out': normal(ks[9], (n_dsa, D_INNER, D_MODEL), BETA * D_INNER ** -0.5),
        'conv_w_in': normal(ks[10], (n_conv, D_MODEL, CONV_IN), D_MODEL ** -0.5),
        'conv_dw_w': normal(ks[11], (n_conv, CONV_WIDTH_2, D_INNER), CONV_WIDTH_2 ** -0.5),
        'conv_dw_b': normal(ks[12], (n_conv, D_INNER), 0.02),
        'conv_ln_g': 1.0 + normal(ks[13], (n_conv, D_INNER), 0.02),
        'conv_ln_b': normal(ks[14], (n_conv, D_INNER), 0.02),
        'conv_w_out': normal(ks[15], (n_conv, D_INNER, D_MODEL), BETA * D_INNER ** -0.5),
        'ln_g': 1.0 + normal(ks[16], (DEPTH_2, D_MODEL), 0.02),
        'ln_b': normal(ks[17], (DEPTH_2, D_MODEL), 0.02),
        'ple_w': normal(ks[18], (DEPTH_2, PLE_DIM, D_MODEL), 0.5 * PLE_DIM ** -0.5),
        'ple_gate_w': normal(ks[19], (DEPTH_2, D_MODEL, D_MODEL), D_MODEL ** -0.5),
    }

def second_block(x, p, positions, gla_w_in, gla_w_a2, gla_b_a, gla_gn_g, gla_w_out,
              dsa_w_in, dsa_w_out, conv_w_in, conv_dw_w, conv_dw_b, conv_ln_g, conv_ln_b,
              conv_w_out, ln_g, ln_b, ple_w, ple_gate_w):
    cos_h, sin_h = rope_tables(positions, DSA_ROT_DIM)
    cos_i, sin_i = rope_tables(positions, IDX_ROT_DIM)
    for i in range(DEPTH_2):
        kind = i % N_MIXERS
        j = i // N_MIXERS
        if kind == 0:
            y = gla_mixer(x, gla_w_in[j], gla_w_a2[j], gla_b_a[j], gla_gn_g[j], gla_w_out[j])
        elif kind == 1:
            y = dsa_mixer(x, cos_h, sin_h, cos_i, sin_i, dsa_w_in[j], dsa_w_out[j])
        else:
            y = conformer_conv_mixer(x, conv_w_in[j], conv_dw_w[j], conv_dw_b[j],
                                     conv_ln_g[j], conv_ln_b[j], conv_w_out[j])
        x = layer_norm(ALPHA * x + y, ln_g[i], ln_b[i])
        x = x + (p[i] @ ple_w[i]) * jax.nn.sigmoid(x @ ple_gate_w[i])
    return x


def setup_inputs(seed=0):
    out = dict(first_inputs(seed))
    for name, value in second_inputs(seed + 1).items():
        if name != "x":
            out[name + "_2"] = value
    return out


def reference(
    x, p, positions, g_mix_pre, w_in, conv_a_w, w_a_out, g_q_lat, w_q_up, g_kv_lat, w_kv_up,
    w_b_out, w_o, g_mix_post, g_ffn_pre, w_ffn_up, conv_ffn_w, b_ffn_conv, w_ffn_down,
    g_ffn_post, w_ple_proj, w_ple_gate, g_ple_post, p_2, positions_2, gla_w_in_2, gla_w_a2_2,
    gla_b_a_2, gla_gn_g_2, gla_w_out_2, dsa_w_in_2, dsa_w_out_2, conv_w_in_2, conv_dw_w_2,
    conv_dw_b_2, conv_ln_g_2, conv_ln_b_2, conv_w_out_2, ln_g_2, ln_b_2, ple_w_2, ple_gate_w_2,
):
    x = first_block(
        x, p, positions, g_mix_pre, w_in, conv_a_w, w_a_out, g_q_lat, w_q_up, g_kv_lat, w_kv_up,
        w_b_out, w_o, g_mix_post, g_ffn_pre, w_ffn_up, conv_ffn_w, b_ffn_conv, w_ffn_down,
        g_ffn_post, w_ple_proj, w_ple_gate, g_ple_post,
    )
    return second_block(
        x, p_2, positions_2, gla_w_in_2, gla_w_a2_2, gla_b_a_2, gla_gn_g_2, gla_w_out_2,
        dsa_w_in_2, dsa_w_out_2, conv_w_in_2, conv_dw_w_2, conv_dw_b_2, conv_ln_g_2,
        conv_ln_b_2, conv_w_out_2, ln_g_2, ln_b_2, ple_w_2, ple_gate_w_2,
    )


_drawn_inputs = setup_inputs


def setup_inputs(seed=0):
    import zlib

    import numpy as np

    out = dict(_drawn_inputs(seed))
    spreads = {}
    factors = {'g_q_lat': 8.0,
     'g_kv_lat': 7.359,
     'b_ffn_conv': 7.149,
     'gla_b_a_2': 7.194,
     'gla_gn_g_2': 8.0}
    for name, (base, spread) in spreads.items():
        noise = np.random.default_rng([zlib.crc32(name.encode()), seed]).standard_normal(out[name].shape)
        drawn = base * np.exp(spread * noise) if base else spread * noise
        out[name] = __import__('jax').numpy.asarray(drawn.astype(out[name].dtype))
    for name, factor in factors.items():
        out[name] = (out[name] * factor).astype(out[name].dtype)
    return out
```

```python
import numpy as np
from contextlib import ExitStack

import concourse.bass as bass
from concourse import mybir

F32 = mybir.dt.float32
F32R = mybir.dt.float32r
I32 = mybir.dt.int32
U32 = mybir.dt.uint32
ACT = mybir.ActivationFunctionType
ALU = mybir.AluOpType
AX = mybir.AxisListType

P = 128
T = 512
QT = T // P
D = 1024
KD = D // P
CONV = 512
JC = CONV // P
NH, NOPE, ROPE, VD = 8, 64, 32, 64
QL, KVL = 384, 256
DFF = 2816
JF = DFF // P
HJ = JF // 2
PLE = 256
EPS = 1e-6
MLA_SCALE = (NOPE + ROPE) ** -0.5
THETA_1, THETA_2 = 10000.0, 500000.0
DI = 2048
GH, GDK, GDV, GRANK = 4, 256, 512, 16
GATE_NORM = 16.0
CHUNK = 64
DH, DHD = 16, 128
IH, ID = 8, 64
TOPK = 128
DSA_SCALE = DHD ** -0.5
INDEX_SCALE = (IH ** -0.5) * (ID ** -0.5)
ALPHA = 4 ** 0.25
NORM_EPS = 1e-5
MASKED = -1.0e30
TAKEN = -3.0e38

STAGES = [("lat", 6), ("mla", NH), ("conv", 3 * JC), ("mix", 3 * KD), ("wo", KD),
          ("up0", 2 * HJ), ("down0", 12), ("up1", 2 * HJ), ("down1", 12),
          ("ple1p", 2), ("ple1", KD),
          ("gla_a", 2), ("gla", 16 * GH), ("ple2p", 2), ("ple2", KD),
          ("idx", 8), ("dsa_z", DH), ("dsa0", DH // 2), ("dout0", KD), ("dsa1", DH // 2), ("dout1", KD),
          ("ple3p", 2), ("ple3", KD)]
U0 = {}
_n = 0
for _name, _count in STAGES:
    U0[_name] = _n
    _n += _count
UNITS = _n
RAW = 4
SLOTS = 2

GAIN_COLS = [("g_mix_pre", KD), ("g_q_lat", QL // P), ("g_kv_lat", KVL // P), ("g_mix_post", KD),
             ("g_ffn_pre", KD), ("g_ffn_post", KD), ("g_ple_post", KD), ("conv_a_w", 3 * JC),
             ("conv_ffn_w", 3 * 2 * JF), ("b_ffn_conv", 2 * JF), ("gla_b_a_2", KD), ("gla_gn_g_2", DI // P),
             ("ln_g_2", 2 * KD), ("ln_b_2", 2 * KD)]
G0 = {}
_n = 0
for _name, _count in GAIN_COLS:
    G0[_name] = _n
    _n += _count
GAINS = _n

CONST_COLS = [("ident", P), ("ones", T), ("mla_bias", T), ("causal", T), ("tri", P), ("reset", T),
              ("inv_freq", 3), ("sign", 3), ("eps", 1), ("eps_ln", 1), ("one", 1)]
C0 = {}
_n = 0
for _name, _count in CONST_COLS:
    C0[_name] = _n
    _n += _count
CONSTS = _n


PI = float(np.nextafter(np.float32(np.pi), np.float32(0)))
TURN = (6.28125, 0.001934051513671875, 2 * np.pi - 6.28125 - 0.001934051513671875)


class Steps:

    def __init__(self, sem, names, n=1):
        self.sem, self.names, self.n = sem, names, n
        self.per = len(names)
        self.credit = max(self.per, 1)
        self.total = self.credit + n * self.per
        self.next = 0

    def at(self, name, i=0):
        return i * self.per + (self.credit + self.names.index(name) + 1)

    def done(self, ins, name):
        assert self.names[self.next] == name, (self.names[self.next], name)
        self.next = (self.next + 1) % self.per
        ins.then_inc(self.sem, 1)


def q_span(j):
    start = sum(T - (P * m + CHUNK) for m in range(j))
    return start, T - (P * j + CHUNK)


GLA_BANK = [(5, 0), (6, 0), (6, q_span(1)[1]), (5, q_span(0)[1])]
GLA_PACK = [sum(T - P * m for m in range(j)) for j in range(QT)]
GLA_AT = sum(T - P * m for m in range(QT))


def build(nc, ins, out):
    ctx = ExitStack()
    with ctx:
        def sb(name, shape, dt):
            return ctx.enter_context(nc.sbuf_tensor(name, shape, dt))

        def sem(name):
            return ctx.enter_context(nc.semaphore(name))

        raw = sb("raw", [P, RAW, 8 * P], F32)
        w_hi = sb("w_hi", [P, SLOTS, 8, P], F32R)
        w_lo = sb("w_lo", [P, SLOTS, 8, P], F32R)
        op_hi = sb("op_hi", [P, KD, T], F32R)
        op_lo = sb("op_lo", [P, KD, T], F32R)
        fb = sb("fb", [P, 24, T], F32)
        h = fb[:, 0:8, :]
        ebuf = fb[:, 8:16, :]
        fbuf = fb[:, 16:24, :]
        r2 = sb("r2", [P, 32 * T], F32R)
        fx = sb("fx", [P, 12, T], F32)
        rope_cos = sb("rope_cos", [P, 3, T], F32)
        rope_sin = sb("rope_sin", [P, 3, T], F32)
        cst = sb("cst", [P, CONSTS], F32)
        gain = sb("gain", [P, GAINS], F32)
        st = sb("st", [P, 64], F32)
        ps = [ctx.enter_context(nc.psum_tensor(f"bank{b}", [P, T], F32)) for b in range(8)]

        def const(name):
            width = dict(CONST_COLS)[name]
            return cst[:, C0[name]:C0[name] + width]

        def gcol(name, i):
            return gain[:, bass.ds(G0[name] + i, 1)]

        ident, ones = const("ident"), const("ones")[:, 0:P]
        rs, acc, sq = fx[:, 0, :], fx[:, 1, :], fx[:, 2, :]

        def pair(at, n):
            a = r2[:, at * T:(at + n) * T].rearrange("p (k t) -> p k t", t=T)
            b = r2[:, (at + n) * T:(at + 2 * n) * T].rearrange("p (k t) -> p k t", t=T)
            return a, b

        ob_hi, ob_lo = pair(0, 4)
        qn_hi, qn_lo = pair(8, 3)
        kvn_hi, kvn_lo = pair(14, 2)
        aq_hi, aq_lo = pair(18, 1)
        ak_hi, ak_lo = pair(20, 2)
        av_hi, av_lo = pair(24, 1)
        apt_hi, apt_lo = pair(26, 2)
        ya_hi, ya_lo = pair(8, 4)
        mix_hi, mix_lo = pair(16, 8)
        f_hi, f_lo = pair(0, HJ)
        p_hi, p_lo = pair(24, 2)
        go_hi, go_lo = pair(0, 4)
        gv_hi, gv_lo = pair(8, 4)
        at_hi, at_lo = pair(16, 3)
        ga_hi, ga_lo = pair(22, 5)
        oz_hi, oz_lo = pair(0, 8)
        qi_hi, qi_lo = pair(0, 4)
        ki_hi, ki_lo = pair(8, 2)
        dpt_hi, dpt_lo = pair(16, 2)
        dq_hi, dq_lo = pair(20, 1)
        dk_hi, dk_lo = pair(22, 1)
        dv_hi, dv_lo = pair(24, 1)

        landed = [sem(f"landed{r}") for r in range(RAW)]
        hi_ready = sem("hi_ready")
        split_ready = sem("split_ready")
        unit_done = sem("unit_done")
        x_in, p_in, pos_in, cst_in, out_sem = sem("x_in"), sem("p_in"), sem("pos_in"), sem("cst_in"), sem("out_sem")

        pool_held, dve_held = sem("pool_held"), sem("dve_held")
        cleared = sem("cleared")
        S = {}

        def stage(name, n, act, dve, pe):
            S[name] = {"act": Steps(sem(f"act_{name}"), act, n), "dve": Steps(sem(f"dve_{name}"), dve, n),
                       "pe": Steps(sem(f"pe_{name}"), pe, n)}

        M8 = range(KD)
        stage("start", 1,
              [f"{a}{m}" for m in M8 for a in ("hi", "sq")] + ["sqrt", "sin", "abs", "cos"],
              [f"{a}{m}" for m in M8 for a in ("lo", "acc")] + ["rs", "pos", "ang0", "ang1", "ang2",
               "turn", "whole", "red1", "red2", "red3", "clip", "quarter", "sin0", "sin1", "sin2"],
              ["sum"])
        LB = range(5)
        stage("lat", 1,
              [f"sq{b}" for b in LB] + ["sqrt_q", "sqrt_kv"] + [f"hi{b}" for b in LB] + ["k0h", "k1h"],
              [f"z{b}" for b in LB[:3]] + [f"acc{b}" for b in LB[:3]] + [f"z{b}" for b in LB[3:]] + ["kr"] + ["rs_q"]
              + [f"acc{b}" for b in LB[3:]] + ["rs_kv"]
              + [x for b in LB for x in (f"n{b}", f"lo{b}")] + ["swap", "swap_sin", "kr_cos", "kr_rot", "k0l", "k1l"],
              ["sum_q", "sum_kv"])
        H2 = range(2)

        def soft_act(x):
            return [f"{a}{x}" for a in ("e0", "e1", "h0", "e2", "h1", "e3", "h2", "h3")]

        def soft_dve(x):
            o = []
            for q in range(QT):
                o += [f"m{q}{x}", f"r{q}{x}", f"n{q}{x}"]
                if q:
                    o.append(f"l{q - 1}{x}")
            return o + [f"l3{x}"]

        def soft_pe(x):
            return [f"{a}{x}" for a in ("s0", "s1", "t0", "s2", "t1", "o0", "s3", "t2", "o1", "t3", "o2", "o3")]

        stage("mla", NH // 2,
              sum([[f"qf{x}", f"kh{x}", f"vh{x}", f"qh{x}"] + soft_act(x) + [f"oh{x}"] for x in "ab"], []),
              sum([[f"sw{x}", f"ss{x}", f"qc{x}", f"qa{x}", f"kl{x}", f"vl{x}", f"ql{x}"] + soft_dve(x) + [f"ol{x}"]
                   for x in "ab"], []),
              sum([[f"q{x}", f"k{x}"] + soft_pe(x) for x in "ab"], []))
        stage("conv", JC // 2,
              sum([[f"hi{x}"] for x in "ab"], []),
              sum([[f"{a}{x}" for a in ("ac", "ax", "c", "ab", "y0", "y1", "y2", "ya", "lo")] for x in "ab"], []), [])
        stage("mix", KD // 2,
              sum([[f"sa{x}", f"sb{x}", f"hi{x}"] for x in "ab"], []),
              sum([[f"{a}{x}" for a in ("ga", "gb", "ma", "mb", "mx", "lo")] for x in "ab"], []), [])
        stage("wo", KD // 2, sum([[f"f{x}", f"sq{x}"] for x in "ab"], []), [f"acc{x}" for x in "ab"], [])
        stage("res1", 1, ["sqrt"] + [f"{a}{m}" for m in M8 for a in ("hi", "sq")] + ["sqrt2"],
              ["rs"] + [f"{a}{m}" for m in M8 for a in ("sc", "h", "lo", "acc")] + ["rs2"], ["sum", "sum2"])
        for half in (0, 1):
            stage(f"up{half}", HJ, ["ge", "hi"],
                  ["g", "g0", "g1", "g2", "v", "v0", "v1", "v2", "pr", "lo"], [])
            if half == 0:
                stage("down0", 2, [f"f{m}" for m in range(4)], [], [])
            else:
                stage("down1", 2, [f"sq{m}" for m in range(4)], [f"{a}{m}" for m in range(4) for a in ("f", "acc")], [])
        stage("ple1p", 1, ["ph"] + [f"e{m}" for m in M8], ["pl"], [f"e{m}" for m in M8 if m % 4 < 3])
        stage("res2", 1, ["sqrt"] + [f"hi{m}" for m in M8],
              ["rs"] + [f"{a}{m}" for m in M8 for a in ("sc", "h", "lo")], ["sum"])
        stage("ple1", KD // 2, sum([[f"g{x}", f"sq{x}"] for x in "ab"], []),
              sum([[f"e{x}", f"acc{x}"] for x in "ab"], []), [])
        stage("res3", 1, ["sqrt"] + [f"hi{m}" for m in M8],
              ["rs"] + [f"{a}{m}" for m in M8 for a in ("sc", "h", "lo")], ["sum"])
        stage("gla_a", 1, ["ah"] + [f"{a}{m}" for m in M8 for a in ("ab", "ex", "ln")],
              ["zero_y", "zero_at", "al"] + [f"{a}{m}" for m in M8 for a in ("mn", "g")], [f"a{m}" for m in range(KD - 1)])
        gla_act, gla_dve = ["q0", "q1", "k0", "k1"], []

        def gla_prep_act(b):
            return ([f"x{b}qt", f"h{b}qt", f"x{b}kt", f"h{b}kt"] + [f"x{b}s{j}" for j in range(QT)] + [f"h{b}ks"]
                    + [f"x{b}j{j}" for j in range(QT)] + [f"h{b}qj"])

        def gla_prep_dve(b):
            return ([f"s64{b}", f"sgl{b}", f"ne{b}", f"po{b}", f"m{b}qt", f"l{b}qt", f"m{b}kt", f"l{b}kt", f"m{b}ks", f"l{b}ks"]
                    + [f"m{b}j{j}" for j in range(QT)] + [f"l{b}qj"])

        gla_act += gla_prep_act(0) + [f"vh{t}" for t in range(QT)] + gla_prep_act(1) + [f"z{b}" for b in range(4)]
        gla_dve += gla_prep_dve(0) + [f"vl{t}" for t in range(QT)] + gla_prep_dve(1)
        gla_act += ["ath"] + [f"osq{b}" for b in range(4)] + ["osqrt"]
        gla_dve += [f"ad{j}" for j in range(QT)] + [f"{a}{j}" for j in range(QT) for a in ("ac", "ao")][:-1] + ["atl"]
        gla_dve += [f"oacc{b}" for b in range(4)] + ["ors"]
        for b in range(4):
            gla_dve += [f"on{b}", f"oz{b}", f"ol{b}"]
            gla_act += [f"oh{b}"]
        gla_dve += [f"y{m}" for m in M8]
        stage("gla", GH, gla_act, gla_dve, ["A0", "A1"] + [f"o{b}" for b in range(4)] + ["osum"] + [f"y{m}" for m in M8 if m % 2 == 0])

        def ln_stage(name):
            stage(name, 1, ["mu"] + [f"sq{m}" for m in M8] + ["sqrt"] + [f"hi{m}" for m in M8],
                  [x for m in M8 for x in (f"ta{m}", f"tb{m}", f"acc{m}")]
                  + [x for m in M8 for x in (f"c{m}", f"v{m}")] + ["rs"]
                  + [f"{a}{m}" for m in M8 for a in ("n", "x", "lo")], ["sum", "sum2"])

        def ple_stages(k):
            stage(f"ple{k}p", 1, ["ph"] + [f"e{m}" for m in M8], ["pl"], [f"e{m}" for m in M8 if m % 4 < 3])
            stage(f"ple{k}", KD // 2, [f"g{x}" for x in "ab"], [f"{a}{x}" for x in "ab" for a in ("e", "h")], [])

        ple_stages(2)
        ln_stage("ln1")
        stage("x2", 1, [f"hi{m}" for m in M8], [f"lo{m}" for m in M8], [])
        idx_act = ["qf0", "qf1", "hi0", "qf2", "hi1", "qf3", "hi2", "qf4", "hi3", "qf5", "kih0", "kih1", "kh", "vh", "wi"]
        idx_dve = [f"zero{n}" for n in range(4)]
        for b in range(6):
            idx_dve += [f"sw{b}", f"ss{b}", f"qc{b}", f"qa{b}"] + ([f"lo{b}"] if b < 4 else [["kil0", "kil1"], ["kl"]][b - 4])
        pairs = [(q, x) for q in range(1, QT) for x in range(IH)]
        stage("idx", 1, idx_act + [f"rel{q}{x}" for q, x in pairs],
              idx_dve + ["vl"] + [f"sc{q}{x}" for q, x in pairs] + [f"ca{q}" for q in range(1, QT)]
              + [f"{a}{q}_{r}" for q in range(1, QT) for r in range(TOPK // 8) for a in ("mx", "mr")]
              + [f"sel{q}" for q in range(1, QT)],
              [f"s{q}{x}" for q, x in pairs])
        stage("dsa_z", DH // 2, ["za", "zb"], [], [])
        for half in (0, 1):
            stage(f"dsa{half}", DH // 4,
                  sum([[f"qf{x}", f"qh{x}"] + soft_act(x) + [f"oh{x}"] for x in "ab"], []),
                  sum([[f"sw{x}", f"ss{x}", f"qc{x}", f"qa{x}", f"ql{x}"] + soft_dve(x) + [f"oz{x}", f"ol{x}"]
                       for x in "ab"], []),
                  sum([soft_pe(x) for x in "ab"], []))
            stage(f"dout{half}", KD // 2, ["fa", "fb"] if half == 0 else [], [] if half == 0 else ["fa", "fb"], [])
        ple_stages(3)
        ln_stage("ln2")

        ORDER = ["start", "lat", "mla", "conv", "mix", "wo", "res1", "up0", "down0", "up1", "down1", "ple1p", "res2",
                 "ple1", "res3", "gla_a", "gla", "ln1", "ple2p", "ple2", "x2", "idx", "dsa_z", "dsa0", "dout0", "dsa1",
                 "dout1", "ln2", "ple3p", "ple3"]

        def enter(eng, who, name):
            k = ORDER.index(name)
            if k:
                before = S[ORDER[k - 1]][who]
                eng.wait_ge(before.sem, before.total)
            if who == "pe":
                used = U0[name] if name in U0 else 0
                if used:
                    eng.wait_ge(unit_done, used)
            mine = S[name][who]
            eng.sem_inc(mine.sem, mine.credit)
            for other in ("act", "dve", "pe"):
                if other != who:
                    eng.wait_ge(S[name][other].sem, S[name][other].credit)
            return S[name]["act"], S[name]["dve"], S[name]["pe"]

        block = ctx.enter_context(nc.Block())

        @block.sync
        def _(sp):
            sp.dma_start(cst[:, :], ins["consts"]).then_inc(cst_in, 16)
            sp.dma_start(gain[:, :], ins["gains"]).then_inc(cst_in, 16)
            sp.dma_start(h, ins["x"].rearrange("k p t -> p k t")).then_inc(x_in, 16)
            for n, name in enumerate(("positions", "positions_2")):
                sp.dma_start(fx[:, 9 + n, :].bitcast(I32), ins[name].broadcast_to([P, T])).then_inc(pos_in, 16)

            def load(u, r):
                sp.dma_start(raw[:, r, :], ins["weights"][bass.ds(u, 1)].rearrange("a p n -> (a p) n")).then_inc(landed[r], 16)

            n = UNITS
            for u in range(min(RAW, n)):
                load(u, u)
            rounds = n // RAW
            if rounds > 1:
                with sp.Fori(1, rounds) as k:
                    for r in range(RAW):
                        sp.wait_ge(split_ready, k * RAW + (r - RAW + 1))
                        load(k * RAW + r, r)
            for u in range(max(rounds, 1) * RAW, n):
                sp.wait_ge(split_ready, u - RAW + 1)
                load(u, u % RAW)
            end = S[ORDER[-1]]
            for who in ("act", "dve", "pe"):
                sp.wait_ge(end[who].sem, end[who].total)
            sp.dma_start(out.rearrange("k p t -> p k t"), h).then_inc(out_sem, 16)
            sp.wait_ge(out_sem, 16)

        @block.gpsimd
        def _(pool):
            def split(u, k, r, free):
                s = r % SLOTS
                pool.wait_ge(landed[r], (k + 1) * 16)
                if free:
                    pool.wait_ge(unit_done, u - (SLOTS - 1))
                hi = w_hi[:, s].rearrange("p k n -> p (k n)")
                lo = w_lo[:, s].rearrange("p k n -> p (k n)")
                pool.sem_inc(pool_held, 1)
                pool.tensor_scalar(hi, raw[:, r, :], 1.0, 0.0, ALU.mult, ALU.add).then_inc(hi_ready, 1)
                pool.wait_ge(hi_ready, u + 1)
                pool.tensor_tensor(lo, raw[:, r, :], hi.bitcast(F32), ALU.subtract).then_inc(split_ready, 1)

            n = UNITS
            for u in range(min(RAW, n)):
                split(u, 0, u, u >= SLOTS)
            rounds = n // RAW
            if rounds > 1:
                with pool.Fori(1, rounds) as k:
                    for r in range(RAW):
                        split(k * RAW + r, k, r, True)
            for u in range(max(rounds, 1) * RAW, n):
                split(u, u // RAW, u % RAW, True)

        @block.tensor
        def _(pe):
            def split_mm(o, ah, al, bh, bl, start, stop, skip=False):
                pe.matmul(o, ah, bh, start=start, stop=False, skip_group_check=skip)
                pe.matmul(o, ah, bl, start=False, stop=False, skip_group_check=skip)
                return pe.matmul(o, al, bh, start=False, stop=stop, skip_group_check=skip)

            def blocks(o, s, kbs, xh, xl, stop=True, start=True):
                for n, (kb, k) in enumerate(kbs):
                    mm = split_mm(o, w_hi[:, s, kb], w_lo[:, s, kb], xh[:, k], xl[:, k],
                                  start and n == 0, stop and n == len(kbs) - 1)
                return mm

            def unit(u, parity, bank, xh=op_hi, xl=op_lo):
                pe.wait_ge(split_ready, u + 1)
                blocks(ps[bank][:, :], parity, [(k, k) for k in range(8)], xh, xl).then_inc(unit_done, 1)

            def full_sum(bank, x=acc):
                return pe.matmul(ps[bank][:, :], ones, x, start=True, stop=True)

            def scores(z, q, x, i, kh, kl, qh, ql):
                if q >= 2:
                    pe.wait_ge(z["dve"].sem, z["dve"].at(f"m{q - 2}{x}", i))
                n = P * (q + 1)
                z["pe"].done(split_mm(ps[3 + q % 2][:, 0:n], qh[:, q * P:(q + 1) * P], ql[:, q * P:(q + 1) * P],
                                      kh[:, 0:n], kl[:, 0:n], True, True), f"s{q}{x}")

            def turn(z, q, x, i, pbuf):
                pe.wait_ge(z["dve"].sem, z["dve"].at(f"n{q}{x}", i))
                if q >= 2:
                    pe.wait_ge(z["dve"].sem, z["dve"].at(f"l{q - 2}{x}", i))
                for kt in range(q + 1):
                    mm = pe.transpose(ps[5 + q % 2][:, kt * P:(kt + 1) * P], pbuf[:, q % 2, kt * P:(kt + 1) * P], ident)
                z["pe"].done(mm, f"t{q}{x}")

            def values(z, q, x, i, vh, vl, pth, ptl):
                pe.wait_ge(z["dve"].sem, z["dve"].at(f"l{q}{x}", i))
                for kt in range(q + 1):
                    mm = split_mm(ps[7][:, q * P:(q + 1) * P], vh[:, kt * P:(kt + 1) * P], vl[:, kt * P:(kt + 1) * P],
                                  pth[:, q % 2, kt * P:(kt + 1) * P], ptl[:, q % 2, kt * P:(kt + 1) * P], kt == 0, kt == q)
                z["pe"].done(mm, f"o{q}{x}")

            def attend(z, x, i, kh, kl, qh, ql, vh, vl, pth, ptl, pbuf):
                for a, q in (("s", 0), ("s", 1), ("t", 0), ("s", 2), ("t", 1), ("o", 0), ("s", 3), ("t", 2), ("o", 1),
                             ("t", 3), ("o", 2), ("o", 3)):
                    if a == "s":
                        scores(z, q, x, i, kh, kl, qh, ql)
                    elif a == "t":
                        turn(z, q, x, i, pbuf)
                    else:
                        values(z, q, x, i, vh, vl, pth, ptl)

            pe.wait_ge(cst_in, 32)
            a, d, z = enter(pe, "pe", "start")
            pe.wait_ge(d.sem, d.at("acc7"))
            z.done(full_sum(2), "sum")

            a, d, z = enter(pe, "pe", "lat")
            u = U0["lat"]
            for n in range(6):
                if n >= 2:
                    pe.wait_ge(d.sem, d.at(f"z{n - 2}"))
                unit(u + n, n % 2, n % 2)
                if n == 3:
                    pe.wait_ge(d.sem, d.at("acc2"))
                    z.done(full_sum(2), "sum_q")
            pe.wait_ge(d.sem, d.at("acc4"))
            z.done(full_sum(3), "sum_kv")

            a, d, z = enter(pe, "pe", "mla")
            with pe.Fori(0, NH // 2) as i:
                for hh, x in enumerate("ab"):
                    u = i * 2 + (U0["mla"] + hh)
                    before, bi = ("b", i - 1) if hh == 0 else ("a", i)
                    pe.wait_ge(split_ready, u + 1)
                    pe.wait_ge(a.sem, a.at(f"oh{before}", bi))
                    pe.wait_ge(d.sem, d.at(f"ol{before}", bi))
                    z.done(blocks(ps[0][:, :], hh, [(k, k) for k in range(3)], qn_hi, qn_lo), f"q{x}")
                    z.done(blocks(ps[1][:, :], hh, [(3 + k, k) for k in range(2)], kvn_hi, kvn_lo), f"k{x}")
                    for t in range(QT):
                        for k in range(2):
                            mm = split_mm(ps[2][:, t * P:(t + 1) * P], kvn_hi[:, k, t * P:(t + 1) * P],
                                          kvn_lo[:, k, t * P:(t + 1) * P], w_hi[:, hh, 3 + k], w_lo[:, hh, 3 + k],
                                          k == 0, k == 1)
                    mm.then_inc(unit_done, 1)
                    pe.wait_ge(d.sem, d.at(f"ql{x}", i))
                    attend(S["mla"], x, i, ak_hi[:, hh], ak_lo[:, hh], aq_hi[:, 0], aq_lo[:, 0], av_hi[:, 0], av_lo[:, 0],
                           apt_hi, apt_lo, fx[:, 6:8, :])

            a, d, z = enter(pe, "pe", "conv")
            with pe.Fori(0, JC // 2) as i:
                for jj, x in enumerate("ab"):
                    before, bi = ("b", i - 1) if jj == 0 else ("a", i)
                    for n, s in enumerate(("ac", "ax", "ab")):
                        c = 3 * jj + n
                        prev = (("ax", before, bi), ("ab", before, bi), ("ac", x, i))[n]
                        pe.wait_ge(d.sem, d.at(prev[0] + prev[1], prev[2]))
                        unit(i * 6 + (U0["conv"] + c), c % 2, c % 2)

            a, d, z = enter(pe, "pe", "mix")
            with pe.Fori(0, KD // 2) as i:
                for mm_, x in enumerate("ab"):
                    u = i * 6 + (U0["mix"] + 3 * mm_)
                    s = mm_ % 2
                    pe.wait_ge(d.sem, d.at(f"mb{x}", i - 1))
                    unit(u, s, 4 * mm_)
                    unit(u + 1, 1 - s, 4 * mm_ + 1)
                    pe.wait_ge(split_ready, u + 3)
                    blocks(ps[4 * mm_ + 2][:, :], s, [(k, k) for k in range(4)], ya_hi, ya_lo)
                    blocks(ps[4 * mm_ + 3][:, :], s, [(4 + k, k) for k in range(4)], ob_hi, ob_lo).then_inc(unit_done, 1)

            a, d, z = enter(pe, "pe", "wo")
            with pe.Fori(0, KD // 2) as i:
                for m, x in enumerate("ab"):
                    pe.wait_ge(a.sem, a.at(f"sq{x}", i - 1))
                    unit(i * 2 + (U0["wo"] + m), m, m, mix_hi, mix_lo)

            a, d, z = enter(pe, "pe", "res1")
            z.done(full_sum(2), "sum")
            pe.wait_ge(d.sem, d.at("acc7"))
            z.done(full_sum(3), "sum2")
            for half in (0, 1):
                name = f"up{half}"
                a, d, z = enter(pe, "pe", name)
                with pe.Fori(0, HJ) as i:
                    for n, s in enumerate("gv"):
                        pe.wait_ge(d.sem, d.at(s, i - 1))
                        unit(i * 2 + (U0[name] + n), n, n)
                name = f"down{half}"
                a, d, z = enter(pe, "pe", name)
                reader, step = (a, "f") if half == 0 else (a, "sq")
                with pe.Fori(0, 2) as i:
                    for m2 in range(2):
                        for m in range(2):
                            reader_step = f"{step}{2 * m2 + m}"
                            pe.wait_ge(reader.sem, reader.at(reader_step, i - 1))
                        for v in range(3):
                            c = 3 * m2 + v
                            pe.wait_ge(split_ready, i * 6 + (U0[name] + c + 1))
                            for kb in range(8):
                                n = 8 * v + kb
                                if n >= 2 * HJ:
                                    break
                                m, k = n // HJ, n % HJ
                                mm = split_mm(ps[2 * m2 + m][:, :], w_hi[:, c % 2, kb], w_lo[:, c % 2, kb],
                                              f_hi[:, k], f_lo[:, k], k == 0, k == HJ - 1)
                            mm.then_inc(unit_done, 1)

            def ple_proj(k):
                name = f"ple{k}p"
                a, d, z = enter(pe, "pe", name)
                pe.wait_ge(d.sem, d.at("pl"))
                for m in range(KD):
                    c = m // 4
                    if m % 4 == 0:
                        pe.wait_ge(split_ready, U0[name] + c + 1)
                    if m >= 4:
                        pe.wait_ge(a.sem, a.at(f"e{m - 4}"))
                    mm = blocks(ps[4 + m % 4][:, :], c % 2, [(2 * (m % 4) + n, n) for n in range(2)], p_hi, p_lo)
                    if m % 4 < 3:
                        z.done(mm, f"e{m}")
                    else:
                        mm.then_inc(unit_done, 1)

            def ple_gate(k):
                name = f"ple{k}"
                a, d, z = enter(pe, "pe", name)
                with pe.Fori(0, KD // 2) as i:
                    for m, x in enumerate("ab"):
                        pe.wait_ge(a.sem, a.at(f"g{x}", i - 1))
                        unit(i * 2 + (U0[name] + m), m, m)

            ple_proj(1)
            a, d, z = enter(pe, "pe", "res2")
            z.done(full_sum(2), "sum")
            ple_gate(1)
            a, d, z = enter(pe, "pe", "res3")
            z.done(full_sum(2), "sum")

            a, d, z = enter(pe, "pe", "gla_a")
            u = U0["gla_a"]
            unit(u, 0, 0)
            pe.wait_ge(d.sem, d.at("al"))
            pe.wait_ge(split_ready, u + 2)
            for m in range(KD):
                if m >= 4:
                    pe.wait_ge(d.sem, d.at(f"mn{m - 4}"))
                mm = blocks(ps[1 + m % 4][:, :], 1, [(m, 0)], ga_hi, ga_lo)
                if m < KD - 1:
                    z.done(mm, f"a{m}")
                else:
                    mm.then_inc(unit_done, 1)

            a, d, z = enter(pe, "pe", "gla")
            qt_h, kt_h, ks_h = ga_hi[:, 0], ga_hi[:, 1], ga_hi[:, 2]
            qt_l, kt_l, ks_l = ga_lo[:, 0], ga_lo[:, 1], ga_lo[:, 2]
            qj_h, qj_l = ga_hi[:, 3:5].rearrange("p k t -> p (k t)"), ga_lo[:, 3:5].rearrange("p k t -> p (k t)")
            ath, atl = at_hi.rearrange("p k t -> p (k t)"), at_lo.rearrange("p k t -> p (k t)")
            with pe.Fori(0, GH) as i:
                base = i * 16 + U0["gla"]

                def products(b):
                    pe.wait_ge(d.sem, d.at(f"l{b}qj", i))
                    for j in range(QT):
                        t = slice(j * P, (j + 1) * P)
                        split_mm(ps[4][:, t], kt_h[:, t], kt_l[:, t], qt_h[:, t], qt_l[:, t],
                                 b == 0 and j == 0, b == 1, skip=True)
                        q0, n = q_span(j)
                        bank, o = GLA_BANK[j]
                        mm = split_mm(ps[bank][:, o:o + n], ks_h[:, t], ks_l[:, t], qj_h[:, q0:q0 + n], qj_l[:, q0:q0 + n],
                                      b == 0 and o == 0, b == 1, skip=True)
                    z.done(mm, f"A{b}")

                pe.wait_ge(d.sem, d.at("y7", i - 1))
                for c in range(4):
                    unit(base + c, c % 2, c)
                pe.wait_ge(a.sem, a.at("k1", i))
                for c in range(4, 8):
                    s = c % 2
                    pe.wait_ge(split_ready, base + (c + 1))
                    for t in range(QT):
                        for kk in range(2):
                            k = 2 * (c - 4) + kk
                            wh = w_hi[:, s, 4 * kk:4 * kk + 4].rearrange("p k n -> p (k n)")
                            wl = w_lo[:, s, 4 * kk:4 * kk + 4].rearrange("p k n -> p (k n)")
                            mm = split_mm(ps[t][:, :], op_hi[:, k, t * P:(t + 1) * P], op_lo[:, k, t * P:(t + 1) * P],
                                          wh, wl, k == 0, k == KD - 1)
                    mm.then_inc(unit_done, 1)
                products(0)
                for t in range(QT):
                    pe.wait_ge(d.sem, d.at(f"vl{t}", i))
                    unit(base + (8 + t), t % 2, t)
                products(1)
                pe.wait_ge(a.sem, a.at("z3", i))
                pe.wait_ge(d.sem, d.at("atl", i))
                for b in range(4):
                    for j in range(QT):
                        o = GLA_PACK[j]
                        mm = split_mm(ps[b][:, j * P:T], gv_hi[:, j, b * P:(b + 1) * P], gv_lo[:, j, b * P:(b + 1) * P],
                                      ath[:, o:o + T - j * P], atl[:, o:o + T - j * P], j == 0, j == QT - 1)
                    z.done(mm, f"o{b}")
                pe.wait_ge(d.sem, d.at("oacc3", i))
                z.done(full_sum(4), "osum")
                pe.wait_ge(d.sem, d.at("ol3", i))
                for m in range(KD):
                    c = 12 + m // 2
                    if m % 2 == 0:
                        pe.wait_ge(split_ready, base + (c + 1))
                    if m >= 4:
                        pe.wait_ge(d.sem, d.at(f"y{m - 4}", i))
                    mm = blocks(ps[4 + (m + 1) % 4][:, :], c % 2, [(4 * (m % 2) + k, k) for k in range(4)], go_hi, go_lo)
                    if m % 2 == 0:
                        z.done(mm, f"y{m}")
                    else:
                        mm.then_inc(unit_done, 1)

            def norm_sums(name):
                a, d, z = enter(pe, "pe", name)
                pe.wait_ge(d.sem, d.at("acc7"))
                z.done(full_sum(2), "sum")
                pe.wait_ge(d.sem, d.at("v7"))
                z.done(full_sum(3), "sum2")

            norm_sums("ln1")
            ple_proj(2)
            ple_gate(2)
            enter(pe, "pe", "x2")

            a, d, z = enter(pe, "pe", "idx")
            u = U0["idx"]
            for n in range(6):
                if n >= 2:
                    pe.wait_ge(a.sem, a.at(f"qf{n - 2}"))
                unit(u + n, (u + n) % 2, n % 2)
            for n, (name, width) in enumerate((("v", P), ("wi", IH))):
                c = u + 6 + n
                pe.wait_ge(split_ready, c + 1)
                for t in range(QT):
                    for k in range(KD):
                        mm = split_mm(ps[2 + n][:, t * width:(t + 1) * width], op_hi[:, k, t * P:(t + 1) * P],
                                      op_lo[:, k, t * P:(t + 1) * P], w_hi[:, c % 2, k, 0:width], w_lo[:, c % 2, k, 0:width],
                                      k == 0, k == KD - 1)
                mm.then_inc(unit_done, 1)
            pe.wait_ge(d.sem, d.at("kil1"))
            n = 0
            for q in range(1, QT):
                for x in range(IH):
                    if n >= 2:
                        last = divmod(n - 2, IH)
                        pe.wait_ge(a.sem, a.at(f"rel{last[0] + 1}{last[1]}"))
                    t = slice(q * P, (q + 1) * P)
                    w = P * (q + 1)
                    z.done(split_mm(ps[4 + n % 2][:, 0:w], qi_hi[:, x // 2, t], qi_lo[:, x // 2, t],
                                    ki_hi[:, x % 2, 0:w], ki_lo[:, x % 2, 0:w], True, True), f"s{q}{x}")
                    n += 1

            a, d, z = enter(pe, "pe", "dsa_z")
            with pe.Fori(0, DH // 2) as i:
                for n, x in enumerate("ab"):
                    pe.wait_ge(a.sem, a.at(f"z{x}", i - 1))
                    unit(i * 2 + (U0["dsa_z"] + n), (U0["dsa_z"] + n) % 2, n)
            for half in (0, 1):
                name = f"dsa{half}"
                a, d, z = enter(pe, "pe", name)
                with pe.Fori(0, DH // 4) as i:
                    for hh, x in enumerate("ab"):
                        before, bi = ("b", i - 1) if hh == 0 else ("a", i)
                        pe.wait_ge(d.sem, d.at(f"ol{before}", bi))
                        unit(i * 2 + (U0[name] + hh), (U0[name] + hh) % 2, 0)
                        pe.wait_ge(d.sem, d.at(f"ql{x}", i))
                        attend(S[name], x, i, dk_hi[:, 0], dk_lo[:, 0], dq_hi[:, 0], dq_lo[:, 0], dv_hi[:, 0], dv_lo[:, 0],
                               dpt_hi, dpt_lo, fx[:, 8:10, :])
                name = f"dout{half}"
                a, d, z = enter(pe, "pe", name)
                reader = a if half == 0 else d
                with pe.Fori(0, KD // 2) as i:
                    for m, x in enumerate("ab"):
                        pe.wait_ge(reader.sem, reader.at(f"f{x}", i - 1))
                        unit(i * 2 + (U0[name] + m), (U0[name] + m) % 2, m, oz_hi, oz_lo)
            norm_sums("ln2")
            ple_proj(3)
            ple_gate(3)

        def sweep(sqs):
            return lambda n: fx[:, sqs[n % 2], :]

        @block.scalar
        def _(act):
            def hi(steps, name, o, i_):
                steps.done(act.activation(o, i_, ACT.Copy), name)

            def root(steps, name, o, bank, n, eps):
                steps.done(act.activation(o, ps[bank][:, :], ACT.Sqrt, bias=const(eps), scale=1.0 / n), name)

            def load_p(src, k):
                act.dma_start(fx[:, 7:9, :], src).then_inc(p_in, 16)

            def softmax(z, x, i, ts, pbuf, pth, done_p):
                a, d, e = z["act"], z["dve"], z["pe"]
                for what, q in (("e", 0), ("e", 1), ("h", 0), ("e", 2), ("h", 1), ("e", 3), ("h", 2), ("h", 3)):
                    n = P * (q + 1)
                    if what == "e":
                        act.wait_ge(d.sem, d.at(f"m{q}{x}", i))
                        a.done(act.activation(pbuf[:, q % 2, 0:n], ts[q % 2][:, 0:n], ACT.Exp, bias=st[:, 40 + q % 2:41 + q % 2],
                                              scale=-1.0, accum_out=st[:, 42 + q % 2:43 + q % 2]), f"e{q}{x}")
                    else:
                        act.wait_ge(e.sem, e.at(f"t{q}{x}", i))
                        if q >= 2:
                            act.wait_ge(e.sem, e.at(f"o{q - 2}{x}", i))
                        hi(a, f"h{q}{x}", pth[:, q % 2, 0:n], ps[5 + q % 2][:, 0:n])

            act.wait_ge(cst_in, 32)
            act.wait_ge(x_in, 16)
            a, d, z = enter(act, "act", "start")
            sqs = sweep((2, 11))
            for m in M8:
                a.done(act.activation(op_hi[:, m], h[:, m], ACT.Copy, scale=gcol("g_mix_pre", m)), f"hi{m}")
                if m >= 2:
                    act.wait_ge(d.sem, d.at(f"acc{m - 2}"))
                a.done(act.activation(sqs(m), h[:, m], ACT.Square), f"sq{m}")
            act.wait_ge(z.sem, z.at("sum"))
            root(a, "sqrt", rs, 2, D, "eps")
            act.wait_ge(d.sem, d.at("clip"))
            a.done(act.activation(rope_sin[:, :, :], fx[:, 3:6, :], ACT.Sin), "sin")
            a.done(act.activation(fx[:, 6:9, :], fx[:, 3:6, :], ACT.Abs), "abs")
            act.wait_ge(d.sem, d.at("quarter"))
            a.done(act.activation(rope_cos[:, :, :], fx[:, 6:9, :], ACT.Sin), "cos")

            a, d, z = enter(act, "act", "lat")
            for b in LB:
                act.wait_ge(d.sem, d.at(f"z{b}"))
                if b >= 2:
                    act.wait_ge(d.sem, d.at(f"acc{b - 2}"))
                a.done(act.activation(sqs(b), fx[:, 3 + b, :], ACT.Square), f"sq{b}")
            act.wait_ge(z.sem, z.at("sum_q"))
            root(a, "sqrt_q", fx[:, 8, :], 2, QL, "eps")
            act.wait_ge(z.sem, z.at("sum_kv"))
            root(a, "sqrt_kv", fx[:, 9, :], 3, KVL, "eps")
            for b in LB:
                act.wait_ge(d.sem, d.at(f"n{b}"))
                hi(a, f"hi{b}", qn_hi[:, b] if b < 3 else kvn_hi[:, b - 3], fx[:, 3 + b, :])
            act.wait_ge(d.sem, d.at("kr_rot"))
            hi(a, "k0h", ak_hi[0:64, 0], fx[0:64, 10, :])
            hi(a, "k1h", ak_hi[64:128, 1], fx[64:128, 10, :])

            a, d, z = enter(act, "act", "mla")
            with act.Fori(0, NH // 2) as i:
                for hh, x in enumerate("ab"):
                    krow = slice(64, 128) if hh == 0 else slice(0, 64)
                    orow = slice(0, 64) if hh == 0 else slice(64, 128)
                    act.wait_ge(z.sem, z.at(f"q{x}", i))
                    hi(a, f"qf{x}", fx[:, 3, :], ps[0][:, :])
                    act.wait_ge(z.sem, z.at(f"k{x}", i))
                    hi(a, f"kh{x}", ak_hi[krow, hh], ps[1][krow, :])
                    act.wait_ge(unit_done, i * 2 + (U0["mla"] + hh + 1))
                    hi(a, f"vh{x}", av_hi[:, 0], ps[2][:, :])
                    act.wait_ge(d.sem, d.at(f"qa{x}", i))
                    hi(a, f"qh{x}", aq_hi[:, 0], fx[:, 3, :])
                    softmax(S["mla"], x, i, (fx[:, 5, :], fx[:, 8, :]), fx[:, 6:8, :], apt_hi, None)
                    act.wait_ge(z.sem, z.at(f"o3{x}", i))
                    hi(a, f"oh{x}", ob_hi[orow, bass.ds(i, 1), :].rearrange("p a t -> p (a t)"), ps[7][orow, :])

            a, d, z = enter(act, "act", "conv")
            with act.Fori(0, JC // 2) as i:
                for jj, x in enumerate("ab"):
                    act.wait_ge(d.sem, d.at(f"ya{x}", i))
                    hi(a, f"hi{x}", ya_hi[:, bass.ds(i * 2 + jj, 1), :].rearrange("p a t -> p (a t)"), fx[:, 7, :])

            a, d, z = enter(act, "act", "mix")
            with act.Fori(0, KD // 2) as i:
                for m, x in enumerate("ab"):
                    for n, g in enumerate(("a", "b")):
                        act.wait_ge(d.sem, d.at(f"g{g}{x}", i))
                        t = fx[:, 3 + 2 * m + n, :]
                        a.done(act.activation(t, t, ACT.Sigmoid), f"s{g}{x}")
                    act.wait_ge(d.sem, d.at(f"mx{x}", i))
                    hi(a, f"hi{x}", mix_hi[:, bass.ds(i * 2 + m, 1), :].rearrange("p a t -> p (a t)"), fx[:, 3 + 2 * m, :])

            a, d, z = enter(act, "act", "wo")
            with act.Fori(0, KD // 2) as i:
                for m, x in enumerate("ab"):
                    act.wait_ge(unit_done, i * 2 + (U0["wo"] + m + 1))
                    a.done(act.activation(fbuf[:, bass.ds(i * 2 + m, 1), :].rearrange("p a t -> p (a t)"), ps[m][:, :], ACT.Copy), f"f{x}")
                    act.wait_ge(d.sem, d.at(f"acc{x}", i - 1))
                    a.done(act.activation(sqs(m), ps[m][:, :], ACT.Square), f"sq{x}")

            a, d, z = enter(act, "act", "res1")
            load_p(ins["p"].rearrange("k p t -> p k t"), 0)
            act.wait_ge(z.sem, z.at("sum"))
            root(a, "sqrt", rs, 2, D, "eps")
            for m in M8:
                act.wait_ge(d.sem, d.at(f"h{m}"))
                a.done(act.activation(op_hi[:, m], h[:, m], ACT.Copy, scale=gcol("g_ffn_pre", m)), f"hi{m}")
                if m >= 2:
                    act.wait_ge(d.sem, d.at(f"acc{m - 2}"))
                a.done(act.activation(sqs(m), h[:, m], ACT.Square), f"sq{m}")
            act.wait_ge(z.sem, z.at("sum2"))
            root(a, "sqrt2", rs, 3, D, "eps")

            for half in (0, 1):
                name = f"up{half}"
                a, d, z = enter(act, "act", name)
                with act.Fori(0, HJ) as i:
                    act.wait_ge(d.sem, d.at("g2", i))
                    a.done(act.activation(fx[:, 5, :], fx[:, 5, :], ACT.Gelu_apprx_tanh), "ge")
                    act.wait_ge(d.sem, d.at("pr", i))
                    hi(a, "hi", f_hi[:, bass.ds(i, 1), :].rearrange("p a t -> p (a t)"), fx[:, 6, :])
                name = f"down{half}"
                a, d, z = enter(act, "act", name)
                with act.Fori(0, 2) as i:
                    for m in range(4):
                        fm = fbuf[:, bass.ds(i * 4 + m, 1), :].rearrange("p a t -> p (a t)")
                        if half == 0:
                            act.wait_ge(unit_done, i * 6 + (U0[name] + 3 * (m // 2) + 2 + m % 2))
                            a.done(act.activation(fm, ps[m][:, :], ACT.Copy), f"f{m}")
                        else:
                            act.wait_ge(d.sem, d.at(f"f{m}", i))
                            if m >= 2:
                                act.wait_ge(d.sem, d.at(f"acc{m - 2}", i))
                            else:
                                act.wait_ge(d.sem, d.at(f"acc{m + 2}", i - 1))
                            a.done(act.activation(sqs(m), fm, ACT.Square), f"sq{m}")

            def ple_proj(k):
                name = f"ple{k}p"
                a, d, z = enter(act, "act", name)
                act.wait_ge(p_in, 16 * k)
                hi(a, "ph", p_hi, fx[:, 7:9, :])
                for m in M8:
                    if m % 4 < 3:
                        act.wait_ge(z.sem, z.at(f"e{m}"))
                    else:
                        act.wait_ge(unit_done, U0[name] + m // 4 + 1)
                    hi(a, f"e{m}", ebuf[:, m, :], ps[4 + m % 4][:, :])

            def ple_gate(k):
                name = f"ple{k}"
                a, d, z = enter(act, "act", name)
                with act.Fori(0, KD // 2) as i:
                    for m, x in enumerate("ab"):
                        act.wait_ge(unit_done, i * 2 + (U0[name] + m + 1))
                        act.wait_ge(d.sem, d.at(f"e{x}", i - 1))
                        a.done(act.activation(fx[:, 3 + m, :], ps[m][:, :], ACT.Sigmoid), f"g{x}")
                        if k == 1:
                            act.wait_ge(d.sem, d.at(f"e{x}", i))
                            act.wait_ge(d.sem, d.at(f"acc{x}", i - 1))
                            a.done(act.activation(sqs(m), ebuf[:, bass.ds(i * 2 + m, 1), :].rearrange("p a t -> p (a t)"), ACT.Square), f"sq{x}")

            def residual(name):
                a, d, z = enter(act, "act", name)
                act.wait_ge(z.sem, z.at("sum"))
                root(a, "sqrt", rs, 2, D, "eps")
                for m in M8:
                    act.wait_ge(d.sem, d.at(f"h{m}"))
                    hi(a, f"hi{m}", op_hi[:, m], h[:, m])

            ple_proj(1)
            residual("res2")
            ple_gate(1)
            residual("res3")

            a, d, z = enter(act, "act", "gla_a")
            act.wait_ge(unit_done, U0["gla_a"] + 1)
            hi(a, "ah", ga_hi[:, 0], ps[0][:, :])
            for m in M8:
                if m < KD - 1:
                    act.wait_ge(z.sem, z.at(f"a{m}"))
                else:
                    act.wait_ge(unit_done, U0["gla_a"] + 2)
                if m >= 2:
                    act.wait_ge(d.sem, d.at(f"g{m - 2}"))
                t = fx[:, 3 + m % 2, :]
                a.done(act.activation(t, ps[1 + m % 4][:, :], ACT.Abs, bias=gcol("gla_b_a_2", m)), f"ab{m}")
                act.wait_ge(a.sem, a.at(f"ab{m}"))
                a.done(act.activation(t, t, ACT.Exp, scale=-1.0), f"ex{m}")
                act.wait_ge(a.sem, a.at(f"ex{m}"))
                a.done(act.activation(t, t, ACT.Ln, bias=const("one")), f"ln{m}")

            a, d, z = enter(act, "act", "gla")
            g64, gl = fx[:, 3, :], fx[:, 4, :]
            ex, tm = fx[:, 5:7, :].rearrange("p k t -> p (k t)"), fx[:, 7:9, :].rearrange("p k t -> p (k t)")
            atf = fx[:, 9:12, :].rearrange("p k t -> p (k t)")
            gsq = sweep((2, 7))
            inv = 1.0 / GATE_NORM
            with act.Fori(0, GH) as i:
                base = i * 16 + U0["gla"]
                for c, n in enumerate(("q0", "q1", "k0", "k1")):
                    act.wait_ge(unit_done, base + (c + 1))
                    a.done(act.activation(h[:, c], ps[c][:, :], ACT.Copy, scale=GDK ** -0.5 if c < 2 else 1.0), n)

                def prep(b):
                    act.wait_ge(d.sem, d.at(f"po{b}", i))
                    a.done(act.activation(ex[:, 0:T], g64, ACT.Exp, scale=inv), f"x{b}qt")
                    act.wait_ge(d.sem, d.at(f"m{b}qt", i))
                    if b:
                        act.wait_ge(z.sem, z.at("A0", i))
                    hi(a, f"h{b}qt", ga_hi[:, 0], tm[:, 0:T])
                    a.done(act.activation(ex[:, 0:T], g64, ACT.Exp, scale=-inv), f"x{b}kt")
                    act.wait_ge(d.sem, d.at(f"m{b}kt", i))
                    hi(a, f"h{b}kt", ga_hi[:, 1], tm[:, 0:T])
                    for j in range(QT):
                        t = slice(j * P, (j + 1) * P)
                        a.done(act.activation(ex[:, t], gl[:, t], ACT.Exp, scale=-inv, bias=st[:, 8 * b + 4 + j:8 * b + 5 + j]), f"x{b}s{j}")
                    act.wait_ge(d.sem, d.at(f"m{b}ks", i))
                    hi(a, f"h{b}ks", ga_hi[:, 2], tm[:, 0:T])
                    for j in range(QT):
                        q0, n = q_span(j)
                        a.done(act.activation(ex[:, q0:q0 + n], gl[:, T - n:T], ACT.Exp, scale=inv, bias=st[:, 8 * b + j:8 * b + j + 1]), f"x{b}j{j}")
                    act.wait_ge(d.sem, d.at(f"m{b}j{QT - 1}", i))
                    hi(a, f"h{b}qj", ga_hi[:, 3:5].rearrange("p k t -> p (k t)"), tm)

                prep(0)
                for t in range(QT):
                    act.wait_ge(unit_done, base + 8)
                    hi(a, f"vh{t}", gv_hi[:, t], ps[t][:, :])
                prep(1)
                for b in range(4):
                    act.wait_ge(unit_done, base + (9 + b))
                    a.done(act.activation(h[:, 4 + b], ps[b][:, :], ACT.Silu), f"z{b}")
                act.wait_ge(d.sem, d.at(f"ac{QT - 1}", i))
                hi(a, "ath", at_hi.rearrange("p k t -> p (k t)")[:, 0:GLA_AT], atf[:, 0:GLA_AT])
                for b in range(4):
                    act.wait_ge(z.sem, z.at(f"o{b}", i))
                    if b >= 2:
                        act.wait_ge(d.sem, d.at(f"oacc{b - 2}", i))
                    a.done(act.activation(gsq(b), ps[b][:, :], ACT.Square), f"osq{b}")
                act.wait_ge(z.sem, z.at("osum", i))
                root(a, "osqrt", rs, 4, GDV, "eps_ln")
                for b in range(4):
                    act.wait_ge(d.sem, d.at(f"oz{b}", i))
                    hi(a, f"oh{b}", go_hi[:, b], fx[:, 5 + b % 2, :])

            def layer_norm(name, p_src, k):
                a, d, z = enter(act, "act", name)
                load_p(p_src, k)
                act.wait_ge(z.sem, z.at("sum"))
                a.done(act.activation(fx[:, 3, :], ps[2][:, :], ACT.Copy, scale=1.0 / D), "mu")
                for m in M8:
                    act.wait_ge(d.sem, d.at(f"c{m}"))
                    if m >= 2:
                        act.wait_ge(d.sem, d.at(f"v{m - 2}"))
                    a.done(act.activation(sqs(m), fbuf[:, m], ACT.Square), f"sq{m}")
                act.wait_ge(z.sem, z.at("sum2"))
                root(a, "sqrt", rs, 3, D, "eps_ln")
                for m in M8:
                    act.wait_ge(d.sem, d.at(f"x{m}"))
                    hi(a, f"hi{m}", op_hi[:, m], h[:, m])

            layer_norm("ln1", ins["p_2"][0:2].rearrange("k p t -> p k t"), 1)
            ple_proj(2)
            ple_gate(2)
            a, d, z = enter(act, "act", "x2")
            for m in M8:
                hi(a, f"hi{m}", op_hi[:, m], h[:, m])

            a, d, z = enter(act, "act", "idx")
            u = U0["idx"]

            def copy_out(b):
                act.wait_ge(unit_done, u + b + 1)
                if b >= 2:
                    act.wait_ge(d.sem, d.at(["lo0", "lo1", "lo2", "lo3"][b - 2]))
                hi(a, f"qf{b}", fx[:, 9 + b % 2, :], ps[b % 2][:, :])

            def high(b):
                act.wait_ge(d.sem, d.at(f"qa{b}"))
                hi(a, f"hi{b}", qi_hi[:, b], fx[:, 9 + b % 2, :])

            copy_out(0)
            copy_out(1)
            for b in range(4):
                high(b)
                copy_out(b + 2)
            act.wait_ge(d.sem, d.at("qa4"))
            act.wait_ge(d.sem, d.at("zero3"))
            hi(a, "kih0", ki_hi[0:64, 0], fx[0:64, 9, :])
            hi(a, "kih1", ki_hi[64:128, 1], fx[64:128, 9, :])
            act.wait_ge(d.sem, d.at("qa5"))
            hi(a, "kh", dk_hi[:, 0], fx[:, 10, :])
            act.wait_ge(unit_done, u + 7)
            hi(a, "vh", dv_hi[:, 0], ps[2][:, :])
            act.wait_ge(unit_done, u + 8)
            a.done(act.activation(st[:, 0:QT * IH], ps[3][:, 0:QT * IH], ACT.Copy, scale=INDEX_SCALE), "wi")
            for n, (q, x) in enumerate(pairs):
                w = P * (q + 1)
                act.wait_ge(z.sem, z.at(f"s{q}{x}"))
                if n >= 2:
                    act.wait_ge(d.sem, d.at("sc%d%d" % pairs[n - 2]))
                a.done(act.activation(fx[:, 7 + n % 2, 0:w], ps[4 + n % 2][:, 0:w], ACT.Relu), f"rel{q}{x}")

            a, d, z = enter(act, "act", "dsa_z")
            with act.Fori(0, DH // 2) as i:
                for n, x in enumerate("ab"):
                    act.wait_ge(unit_done, i * 2 + (U0["dsa_z"] + n + 1))
                    a.done(act.activation(fb[:, bass.ds(i * 2 + n, 1), :].rearrange("p a t -> p (a t)"), ps[n][:, :], ACT.Silu), f"z{x}")
            for half in (0, 1):
                name = f"dsa{half}"
                a, d, z = enter(act, "act", name)
                with act.Fori(0, DH // 4) as i:
                    for hh, x in enumerate("ab"):
                        act.wait_ge(unit_done, i * 2 + (U0[name] + hh + 1))
                        hi(a, f"qf{x}", fx[:, 10, :], ps[0][:, :])
                        act.wait_ge(d.sem, d.at(f"qa{x}", i))
                        hi(a, f"qh{x}", dq_hi[:, 0], fx[:, 10, :])
                        softmax(S[name], x, i, (fx[:, 7, :], fx[:, 3, :]), fx[:, 8:10, :], dpt_hi, None)
                        act.wait_ge(d.sem, d.at(f"oz{x}", i))
                        hi(a, f"oh{x}", oz_hi[:, bass.ds(i * 2 + hh, 1), :].rearrange("p a t -> p (a t)"), fx[:, 10, :])
                name = f"dout{half}"
                a, d, z = enter(act, "act", name)
                if half == 0:
                    with act.Fori(0, KD // 2) as i:
                        for m, x in enumerate("ab"):
                            act.wait_ge(unit_done, i * 2 + (U0[name] + m + 1))
                            hi(a, f"f{x}", fbuf[:, bass.ds(i * 2 + m, 1), :].rearrange("p a t -> p (a t)"), ps[m][:, :])
            layer_norm("ln2", ins["p_2"][2:4].rearrange("k p t -> p k t"), 2)
            ple_proj(3)
            ple_gate(3)

        @block.vector
        def _(dve):
            def lo(steps, name, o, src, high):
                steps.done(dve.tensor_tensor(o, src, high.bitcast(F32), ALU.subtract), name)

            def mul(steps, name, o, x, y):
                steps.done(dve.tensor_tensor(o, x, y, ALU.mult), name)

            def add(steps, name, o, x, y):
                steps.done(dve.tensor_tensor(o, x, y, ALU.add), name)

            def stt(steps, name, o, x, s, y, op0, op1):
                steps.done(dve.scalar_tensor_tensor(out=o, in0=x, scalar=s, in1=y, op0=op0, op1=op1), name)

            def sync(steps, name, i=0):
                dve.wait_ge(steps.sem, steps.at(name, i))

            def at(tile, i):
                return tile[:, bass.ds(i, 1), :].rearrange("p a t -> p (a t)")

            def accumulate(steps, name, first, s):
                if first:
                    steps.done(dve.tensor_copy(acc, s), name)
                else:
                    add(steps, name, acc, acc, s)

            zeroed = [0]

            def clear(x):
                dve.memset(x, 0.0).then_inc(cleared, 1)
                zeroed[0] += 1
                dve.wait_ge(cleared, zeroed[0])

            def rotate(steps, x, i, f, tmp, table, rows, half, where=""):
                n = where if where else x
                size = 2 * half
                swap = [(r + half) % size + (r - r % size) if r % 32 < size else r for r in range(32)]
                dve.sem_inc(dve_held, 1)
                steps.done(dve.stream_shuffle(tmp[rows, :], f[rows, :], swap), f"sw{n}")
                sync(steps, f"sw{n}", i)
                mul(steps, f"ss{n}", tmp[rows, :], tmp[rows, :], rope_sin[rows, table, :])
                mul(steps, f"qc{n}", f[rows, :], f[rows, :], rope_cos[rows, table, :])
                sync(steps, f"qc{n}", i)
                add(steps, f"qa{n}", f[rows, :], f[rows, :], tmp[rows, :])

            def softmax(z, x, i, ts, pbuf, pth, ptl, bias, scale):
                a, d, e = z["act"], z["dve"], z["pe"]

                def low(q):
                    n = P * (q + 1)
                    sync(a, f"h{q}{x}", i)
                    lo(d, f"l{q}{x}", ptl[:, q % 2, 0:n], ps[5 + q % 2][:, 0:n], pth[:, q % 2, 0:n])

                for q in range(QT):
                    n = P * (q + 1)
                    c = q % 2
                    sync(e, f"s{q}{x}", i)
                    dve.sem_inc(dve_held, 1)
                    d.done(dve.tensor_tensor_reduce(out=ts[c][:, 0:n], in0=ps[3 + c][:, 0:n], in1=bias(q), scale=-scale,
                                                    scalar=3.0e38, op0=ALU.add, op1=ALU.min, accum_out=st[:, 40 + c:41 + c]), f"m{q}{x}")
                    sync(a, f"e{q}{x}", i)
                    d.done(dve.reciprocal(st[:, 44 + c:45 + c], st[:, 42 + c:43 + c]), f"r{q}{x}")
                    sync(d, f"r{q}{x}", i)
                    d.done(dve.tensor_scalar(pbuf[:, c, 0:n], pbuf[:, c, 0:n], st[:, 44 + c:45 + c], None, ALU.mult), f"n{q}{x}")
                    if q:
                        low(q - 1)
                low(QT - 1)

            dve.wait_ge(cst_in, 32)
            dve.wait_ge(x_in, 16)
            a, d, z = enter(dve, "dve", "start")
            sqs = sweep((2, 11))
            for m in M8:
                sync(a, f"hi{m}")
                stt(d, f"lo{m}", op_lo[:, m], h[:, m], gcol("g_mix_pre", m), op_hi[:, m].bitcast(F32), ALU.mult, ALU.subtract)
                sync(a, f"sq{m}")
                accumulate(d, f"acc{m}", m == 0, sqs(m))
                sync(d, f"acc{m}")
            sync(a, "sqrt")
            d.done(dve.reciprocal(rs, rs), "rs")
            dve.wait_ge(pos_in, 32)
            d.done(dve.tensor_copy(fx[:, 6:8, :], fx[:, 9:11, :].bitcast(I32)), "pos")
            sync(d, "pos")
            for t in range(3):
                d.done(dve.tensor_scalar(fx[:, 3 + t, :], fx[:, 6 + (t > 0), :], const("inv_freq")[:, t:t + 1], None, ALU.mult), f"ang{t}")
            sync(d, "ang2")
            ang, turns = fx[:, 3:6, :], fx[:, 6:9, :]
            magic = 1.5 * 2 ** 23
            d.done(dve.tensor_scalar(turns, ang, 1.0 / (2 * np.pi), magic, ALU.mult, ALU.add), "turn")
            sync(d, "turn")
            d.done(dve.tensor_scalar(turns, turns, magic, None, ALU.subtract), "whole")
            sync(d, "whole")
            for n, part in enumerate(TURN):
                stt(d, f"red{n + 1}", ang, turns, -part, ang, ALU.mult, ALU.add)
                sync(d, f"red{n + 1}")
            d.done(dve.tensor_scalar(ang, ang, PI, -PI, ALU.min, ALU.max), "clip")
            sync(a, "abs")
            d.done(dve.tensor_scalar(turns, turns, -1.0, np.pi / 2, ALU.mult, ALU.add), "quarter")
            sync(a, "sin")
            for t in range(3):
                d.done(dve.tensor_scalar(rope_sin[:, t, :], rope_sin[:, t, :], const("sign")[:, t:t + 1], None, ALU.mult), f"sin{t}")

            a, d, z = enter(dve, "dve", "lat")
            lat = fx[:, 3:8, :]

            def scaled(b):
                dve.wait_ge(unit_done, U0["lat"] + b + 1)
                mul(d, f"z{b}" if b < 5 else "kr", lat[:, b] if b < 5 else fx[:, 10, :], ps[b % 2][:, :], rs)

            def squares(b):
                sync(a, f"sq{b}")
                accumulate(d, f"acc{b}", b in (0, 3), sqs(b))
                sync(d, f"acc{b}")

            for b in range(3):
                scaled(b)
            for b in range(3):
                squares(b)
            for b in (3, 4, 5):
                scaled(b)
            sync(a, "sqrt_q")
            d.done(dve.reciprocal(fx[:, 8, :], fx[:, 8, :]), "rs_q")
            squares(3)
            squares(4)
            sync(a, "sqrt_kv")
            d.done(dve.reciprocal(fx[:, 9, :], fx[:, 9, :]), "rs_kv")
            sync(d, "rs_kv")
            for b in LB:
                g, o_hi, o_lo = ((gcol("g_q_lat", b), qn_hi[:, b], qn_lo[:, b]) if b < 3 else
                                 (gcol("g_kv_lat", b - 3), kvn_hi[:, b - 3], kvn_lo[:, b - 3]))
                stt(d, f"n{b}", lat[:, b], lat[:, b], g, fx[:, 8 + (b > 2), :], ALU.mult, ALU.mult)
                sync(a, f"hi{b}")
                lo(d, f"lo{b}", o_lo, lat[:, b], o_hi)
            kr, tmp = fx[:, 10, :], fx[:, 2, :]
            d.done(dve.stream_shuffle(tmp, kr, [(r + 16) % 32 for r in range(32)]), "swap")
            sync(d, "swap")
            mul(d, "swap_sin", tmp, tmp, rope_sin[:, 0, :])
            mul(d, "kr_cos", kr, kr, rope_cos[:, 0, :])
            sync(d, "kr_cos")
            add(d, "kr_rot", kr, kr, tmp)
            sync(a, "k0h")
            lo(d, "k0l", ak_lo[0:64, 0], kr[0:64, :], ak_hi[0:64, 0])
            sync(a, "k1h")
            lo(d, "k1l", ak_lo[64:128, 1], kr[64:128, :], ak_hi[64:128, 1])

            a, d, z = enter(dve, "dve", "mla")
            with dve.Fori(0, NH // 2) as i:
                for hh, x in enumerate("ab"):
                    krow = slice(64, 128) if hh == 0 else slice(0, 64)
                    rrow = slice(0, 32) if hh == 0 else slice(64, 96)
                    orow = slice(0, 64) if hh == 0 else slice(64, 128)
                    qf = fx[:, 3, :]
                    sync(a, f"qf{x}", i)
                    rotate(d, x, i, qf, fx[:, 4, :], 0, rrow, ROPE // 2)
                    sync(a, f"kh{x}", i)
                    lo(d, f"kl{x}", ak_lo[krow, hh], ps[1][krow, :], ak_hi[krow, hh])
                    sync(a, f"vh{x}", i)
                    lo(d, f"vl{x}", av_lo[:, 0], ps[2][:, :], av_hi[:, 0])
                    sync(a, f"qh{x}", i)
                    lo(d, f"ql{x}", aq_lo[:, 0], qf, aq_hi[:, 0])
                    softmax(S["mla"], x, i, (fx[:, 5, :], fx[:, 8, :]), fx[:, 6:8, :], apt_hi, apt_lo,
                            lambda q: const("mla_bias")[:, T - P * (q + 1):T], MLA_SCALE)
                    sync(a, f"oh{x}", i)
                    lo(d, f"ol{x}", ob_lo[orow, bass.ds(i, 1), :].rearrange("p a t -> p (a t)"), ps[7][orow, :],
                       ob_hi[orow, bass.ds(i, 1), :].rearrange("p a t -> p (a t)"))

            a, d, z = enter(dve, "dve", "conv")
            tA, tB, cc, yy = fx[:, 3, :], fx[:, 4, :], fx[:, 5, :], fx[:, 7, :]
            with dve.Fori(0, JC // 2) as i:
                for jj, x in enumerate("ab"):
                    j = i * 2 + jj
                    u = i * 6 + (U0["conv"] + 3 * jj)
                    sync(d, "lob" if jj == 0 else "loa", i - 1 if jj == 0 else i)
                    for n, (name, o) in enumerate((("ac", tA), ("ax", tB))):
                        dve.wait_ge(unit_done, u + (n + 1))
                        mul(d, name + x, o, ps[(3 * jj + n) % 2][:, :], rs)
                    sync(d, f"ax{x}", i)
                    mul(d, f"c{x}", cc, tA, tB)
                    sync(d, f"c{x}", i)
                    dve.wait_ge(unit_done, u + 3)
                    mul(d, f"ab{x}", tA, ps[(3 * jj + 2) % 2][:, :], rs)
                    d.done(dve.tensor_scalar(yy, cc, gcol("conv_a_w", j + 2 * JC), None, ALU.mult), f"y0{x}")
                    sync(d, f"y0{x}", i)
                    stt(d, f"y1{x}", yy[:, 1:T], cc[:, 0:T - 1], gcol("conv_a_w", j + JC), yy[:, 1:T], ALU.mult, ALU.add)
                    sync(d, f"y1{x}", i)
                    stt(d, f"y2{x}", yy[:, 2:T], cc[:, 0:T - 2], gcol("conv_a_w", j), yy[:, 2:T], ALU.mult, ALU.add)
                    sync(d, f"y2{x}", i)
                    mul(d, f"ya{x}", yy, yy, tA)
                    sync(a, f"hi{x}", i)
                    lo(d, f"lo{x}", at(ya_lo, j), yy, at(ya_hi, j))

            a, d, z = enter(dve, "dve", "mix")
            with dve.Fori(0, KD // 2) as i:
                for m, x in enumerate("ab"):
                    u = i * 6 + (U0["mix"] + 3 * m)
                    ga, gb = fx[:, 3 + 2 * m, :], fx[:, 4 + 2 * m, :]
                    dve.wait_ge(unit_done, u + 1)
                    mul(d, f"ga{x}", ga, ps[4 * m][:, :], rs)
                    dve.wait_ge(unit_done, u + 2)
                    mul(d, f"gb{x}", gb, ps[4 * m + 1][:, :], rs)
                    dve.wait_ge(unit_done, u + 3)
                    sync(a, f"sa{x}", i)
                    mul(d, f"ma{x}", ga, ps[4 * m + 2][:, :], ga)
                    sync(a, f"sb{x}", i)
                    mul(d, f"mb{x}", gb, ps[4 * m + 3][:, :], gb)
                    sync(d, f"mb{x}", i)
                    add(d, f"mx{x}", ga, ga, gb)
                    sync(a, f"hi{x}", i)
                    lo(d, f"lo{x}", at(mix_lo, i * 2 + m), ga, at(mix_hi, i * 2 + m))

            a, d, z = enter(dve, "dve", "wo")
            clear(acc)
            with dve.Fori(0, KD // 2) as i:
                for m, x in enumerate("ab"):
                    sync(a, f"sq{x}", i)
                    add(d, f"acc{x}", acc, acc, sqs(m))
                    sync(d, f"acc{x}", i)

            def post_norm(a, d, f, g):
                sync(a, "sqrt")
                d.done(dve.reciprocal(rs, rs), "rs")
                sync(d, "rs")

                def update(m):
                    stt(d, f"sc{m}", f[:, m], f[:, m], gcol(g, m), rs, ALU.mult, ALU.mult)
                    sync(d, f"sc{m}")
                    add(d, f"h{m}", h[:, m], h[:, m], f[:, m])

                return update

            a, d, z = enter(dve, "dve", "res1")
            update = post_norm(a, d, fbuf, "g_mix_post")
            for m in M8:
                update(m)
                sync(a, f"hi{m}")
                stt(d, f"lo{m}", op_lo[:, m], h[:, m], gcol("g_ffn_pre", m), op_hi[:, m].bitcast(F32), ALU.mult, ALU.subtract)
                sync(a, f"sq{m}")
                accumulate(d, f"acc{m}", m == 0, sqs(m))
                sync(d, f"acc{m}")
            sync(a, "sqrt2")
            d.done(dve.reciprocal(rs, rs), "rs2")

            for half in (0, 1):
                name = f"up{half}"
                a, d, z = enter(dve, "dve", name)
                with dve.Fori(0, HJ) as i:
                    u = i * 2 + U0[name]
                    for n, x in enumerate("gv"):
                        c, y = fx[:, 3 + n, :], fx[:, 5 + n, :]
                        blk = i + (half * HJ + n * JF)
                        dve.wait_ge(unit_done, u + (n + 1))
                        mul(d, x, c, ps[n][:, :], rs)
                        sync(d, x, i)
                        d.done(dve.tensor_scalar(y, c, gcol("conv_ffn_w", blk + 4 * JF), gcol("b_ffn_conv", blk), ALU.mult, ALU.add), f"{x}0")
                        sync(d, f"{x}0", i)
                        stt(d, f"{x}1", y[:, 1:T], c[:, 0:T - 1], gcol("conv_ffn_w", blk + 2 * JF), y[:, 1:T], ALU.mult, ALU.add)
                        sync(d, f"{x}1", i)
                        stt(d, f"{x}2", y[:, 2:T], c[:, 0:T - 2], gcol("conv_ffn_w", blk), y[:, 2:T], ALU.mult, ALU.add)
                    sync(d, "v2", i)
                    sync(a, "ge", i)
                    mul(d, "pr", fx[:, 6, :], fx[:, 5, :], fx[:, 6, :])
                    sync(a, "hi", i)
                    lo(d, "lo", at(f_lo, i), fx[:, 6, :], at(f_hi, i))
                name = f"down{half}"
                a, d, z = enter(dve, "dve", name)
                if half:
                    clear(acc)
                    with dve.Fori(0, 2) as i:
                        for m in range(4):
                            dve.wait_ge(unit_done, i * 6 + (U0[name] + 3 * (m // 2) + 2 + m % 2))
                            fm = at(fbuf, i * 4 + m)
                            add(d, f"f{m}", fm, fm, ps[m][:, :])
                            sync(a, f"sq{m}", i)
                            add(d, f"acc{m}", acc, acc, sqs(m))
                            sync(d, f"acc{m}", i)

            def ple_proj(k):
                a, d, z = enter(dve, "dve", f"ple{k}p")
                sync(a, "ph")
                lo(d, "pl", p_lo, fx[:, 7:9, :], p_hi)

            def ple_gate(k):
                a, d, z = enter(dve, "dve", f"ple{k}")
                if k == 1:
                    clear(acc)
                with dve.Fori(0, KD // 2) as i:
                    for m, x in enumerate("ab"):
                        e = at(ebuf, i * 2 + m)
                        sync(a, f"g{x}", i)
                        mul(d, f"e{x}", e, e, fx[:, 3 + m, :])
                        if k == 1:
                            sync(a, f"sq{x}", i)
                            add(d, f"acc{x}", acc, acc, sqs(m))
                            sync(d, f"acc{x}", i)
                        else:
                            sync(d, f"e{x}", i)
                            add(d, f"h{x}", at(h, i * 2 + m), at(h, i * 2 + m), e)

            def residual(name, f, g):
                a, d, z = enter(dve, "dve", name)
                update = post_norm(a, d, f, g)
                for m in M8:
                    update(m)
                    sync(a, f"hi{m}")
                    lo(d, f"lo{m}", op_lo[:, m], h[:, m], op_hi[:, m])

            ple_proj(1)
            residual("res2", fbuf, "g_ffn_post")
            ple_gate(1)
            residual("res3", ebuf, "g_ple_post")

            a, d, z = enter(dve, "dve", "gla_a")
            d.done(dve.memset(fbuf, 0.0), "zero_y")
            d.done(dve.memset(fx[:, 9:12, :], 0.0), "zero_at")
            sync(a, "ah")
            lo(d, "al", ga_lo[:, 0], ps[0][:, :], ga_hi[:, 0])
            for m in M8:
                sync(a, f"ab{m}")
                t = fx[:, 5 + m % 2, :]
                d.done(dve.tensor_scalar(t, ps[1 + m % 4][:, :], gcol("gla_b_a_2", m), 0.0, ALU.add, ALU.min), f"mn{m}")
                sync(a, f"ln{m}")
                sync(d, f"mn{m}")
                d.done(dve.tensor_tensor(ebuf[:, m], t, fx[:, 3 + m % 2, :], ALU.subtract), f"g{m}")

            a, d, z = enter(dve, "dve", "gla")
            g64, gl = fx[:, 3, :], fx[:, 4, :]
            ex, tm = fx[:, 5:7, :].rearrange("p k t -> p (k t)"), fx[:, 7:9, :].rearrange("p k t -> p (k t)")
            atf = fx[:, 9:12, :].rearrange("p k t -> p (k t)")
            gsq = sweep((2, 7))
            with dve.Fori(0, GH) as i:
                base = i * 16 + U0["gla"]

                def prep(b):
                    g = at(ebuf, i * 2 + b)
                    if b:
                        sync(a, "x0j3", i)
                    d.done(dve.tensor_tensor_scan(g64, const("reset"), g, 0.0, ALU.mult, ALU.add), f"s64{b}")
                    d.done(dve.tensor_tensor_scan(gl, const("ones"), g, 0.0, ALU.mult, ALU.add), f"sgl{b}")
                    sync(d, f"sgl{b}", i)
                    ends = gl.rearrange("p (j t) -> p j t", t=P)[:, :, P - 1]
                    d.done(dve.tensor_scalar(st[:, 8 * b:8 * b + 4], ends, -1.0 / GATE_NORM, None, ALU.mult), f"ne{b}")
                    d.done(dve.tensor_scalar(st[:, 8 * b + 4:8 * b + 8], ends, 1.0 / GATE_NORM, None, ALU.mult), f"po{b}")
                    for n, (name, src) in enumerate((("qt", h[:, b]), ("kt", h[:, 2 + b]), ("ks", h[:, 2 + b]))):
                        if n == 0:
                            sync(a, "k1", i)
                        sync(a, f"x{b}{name}" if n < 2 else f"x{b}s{QT - 1}", i)
                        if n:
                            sync(d, f"l{b}{('qt', 'kt')[n - 1]}", i)
                        mul(d, f"m{b}{name}", tm[:, 0:T], src, ex[:, 0:T])
                        sync(a, f"h{b}{name}", i)
                        lo(d, f"l{b}{name}", ga_lo[:, n], tm[:, 0:T], ga_hi[:, n])
                    for j in range(QT):
                        q0, n = q_span(j)
                        if j == 0:
                            sync(d, f"l{b}ks", i)
                        sync(a, f"x{b}j{j}", i)
                        mul(d, f"m{b}j{j}", tm[:, q0:q0 + n], h[:, b, T - n:T], ex[:, q0:q0 + n])
                    sync(a, f"h{b}qj", i)
                    lo(d, f"l{b}qj", ga_lo[:, 3:5].rearrange("p k t -> p (k t)"), tm, ga_hi[:, 3:5].rearrange("p k t -> p (k t)"))

                prep(0)
                for t in range(QT):
                    sync(a, f"vh{t}", i)
                    lo(d, f"vl{t}", gv_lo[:, t], ps[t][:, :], gv_hi[:, t])
                prep(1)
                sync(z, "A1", i)
                dve.sem_inc(dve_held, 1)
                for j in range(QT):
                    o = GLA_PACK[j]
                    d.done(dve.copy_predicated(atf[:, o:o + P], const("tri").bitcast(U32), ps[4][:, j * P:(j + 1) * P]), f"ad{j}")
                for j in range(QT):
                    o = GLA_PACK[j]
                    q0, n = q_span(j)
                    bank, c = GLA_BANK[j]
                    sync(d, f"ad{j}", i)
                    d.done(dve.tensor_copy(atf[0:CHUNK, o + CHUNK:o + P], ps[bank][0:CHUNK, c:c + CHUNK]), f"ac{j}")
                    if j < QT - 1:
                        d.done(dve.tensor_copy(atf[:, o + P:o + T - j * P], ps[bank][:, c + CHUNK:c + n]), f"ao{j}")
                sync(a, "ath", i)
                lo(d, "atl", at_lo.rearrange("p k t -> p (k t)")[:, 0:GLA_AT], atf[:, 0:GLA_AT],
                   at_hi.rearrange("p k t -> p (k t)")[:, 0:GLA_AT])
                for b in range(4):
                    sync(a, f"osq{b}", i)
                    accumulate(d, f"oacc{b}", b == 0, gsq(b))
                    sync(d, f"oacc{b}", i)
                sync(a, "osqrt", i)
                d.done(dve.reciprocal(rs, rs), "ors")
                sync(d, "ors", i)
                for b in range(4):
                    t = fx[:, 5 + b % 2, :]
                    mul(d, f"on{b}", t, ps[b][:, :], rs)
                    sync(d, f"on{b}", i)
                    stt(d, f"oz{b}", t, t, gcol("gla_gn_g_2", i * 4 + b), h[:, 4 + b], ALU.mult, ALU.mult)
                    sync(a, f"oh{b}", i)
                    lo(d, f"ol{b}", go_lo[:, b], t, go_hi[:, b])
                for m in M8:
                    if m % 2 == 0:
                        sync(z, f"y{m}", i)
                    else:
                        dve.wait_ge(unit_done, base + (12 + m // 2 + 1))
                    add(d, f"y{m}", fbuf[:, m], fbuf[:, m], ps[4 + (m + 1) % 4][:, :])

            def layer_norm(name, k):
                a, d, z = enter(dve, "dve", name)
                for m in M8:
                    f = fbuf[:, m]
                    stt(d, f"ta{m}", f, op_hi[:, m].bitcast(F32), ALPHA, f, ALU.mult, ALU.add)
                    sync(d, f"ta{m}")
                    stt(d, f"tb{m}", f, op_lo[:, m].bitcast(F32), ALPHA, f, ALU.mult, ALU.add)
                    sync(d, f"tb{m}")
                    accumulate(d, f"acc{m}", m == 0, f)
                    sync(d, f"acc{m}")
                sync(a, "mu")
                for m in M8:
                    d.done(dve.tensor_tensor(fbuf[:, m], fbuf[:, m], fx[:, 3, :], ALU.subtract), f"c{m}")
                    sync(a, f"sq{m}")
                    accumulate(d, f"v{m}", m == 0, sqs(m))
                    sync(d, f"v{m}")
                sync(a, "sqrt")
                d.done(dve.reciprocal(rs, rs), "rs")
                sync(d, "rs")
                for m in M8:
                    mul(d, f"n{m}", fbuf[:, m], fbuf[:, m], rs)
                    sync(d, f"n{m}")
                    d.done(dve.tensor_scalar(h[:, m], fbuf[:, m], gcol("ln_g_2", k * KD + m), gcol("ln_b_2", k * KD + m),
                                             ALU.mult, ALU.add), f"x{m}")
                    sync(a, f"hi{m}")
                    lo(d, f"lo{m}", op_lo[:, m], h[:, m], op_hi[:, m])

            layer_norm("ln1", 0)
            ple_proj(2)
            ple_gate(2)
            a, d, z = enter(dve, "dve", "x2")
            for m in M8:
                sync(a, f"hi{m}")
                lo(d, f"lo{m}", op_lo[:, m], h[:, m], op_hi[:, m])

            a, d, z = enter(dve, "dve", "idx")
            for n, tile in enumerate((ki_hi[:, 0], ki_hi[:, 1], ki_lo[:, 0], ki_lo[:, 1])):
                d.done(dve.tensor_scalar(tile, const("ones"), 0.0, None, ALU.mult), f"zero{n}")
            for b in range(6):
                f = fx[:, 9 + b % 2, :]
                sync(a, f"qf{b}")
                rows, table, half = (slice(0, P), 2, ID // 8) if b < 5 else (slice(0, 32), 1, DHD // 8)
                rotate(d, str(b), 0, f, fx[:, 11, :], table, rows, half)
                if b < 4:
                    sync(a, f"hi{b}")
                    lo(d, f"lo{b}", qi_lo[:, b], f, qi_hi[:, b])
                elif b == 4:
                    sync(a, "kih0")
                    lo(d, "kil0", ki_lo[0:64, 0], f[0:64, :], ki_hi[0:64, 0])
                    sync(a, "kih1")
                    lo(d, "kil1", ki_lo[64:128, 1], f[64:128, :], ki_hi[64:128, 1])
                else:
                    sync(a, "kh")
                    lo(d, "kl", dk_lo[:, 0], f, dk_hi[:, 0])
            sync(a, "vh")
            lo(d, "vl", dv_lo[:, 0], ps[2][:, :], dv_hi[:, 0])
            sync(a, "wi")
            for n, (q, x) in enumerate(pairs):
                w = P * (q + 1)
                sync(a, f"rel{q}{x}")
                s, rel, wt = fx[:, 3 + q, 0:w], fx[:, 7 + n % 2, 0:w], st[:, q * IH + x:q * IH + x + 1]
                if x == 0:
                    d.done(dve.tensor_scalar(s, rel, wt, None, ALU.mult), f"sc{q}{x}")
                else:
                    stt(d, f"sc{q}{x}", s, rel, wt, s, ALU.mult, ALU.add)
                sync(d, f"sc{q}{x}")
            for q in range(1, QT):
                s = fx[:, 3 + q, q * P:(q + 1) * P]
                add(d, f"ca{q}", s, s, const("causal")[:, T - P:T])
            for q in range(1, QT):
                s = fx[:, 3 + q, 0:P * (q + 1)]
                sync(d, f"ca{q}")
                for r in range(TOPK // 8):
                    d.done(dve.max(st[:, 32:40], s), f"mx{q}_{r}")
                    sync(d, f"mx{q}_{r}")
                    d.done(dve.match_replace(s, st[:, 32:40], s, TAKEN), f"mr{q}_{r}")
                    sync(d, f"mr{q}_{r}")
            for q in range(1, QT):
                s = fx[:, 3 + q, 0:P * (q + 1)]
                d.done(dve.tensor_scalar(s, s, 0.5 * TAKEN, MASKED, ALU.is_gt, ALU.mult), f"sel{q}")

            enter(dve, "dve", "dsa_z")
            for half in (0, 1):
                name = f"dsa{half}"
                a, d, z = enter(dve, "dve", name)
                with dve.Fori(0, DH // 4) as i:
                    for hh, x in enumerate("ab"):
                        qf = fx[:, 10, :]
                        sync(a, f"qf{x}", i)
                        rotate(d, x, i, qf, fx[:, 11, :], 1, slice(0, 32), DHD // 8)
                        sync(a, f"qh{x}", i)
                        lo(d, f"ql{x}", dq_lo[:, 0], qf, dq_hi[:, 0])
                        softmax(S[name], x, i, (fx[:, 7, :], fx[:, 3, :]), fx[:, 8:10, :], dpt_hi, dpt_lo,
                                lambda q: fx[:, 3 + q, 0:P * (q + 1)] if q else const("causal")[:, T - P:T], DSA_SCALE)
                        sync(z, f"o3{x}", i)
                        mul(d, f"oz{x}", qf, ps[7][:, :], at(fb, i * 2 + (hh + half * DH // 2)))
                        sync(a, f"oh{x}", i)
                        lo(d, f"ol{x}", at(oz_lo, i * 2 + hh), qf, at(oz_hi, i * 2 + hh))
                name = f"dout{half}"
                a, d, z = enter(dve, "dve", name)
                if half:
                    with dve.Fori(0, KD // 2) as i:
                        for m, x in enumerate("ab"):
                            dve.wait_ge(unit_done, i * 2 + (U0[name] + m + 1))
                            f = at(fbuf, i * 2 + m)
                            add(d, f"f{x}", f, f, ps[m][:, :])
            layer_norm("ln2", 1)
            ple_proj(3)
            ple_gate(3)

    return nc


def blocks_of(w, rows, cols):
    return w[rows, cols].reshape(-1, P, w[rows, cols].shape[1]).transpose(1, 0, 2)


def weight_units(a):
    units = []

    def put(*parts):
        u = np.zeros((P, 8 * P), np.float32)
        at = 0
        for x in parts:
            x = x.reshape(P, -1)
            u[:, at:at + x.shape[1]] = x
            at += x.shape[1]
        units.append(u)

    def col(w, c, n=P):
        return blocks_of(w, slice(None), slice(c, c + n))

    def wide(w, pieces):
        x = np.zeros((w.shape[0], P), np.float32)
        for at, c, n in pieces:
            x[:, at:at + n] = w[:, c:c + n]
        return col(x, 0)

    w = a["w_in"][0]
    c_q = 3 * CONV
    c_kv = c_q + QL
    c_r = c_kv + KVL
    c_ga = c_r + ROPE
    for b in range((QL + KVL) // P):
        put(col(w, c_q + b * P))
    put(wide(w, [(0, c_r, ROPE), (64, c_r, ROPE)]))
    wq, wkv = a["w_q_up"][0], a["w_kv_up"][0]
    for n in range(NH):
        q, k = n * (NOPE + ROPE), n * (NOPE + VD)
        if n % 2 == 0:
            put(wide(wq, [(0, q + NOPE, ROPE), (64, q, NOPE)]), wide(wkv, [(0, k + NOPE, VD), (64, k, NOPE)]))
        else:
            put(wide(wq, [(0, q, NOPE), (64, q + NOPE, ROPE)]), wide(wkv, [(0, k, NOPE), (64, k + NOPE, VD)]))
    for j in range(JC):
        for part in (1, 2, 0):
            put(col(w, part * CONV + j * P))
    for m in range(KD):
        put(col(w, c_ga + m * P))
        put(col(w, c_ga + D + m * P))
        put(col(a["w_a_out"][0], m * P), col(a["w_b_out"][0], m * P))
    for m in range(KD):
        put(col(a["w_o"][0], m * P))
    for half in range(2):
        for j in range(half * HJ, (half + 1) * HJ):
            put(col(a["w_ffn_up"][0], j * P))
            put(col(a["w_ffn_up"][0], DFF + j * P))
        down = a["w_ffn_down"][0][half * HJ * P:(half + 1) * HJ * P]
        for m in range(0, KD, 2):
            both = np.concatenate([col(down, m * P), col(down, (m + 1) * P)], axis=1)
            for v in range(3):
                put(both[:, 8 * v:8 * v + 8])

    def ple(proj, gate):
        for m in range(0, KD, 4):
            put(*[col(proj, (m + n) * P) for n in range(4)])
        for m in range(KD):
            put(col(gate, m * P))

    ple(a["w_ple_proj"][0], a["w_ple_gate"][0])
    w = a["gla_w_in_2"][0]
    qk = GH * GDK
    put(wide(w, [(0, 2 * qk + 2 * DI, GRANK)]))
    up = np.zeros((P, D), np.float32)
    up[:GRANK] = a["gla_w_a2_2"][0]
    put(up)
    for n in range(GH):
        for c in (n * GDK, n * GDK + P, qk + n * GDK, qk + n * GDK + P):
            put(col(w, c))
        v = col(w, 2 * qk + n * GDV, GDV)
        for c in range(4):
            put(v[:, 2 * c:2 * c + 2])
        for b in range(4):
            put(col(w, 2 * qk + DI + n * GDV + b * P))
        rows = a["gla_w_out_2"][0][n * GDV:(n + 1) * GDV]
        for m in range(0, KD, 2):
            put(col(rows, m * P), col(rows, (m + 1) * P))
    ple(a["ple_w_2"][0], a["ple_gate_w_2"][0])
    w = a["dsa_w_in_2"][0]
    c_k, c_v, c_z = DI, DI + DHD, DI + 2 * DHD
    c_qi = c_z + DI
    c_ki = c_qi + IH * ID
    c_wi = c_ki + ID
    for b in range(4):
        put(col(w, c_qi + b * P))
    put(wide(w, [(0, c_ki, ID), (ID, c_ki, ID)]))
    put(col(w, c_k))
    put(col(w, c_v))
    put(wide(w, [(0, c_wi, IH)]))
    for n in range(DH):
        put(col(w, c_z + n * P))
    for half in range(2):
        for n in range(half * DH // 2, (half + 1) * DH // 2):
            put(col(w, n * P))
        rows = a["dsa_w_out_2"][0][half * D:(half + 1) * D]
        for m in range(KD):
            put(col(rows, m * P))
    ple(a["ple_w_2"][1], a["ple_gate_w_2"][1])
    assert len(units) == UNITS, (len(units), UNITS)
    return np.stack(units)


def constants():
    c = np.zeros((P, CONSTS), np.float32)

    def put(name, x):
        c[:, C0[name]:C0[name] + x.shape[1]] = x

    r = np.arange(P)
    put("ident", np.eye(P, dtype=np.float32))
    put("ones", np.ones((P, T), np.float32))
    mla, causal = np.zeros((P, T), np.float32), np.zeros((P, T), np.float32)
    mla[:, T - P:] = np.where(r[None, :] // CHUNK <= r[:, None] // CHUNK, 0.0, MASKED)
    causal[:, T - P:] = np.where(r[None, :] <= r[:, None], 0.0, MASKED)
    put("mla_bias", mla)
    put("causal", causal)
    put("tri", ((r[:, None] <= r[None, :]) & (r[:, None] // CHUNK == r[None, :] // CHUNK)).astype(np.float32))
    put("reset", np.broadcast_to(np.arange(T) % CHUNK != 0, (P, T)).astype(np.float32))

    def frequencies(theta, rot, period):
        half = rot // 2
        inv = (np.float32(1.0) / np.float32(theta) ** (np.arange(half, dtype=np.float32) * np.float32(2.0 / rot))).astype(np.float32)
        f, s = np.zeros(P, np.float32), np.ones(P, np.float32)
        on = r % period < rot
        f[on] = inv[(r[on] % period) % half]
        s[on] = np.where(r[on] % period < half, -1.0, 1.0)
        return f, s

    tables = [frequencies(THETA_1, ROPE, 32), frequencies(THETA_2, DHD // 4, 32), frequencies(THETA_2, ID // 4, ID)]
    put("inv_freq", np.stack([f for f, _ in tables], axis=1))
    put("sign", np.stack([s for _, s in tables], axis=1))
    put("eps", np.full((P, 1), EPS, np.float32))
    put("eps_ln", np.full((P, 1), NORM_EPS, np.float32))
    put("one", np.ones((P, 1), np.float32))
    return c


def arrays_of(a):
    def columns(x):
        return x.reshape(-1, P).T

    def turned(x):
        return np.ascontiguousarray(np.swapaxes(x, -1, -2)).reshape(-1, P, T)

    gains = np.concatenate([columns(np.asarray(a[name])) for name, _ in GAIN_COLS], axis=1)
    return {"x": turned(a["x"][0]), "p": turned(a["p"][0, 0]), "p_2": turned(a["p_2"][:, 0]),
            "positions": np.ascontiguousarray(a["positions"]), "positions_2": np.ascontiguousarray(a["positions_2"]),
            "gains": np.ascontiguousarray(gains), "consts": constants(), "weights": weight_units(a)}


def kernel(**inputs):
    import concourse.bacc as bacc
    from concourse.bass_utils import run_bass_kernel_spmd

    arrays = arrays_of({n: np.asarray(x) for n, x in inputs.items()})
    nc = bacc.Bacc("TRN2", target_bir_lowering=False, num_devices=1, dynamic_dma_scratch_size=1024)
    ins = {n: nc.dram_tensor(f"in_{n}", x.shape, mybir.dt.from_np(x.dtype), kind="ExternalInput").ap() for n, x in arrays.items()}
    out = nc.dram_tensor("out_0", (KD, P, T), F32, kind="ExternalOutput").ap()
    build(nc, ins, out)
    r = run_bass_kernel_spmd(nc, [{f"in_{n}": x for n, x in arrays.items()}], core_ids=[0])
    return np.ascontiguousarray(r.results[0]["out_0"].reshape(D, T).T).reshape(1, T, D)
```

```python
import numpy as np
from contextlib import ExitStack

import concourse.bass as bass
from concourse import mybir

F32 = mybir.dt.float32
F32R = mybir.dt.float32r
I32 = mybir.dt.int32
U32 = mybir.dt.uint32
ACT = mybir.ActivationFunctionType
ALU = mybir.AluOpType
AX = mybir.AxisListType

P = 128
T = 512
QT = T // P
D = 1024
KD = D // P
CONV = 512
JC = CONV // P
NH, NOPE, ROPE, VD = 8, 64, 32, 64
QL, KVL = 384, 256
DFF = 2816
JF = DFF // P
HJ = JF // 2
PLE = 256
EPS = 1e-6
MLA_SCALE = (NOPE + ROPE) ** -0.5
THETA_1, THETA_2 = 10000.0, 500000.0
DI = 2048
GH, GDK, GDV, GRANK = 4, 256, 512, 16
GATE_NORM = 16.0
CHUNK = 64
DH, DHD = 16, 128
IH, ID = 8, 64
TOPK = 128
DSA_SCALE = DHD ** -0.5
INDEX_SCALE = (IH ** -0.5) * (ID ** -0.5)
ALPHA = 4 ** 0.25
NORM_EPS = 1e-5
MASKED = -1.0e30
TAKEN = -3.0e38

STAGES = [("lat", 6), ("mla", NH), ("conv", 3 * JC), ("mix", 3 * KD), ("wo", KD), ("res1", 2),
          ("up0", 2 * HJ), ("down0", 12), ("up1", 2 * HJ), ("down1", 12),
          ("ple1", KD),
          ("gla_a", 2), ("gla", 16 * GH), ("ln1", 2), ("ple2", KD),
          ("idx", 8), ("dsa_z", DH), ("dsa0", DH // 2 + 2), ("dout0", KD), ("dsa1", DH // 2 - 2), ("dout1", KD),
          ("ln2", 2), ("ple3", KD)]
U0 = {}
_n = 0
for _name, _count in STAGES:
    U0[_name] = _n
    _n += _count
UNITS = _n
RAW = 4
SLOTS = 2

GAIN_COLS = [("g_mix_pre", KD), ("g_q_lat", QL // P), ("g_kv_lat", KVL // P), ("g_mix_post", KD),
             ("g_ffn_pre", KD), ("g_ffn_post", KD), ("g_ple_post", KD), ("conv_a_w", 3 * JC),
             ("conv_ffn_w", 3 * 2 * JF), ("b_ffn_conv", 2 * JF), ("gla_b_a_2", KD), ("gla_gn_g_2", DI // P),
             ("ln_g_2", 2 * KD), ("ln_b_2", 2 * KD)]
G0 = {}
_n = 0
for _name, _count in GAIN_COLS:
    G0[_name] = _n
    _n += _count
GAINS = _n

CONST_COLS = [("ident", P), ("ones", T), ("mla_bias", T), ("causal", T), ("tri", P), ("reset", T),
              ("inv_freq", 3), ("sign", 3), ("eps", 1), ("eps_ln", 1), ("one", 1)]
C0 = {}
_n = 0
for _name, _count in CONST_COLS:
    C0[_name] = _n
    _n += _count
CONSTS = _n


PI = float(np.nextafter(np.float32(np.pi), np.float32(0)))
TURN = (6.28125, 0.001934051513671875, 2 * np.pi - 6.28125 - 0.001934051513671875)


class Steps:

    def __init__(self, sem, names, n=1):
        self.sem, self.names, self.n = sem, names, n
        self.per = len(names)
        self.credit = max(self.per, 1)
        self.total = self.credit + n * self.per
        self.next = 0

    def at(self, name, i=0):
        return i * self.per + (self.credit + self.names.index(name) + 1)

    def done(self, ins, name):
        assert self.names[self.next] == name, (self.names[self.next], name)
        self.next = (self.next + 1) % self.per
        ins.then_inc(self.sem, 1)


def q_span(j):
    start = sum(T - (P * m + CHUNK) for m in range(j))
    return start, T - (P * j + CHUNK)


GLA_BANK = [(5, 0), (6, 0), (6, q_span(1)[1]), (5, q_span(0)[1])]
GLA_PACK = [sum(T - P * m for m in range(j)) for j in range(QT)]
GLA_AT = sum(T - P * m for m in range(QT))


def build(nc, ins, out):
    ctx = ExitStack()
    with ctx:
        def sb(name, shape, dt):
            return ctx.enter_context(nc.sbuf_tensor(name, shape, dt))

        def sem(name):
            return ctx.enter_context(nc.semaphore(name))

        raw = sb("raw", [P, RAW, 8 * P], F32)
        w_hi = sb("w_hi", [P, SLOTS, 8, P], F32R)
        w_lo = sb("w_lo", [P, SLOTS, 8, P], F32R)
        op_hi = sb("op_hi", [P, KD, T], F32R)
        op_lo = sb("op_lo", [P, KD, T], F32R)
        fb = sb("fb", [P, 24, T], F32)
        h = fb[:, 0:8, :]
        ebuf = fb[:, 8:16, :]
        fbuf = fb[:, 16:24, :]
        r2 = sb("r2", [P, 32 * T], F32R)
        fx = sb("fx", [P, 12, T], F32)
        rope_cos = sb("rope_cos", [P, 3, T], F32)
        rope_sin = sb("rope_sin", [P, 3, T], F32)
        cst = sb("cst", [P, CONSTS], F32)
        gain = sb("gain", [P, GAINS], F32)
        st = sb("st", [P, 64], F32)
        ps = [ctx.enter_context(nc.psum_tensor(f"bank{b}", [P, T], F32)) for b in range(8)]

        def const(name):
            width = dict(CONST_COLS)[name]
            return cst[:, C0[name]:C0[name] + width]

        def gcol(name, i):
            return gain[:, bass.ds(G0[name] + i, 1)]

        ident, ones = const("ident"), const("ones")[:, 0:P]
        rs, acc, sq = fx[:, 0, :], fx[:, 1, :], fx[:, 2, :]

        def pair(at, n):
            a = r2[:, at * T:(at + n) * T].rearrange("p (k t) -> p k t", t=T)
            b = r2[:, (at + n) * T:(at + 2 * n) * T].rearrange("p (k t) -> p k t", t=T)
            return a, b

        ob_hi, ob_lo = pair(0, 4)
        qn_hi, qn_lo = pair(8, 3)
        kvn_hi, kvn_lo = pair(14, 2)
        aq_hi, aq_lo = pair(18, 1)
        ak_hi, ak_lo = pair(20, 2)
        av = [pair(24, 1), pair(30, 1)]
        apt_hi, apt_lo = pair(26, 2)
        ya_hi, ya_lo = pair(8, 4)
        mix_hi, mix_lo = pair(16, 8)
        f_hi, f_lo = pair(0, HJ)
        p_hi, p_lo = pair(24, 2)
        p_raw = [rope_cos[:, 0, :], rope_sin[:, 0, :]]
        go_hi, go_lo = pair(0, 4)
        gv_hi, gv_lo = pair(8, 4)
        at_hi, at_lo = pair(16, 3)
        ga_hi, ga_lo = pair(22, 5)
        x2_hi, x2_lo = pair(0, 8)
        oz_hi, oz_lo = op_hi, op_lo
        qi_hi, qi_lo = op_hi[:, 0:4], op_lo[:, 0:4]
        ki_hi, ki_lo = op_hi[:, 4:6], op_lo[:, 4:6]
        dpt_hi, dpt_lo = pair(16, 2)
        dq_hi, dq_lo = pair(20, 1)
        dk_hi, dk_lo = pair(22, 1)
        dv_hi, dv_lo = pair(24, 1)

        def packed(f):
            def tile(q):
                block, at = ((1, 3 * P), (2, 0), (1, 0), (0, 0))[q]
                return fx[:, f + block, at:at + P * (q + 1)]

            return tile

        mla_probs, dsa_probs = packed(5), packed(7)

        landed = [sem(f"landed{r}") for r in range(RAW)]
        hi_ready = sem("hi_ready")
        split_ready = sem("split_ready")
        unit_done = sem("unit_done")
        x_in, p_in, pos_in, cst_in, out_sem = sem("x_in"), sem("p_in"), sem("pos_in"), sem("cst_in"), sem("out_sem")

        pool_held, dve_held = sem("pool_held"), sem("dve_held")
        cleared = sem("cleared")
        S = {}

        def stage(name, n, act, dve, pe):
            S[name] = {"act": Steps(sem(f"act_{name}"), act, n), "dve": Steps(sem(f"dve_{name}"), dve, n),
                       "pe": Steps(sem(f"pe_{name}"), pe, n)}

        M8 = range(KD)
        stage("start", 1,
              [f"{a}{m}" for m in M8 for a in ("hi", "sq")] + ["sqrt", "sin", "abs", "cos"],
              [f"{a}{m}" for m in M8 for a in ("lo", "acc")] + ["rs", "pos", "ang0", "ang1", "ang2",
               "turn", "whole", "red1", "red2", "red3", "clip", "quarter", "sin0", "sin1", "sin2"],
              ["sum"])
        LB = range(5)
        stage("lat", 1,
              [f"sq{b}" for b in LB] + ["sqrt_q", "sqrt_kv"] + [f"hi{b}" for b in LB] + ["k0h", "k1h"],
              [f"z{b}" for b in LB[:3]] + [f"acc{b}" for b in LB[:3]] + [f"z{b}" for b in LB[3:]] + ["kr"] + ["rs_q"]
              + [f"acc{b}" for b in LB[3:]] + ["rs_kv"]
              + [x for b in LB for x in (f"n{b}", f"lo{b}")] + ["swap", "swap_sin", "kr_cos", "kr_rot", "k0l", "k1l"],
              ["sum_q", "sum_kv"])
        H2 = range(2)

        def soft_act(x):
            return [f"{a}{x}" for a in ("e0", "e1", "e2", "e3", "h0", "h1", "h2", "h3")]

        def soft_dve(x, chores):
            c = [[f"{name}{x}" for name in chore] for chore in chores]
            return ([f"m0{x}", f"m1{x}"] + c[0] + [f"{a}{q}{x}" for q in (0, 1) for a in "rn"] + [f"m2{x}", f"m3{x}"] + c[1]
                    + [f"{a}{q}{x}" for q in (2, 3) for a in "rn"] + [f"l0{x}", f"l1{x}"] + c[2] + [f"l2{x}"] + c[3] + [f"l3{x}"])

        def soft_pe(x):
            return [f"{a}{x}" for a in ("s0", "s1", "s2", "s3", "t0", "t1", "o0", "t2", "o1", "t3", "o2", "o3")]

        NONE = [[]] * 4
        MLA_CHORES = [["kl", "sw"], ["qc", "ss", "vl"], ["qa"], ["ql"]]
        DSA_CHORES = [["sw"], ["qc", "ss"], ["qa"], ["ql"]]
        stage("mla0", 1, ["qf", "kh", "vh", "qh"], ["kl", "sw", "qc", "ss", "vl", "qa", "ql"], [])
        for name, n in (("mla", NH // 2 - 1), ("mla_end", 1)):
            more = [x for x in "ab" if (name, x) != ("mla_end", "b")]
            stage(name, n,
                  sum([([f"qf{x}", f"kh{x}"] if x in more else []) + soft_act(x)[:2] + ([f"vh{x}"] if x in more else [])
                       + soft_act(x)[2:6] + ([f"qh{x}"] if x in more else []) + soft_act(x)[6:] + [f"oh{x}"] for x in "ab"], []),
                  sum([soft_dve(x, MLA_CHORES if x in more else NONE) + [f"ol{x}"] for x in "ab"], []),
                  sum([soft_pe(x) for x in "ab"], []))
        stage("conv", JC // 2,
              sum([[f"hi{x}"] for x in "ab"], []),
              sum([[f"{a}{x}" for a in ("ac", "ax", "c", "ab", "y0", "y1", "y2", "ya", "lo")] for x in "ab"], []), [])
        stage("mix", KD // 2,
              sum([[f"sa{x}", f"sb{x}", f"hi{x}"] for x in "ab"], []),
              sum([[f"{a}{x}" for a in ("ga", "gb", "ma", "mb", "mx", "lo")] for x in "ab"], []), [])
        stage("wo", KD // 2, sum([[f"f{x}", f"sq{x}"] for x in "ab"], []), [f"acc{x}" for x in "ab"], [])
        stage("res1", 1, ["ph0", "ph1", "sqrt"] + [f"e{m}" for m in range(4)]
              + [x for m in M8 for x in [f"hi{m}", f"sq{m}"] + ([f"e{m + 4}"] if m < 4 else [])] + ["sqrt2"],
              ["pl0", "pl1", "rs"] + [f"{a}{m}" for m in M8 for a in ("sc", "h", "lo", "acc")] + ["rs2"], ["sum"] + [f"e{m}" for m in M8 if m % 4 < 3] + ["sum2"])
        for half in (0, 1):
            stage(f"up{half}", HJ, ["ge", "hi"],
                  ["g", "g0", "g1", "g2", "v", "v0", "v1", "v2", "pr", "lo"], [])
            if half == 0:
                stage("down0", 2, [f"f{m}" for m in range(4)], [], [])
            else:
                stage("down1", 2, [f"sq{m}" for m in range(4)], [f"{a}{m}" for m in range(4) for a in ("f", "acc")], [])
        stage("res2", 1, ["sqrt"] + [f"hi{m}" for m in M8],
              ["rs"] + [f"{a}{m}" for m in M8 for a in ("sc", "h", "lo")], ["sum"])
        stage("ple1", KD // 2, sum([[f"g{x}", f"sq{x}"] for x in "ab"], []),
              sum([[f"e{x}", f"acc{x}"] for x in "ab"], []), [])
        stage("res3", 1, ["sqrt"] + [f"hi{m}" for m in M8],
              ["rs"] + [f"{a}{m}" for m in M8 for a in ("sc", "h", "lo")], ["sum"])
        stage("gla_a", 1, ["ah"] + [f"{a}{m}" for m in M8 for a in ("ab", "ex", "ln")],
              ["zero_y", "zero_at", "al"] + [f"{a}{m}" for m in M8 for a in ("mn", "g")], [f"a{m}" for m in range(KD - 1)])
        gla_act, gla_dve = ["q0", "q1", "k0", "k1"], []

        def gla_prep_act(b):
            return ([f"x{b}qt", f"h{b}qt", f"x{b}kt", f"h{b}kt"] + [f"x{b}s{j}" for j in range(QT)] + [f"h{b}ks"]
                    + [f"x{b}j{j}" for j in range(QT)] + [f"h{b}qj"])

        def gla_prep_dve(b):
            return ([f"s64{b}", f"sgl{b}", f"ne{b}", f"po{b}", f"m{b}qt", f"l{b}qt", f"m{b}kt", f"l{b}kt", f"m{b}ks", f"l{b}ks"]
                    + [f"m{b}j{j}" for j in range(QT)] + [f"l{b}qj"])

        gla_act += gla_prep_act(0) + [f"vh{t}" for t in range(QT)] + gla_prep_act(1) + [f"z{b}" for b in range(4)]
        gla_dve += gla_prep_dve(0) + [f"vl{t}" for t in range(QT)] + gla_prep_dve(1)
        gla_act += ["ath"] + [f"osq{b}" for b in range(4)] + ["osqrt"]
        gla_dve += [f"ad{j}" for j in range(QT)] + [f"{a}{j}" for j in range(QT) for a in ("ac", "ao")][:-1] + ["atl"]
        gla_dve += [f"oacc{b}" for b in range(4)] + ["ors"]
        for b in range(4):
            gla_dve += [f"on{b}", f"oz{b}", f"ol{b}"]
            gla_act += [f"oh{b}"]
        gla_dve += [f"y{m}" for m in M8]
        stage("gla", GH, gla_act, gla_dve, ["A0", "A1"] + [f"o{b}" for b in range(4)] + ["osum"] + [f"y{m}" for m in M8 if m % 2 == 0])

        def ln_stage(name, summed):
            stage(name, 1, ["ph0", "ph1", "mu"] + [f"{a}{m}" for m in M8 for a in ("sq", "e")] + ["sqrt"] + [f"hi{m}" for m in M8],
                  ["pl0", "pl1"] + ([] if summed else [f"acc{m}" for m in M8]) + [x for m in M8 for x in (f"c{m}", f"v{m}")] + ["rs"]
                  + [f"{a}{m}" for m in M8 for a in ("n", "x", "lo")],
                  ["sum"] + [f"e{m}" for m in M8 if m % 4 < 3] + ["sum2"])

        ln_stage("ln1", False)
        stage("ple2", KD // 2, [f"{a}{x}" for x in "ab" for a in ("g", "hi")],
              [f"{a}{x}" for x in "ab" for a in ("e", "h", "t", "lo")], [])
        idx_act = ["qf0", "qf1", "hi0", "qf2", "hi1", "qf3", "hi2", "qf4", "hi3", "qf5", "kih0", "kih1", "kh", "vh", "wi"]
        idx_dve = [f"zero{n}" for n in range(4)]
        for b in range(6):
            idx_dve += [f"sw{b}", f"qc{b}", f"ss{b}", f"qa{b}"] + ([f"lo{b}"] if b < 4 else [["kil0", "kil1"], ["kl"]][b - 4])
        pairs = [(q, x) for q in range(1, QT) for x in range(IH)]
        stage("idx", 1, idx_act + [f"rel{q}{x}" for q, x in pairs],
              idx_dve + ["vl"] + [f"sc{q}{x}" for q, x in pairs] + [f"ca{q}" for q in range(1, QT)]
              + [f"{a}{q}_{r}" for q in range(1, QT) for r in range(TOPK // 8) for a in ("mx", "mr")]
              + [f"sel{q}" for q in range(1, QT)],
              [f"s{q}{x}" for q, x in pairs])
        stage("dsa_z", DH // 2, ["za", "zb"], [], [])
        stage("dsa_p", 1, ["qf", "qh"], ["sw", "qc", "ss", "qa", "ql"], [])
        for name, n in (("dsa0", DH // 4), ("dsa1", DH // 4 - 1), ("dsa1_end", 1)):
            more = [x for x in "ab" if (name, x) != ("dsa1_end", "b")]
            stage(name, n,
                  sum([([f"qf{x}"] if x in more else []) + soft_act(x)[:6] + ([f"qh{x}"] if x in more else [])
                       + soft_act(x)[6:] + [f"oh{x}"] for x in "ab"], []),
                  sum([soft_dve(x, DSA_CHORES if x in more else NONE) + [f"oz{x}", f"ol{x}"] for x in "ab"], []),
                  sum([soft_pe(x) for x in "ab"], []))
        for half in (0, 1):
            stage(f"dout{half}", KD // 2, [], ["fa", "fb"] if half == 0 else ["fa", "acca", "fb", "accb"], [])
        ln_stage("ln2", True)
        stage("ple3", KD // 2, [f"g{x}" for x in "ab"], [f"{a}{x}" for x in "ab" for a in ("e", "h")], [])

        ORDER = ["start", "lat", "mla0", "mla", "mla_end", "conv", "mix", "wo", "res1", "up0", "down0", "up1", "down1", "res2",
                 "ple1", "res3", "gla_a", "gla", "ln1", "ple2", "idx", "dsa_z", "dsa_p", "dsa0", "dout0", "dsa1",
                 "dsa1_end", "dout1", "ln2", "ple3"]

        def enter(eng, who, name, others=("act", "dve", "pe")):
            k = ORDER.index(name)
            if k:
                before = S[ORDER[k - 1]][who]
                eng.wait_ge(before.sem, before.total)
            if who == "pe":
                used = U0[name] if name in U0 else 0
                if used:
                    eng.wait_ge(unit_done, used)
            mine = S[name][who]
            eng.sem_inc(mine.sem, mine.credit)
            for other in others:
                if other != who:
                    eng.wait_ge(S[name][other].sem, S[name][other].credit)
            return S[name]["act"], S[name]["dve"], S[name]["pe"]

        block = ctx.enter_context(nc.Block())

        @block.sync
        def _(sp):
            sp.dma_start(cst[:, :], ins["consts"]).then_inc(cst_in, 16)
            sp.dma_start(gain[:, :], ins["gains"]).then_inc(cst_in, 16)
            sp.dma_start(h, ins["x"].rearrange("k p t -> p k t")).then_inc(x_in, 16)
            for n, name in enumerate(("positions", "positions_2")):
                sp.dma_start(fx[:, 9 + n, :].bitcast(I32), ins[name].broadcast_to([P, T])).then_inc(pos_in, 16)

            def load(u, r):
                sp.dma_start(raw[:, r, :], ins["weights"][bass.ds(u, 1)].rearrange("a p n -> (a p) n")).then_inc(landed[r], 16)

            n = UNITS
            for u in range(min(RAW, n)):
                load(u, u)
            rounds = n // RAW
            if rounds > 1:
                with sp.Fori(1, rounds) as k:
                    for r in range(RAW):
                        sp.wait_ge(split_ready, k * RAW + (r - RAW + 1))
                        load(k * RAW + r, r)
            for u in range(max(rounds, 1) * RAW, n):
                sp.wait_ge(split_ready, u - RAW + 1)
                load(u, u % RAW)
            end = S[ORDER[-1]]
            for who in ("act", "dve", "pe"):
                sp.wait_ge(end[who].sem, end[who].total)
            sp.dma_start(out.rearrange("k p t -> p k t"), h).then_inc(out_sem, 16)
            sp.wait_ge(out_sem, 16)

        @block.gpsimd
        def _(pool):
            def split(u, k, r, free):
                s = r % SLOTS
                pool.wait_ge(landed[r], (k + 1) * 16)
                if free:
                    pool.wait_ge(unit_done, u - (SLOTS - 1))
                hi = w_hi[:, s].rearrange("p k n -> p (k n)")
                lo = w_lo[:, s].rearrange("p k n -> p (k n)")
                pool.sem_inc(pool_held, 1)
                pool.tensor_scalar(hi, raw[:, r, :], 1.0, 0.0, ALU.mult, ALU.add).then_inc(hi_ready, 1)
                pool.wait_ge(hi_ready, u + 1)
                pool.tensor_tensor(lo, raw[:, r, :], hi.bitcast(F32), ALU.subtract).then_inc(split_ready, 1)

            n = UNITS
            for u in range(min(RAW, n)):
                split(u, 0, u, u >= SLOTS)
            rounds = n // RAW
            if rounds > 1:
                with pool.Fori(1, rounds) as k:
                    for r in range(RAW):
                        split(k * RAW + r, k, r, True)
            for u in range(max(rounds, 1) * RAW, n):
                split(u, u // RAW, u % RAW, True)

        @block.tensor
        def _(pe):
            def split_mm(o, ah, al, bh, bl, start, stop, skip=False):
                pe.matmul(o, ah, bh, start=start, stop=False, skip_group_check=skip)
                pe.matmul(o, ah, bl, start=False, stop=False, skip_group_check=skip)
                return pe.matmul(o, al, bh, start=False, stop=stop, skip_group_check=skip)

            def blocks(o, s, kbs, xh, xl, stop=True, start=True):
                for n, (kb, k) in enumerate(kbs):
                    mm = split_mm(o, w_hi[:, s, kb], w_lo[:, s, kb], xh[:, k], xl[:, k],
                                  start and n == 0, stop and n == len(kbs) - 1)
                return mm

            def unit(u, parity, bank, xh=op_hi, xl=op_lo):
                pe.wait_ge(split_ready, u + 1)
                blocks(ps[bank][:, :], parity, [(k, k) for k in range(8)], xh, xl).then_inc(unit_done, 1)

            def full_sum(bank, x=acc):
                return pe.matmul(ps[bank][:, :], ones, x, start=True, stop=True)

            def scores(z, q, x, i, kh, kl, qh, ql):
                if q >= 2:
                    pe.wait_ge(z["dve"].sem, z["dve"].at(f"m{q - 2}{x}", i))
                n = P * (q + 1)
                z["pe"].done(split_mm(ps[3 + q % 2][:, 0:n], qh[:, q * P:(q + 1) * P], ql[:, q * P:(q + 1) * P],
                                      kh[:, 0:n], kl[:, 0:n], True, True), f"s{q}{x}")

            def turn(z, q, x, i, p):
                pe.wait_ge(z["dve"].sem, z["dve"].at(f"n{q}{x}", i))
                if q >= 2:
                    pe.wait_ge(z["dve"].sem, z["dve"].at(f"l{q - 2}{x}", i))
                for kt in range(q + 1):
                    mm = pe.transpose(ps[5 + q % 2][:, kt * P:(kt + 1) * P], p[:, kt * P:(kt + 1) * P], ident)
                z["pe"].done(mm, f"t{q}{x}")

            def values(z, q, x, i, vh, vl, pth, ptl):
                pe.wait_ge(z["dve"].sem, z["dve"].at(f"l{q}{x}", i))
                for kt in range(q + 1):
                    mm = split_mm(ps[7][:, q * P:(q + 1) * P], vh[:, kt * P:(kt + 1) * P], vl[:, kt * P:(kt + 1) * P],
                                  pth[:, q % 2, kt * P:(kt + 1) * P], ptl[:, q % 2, kt * P:(kt + 1) * P], kt == 0, kt == q)
                z["pe"].done(mm, f"o{q}{x}")

            def attend(z, x, i, kh, kl, qh, ql, vh, vl, pth, ptl, probs, project, left):
                scores(z, 0, x, i, kh, kl, qh, ql)
                scores(z, 1, x, i, kh, kl, qh, ql)
                project(0)
                scores(z, 2, x, i, kh, kl, qh, ql)
                scores(z, 3, x, i, kh, kl, qh, ql)
                project(1)
                turn(z, 0, x, i, probs(0))
                turn(z, 1, x, i, probs(1))
                project(2)
                pe.wait_ge(z["dve"].sem, left)
                values(z, 0, x, i, vh, vl, pth, ptl)
                turn(z, 2, x, i, probs(2))
                project(3)
                values(z, 1, x, i, vh, vl, pth, ptl)
                turn(z, 3, x, i, probs(3))
                project(4)
                values(z, 2, x, i, vh, vl, pth, ptl)
                values(z, 3, x, i, vh, vl, pth, ptl)

            pe.wait_ge(cst_in, 32)
            a, d, z = enter(pe, "pe", "start")
            pe.wait_ge(d.sem, d.at("acc7"))
            z.done(full_sum(2), "sum")

            a, d, z = enter(pe, "pe", "lat")
            u = U0["lat"]
            for n in range(6):
                if n >= 2:
                    pe.wait_ge(d.sem, d.at(f"z{n - 2}"))
                unit(u + n, n % 2, n % 2)
                if n == 3:
                    pe.wait_ge(d.sem, d.at("acc2"))
                    z.done(full_sum(2), "sum_q")
            pe.wait_ge(d.sem, d.at("acc4"))
            z.done(full_sum(3), "sum_kv")

            def split_before(d, hh, i):
                if hh:
                    return d.at("qla", i)
                return d.at("qlb", i - 1) if "qlb" in d.names else d.credit

            def mla_query(s):
                return blocks(ps[0][:, :], s, [(k, k) for k in range(3)], qn_hi, qn_lo)

            def mla_key(s):
                return blocks(ps[1][:, :], s, [(3 + k, k) for k in range(2)], kvn_hi, kvn_lo)

            def mla_value(s, tiles):
                for t in tiles:
                    for k in range(2):
                        mm = split_mm(ps[2][:, t * P:(t + 1) * P], kvn_hi[:, k, t * P:(t + 1) * P],
                                      kvn_lo[:, k, t * P:(t + 1) * P], w_hi[:, s, 3 + k], w_lo[:, s, 3 + k], k == 0, k == 1)
                return mm

            a, d, z = enter(pe, "pe", "mla0")
            for n in range(2):
                pe.wait_ge(split_ready, U0["mla"] + n + 1)
                if n:
                    pe.wait_ge(a.sem, a.at("qf"))
                    pe.wait_ge(d.sem, d.at("vl"))
                mla_query(n)
                mla_key(n)
                mla_value(n, range(QT)).then_inc(unit_done, 1)

            def mla_heads(name, i, i0, last):
                a, d, z = S[name]["act"], S[name]["dve"], S[name]["pe"]
                for hh, x in enumerate("ab"):
                    before, bi = ("b", i - 1) if hh == 0 else ("a", i)

                    def project(piece):
                        if last:
                            return
                        if piece == 0:
                            pe.wait_ge(split_ready, i0 * 2 + (U0["mla"] + hh + 3))
                            pe.wait_ge(a.sem, a.at(f"qf{x}", i))
                            mla_query(hh)
                        elif piece == 1:
                            pe.wait_ge(d.sem, d.at(f"kl{x}", i))
                            mla_key(hh)
                        elif piece == 2:
                            pe.wait_ge(d.sem, d.at(f"vl{x}", i))
                            mla_value(hh, [0, 1])
                        elif piece == 3:
                            mla_value(hh, [2])
                        else:
                            mla_value(hh, [3]).then_inc(unit_done, 1)

                    pe.wait_ge(d.sem, split_before(d, hh, i))
                    attend(S[name], x, i, ak_hi[:, hh], ak_lo[:, hh], aq_hi[:, 0], aq_lo[:, 0], av[hh][0][:, 0], av[hh][1][:, 0],
                           apt_hi, apt_lo, mla_probs, project, d.at(f"ol{before}", bi))

            enter(pe, "pe", "mla")
            with pe.Fori(0, NH // 2 - 1) as i:
                mla_heads("mla", i, i, False)
            enter(pe, "pe", "mla_end")
            mla_heads("mla_end", 0, NH // 2 - 1, True)

            a, d, z = enter(pe, "pe", "conv")
            with pe.Fori(0, JC // 2) as i:
                for jj, x in enumerate("ab"):
                    before, bi = ("b", i - 1) if jj == 0 else ("a", i)
                    for n, s in enumerate(("ac", "ax", "ab")):
                        c = 3 * jj + n
                        prev = (("ax", before, bi), ("ab", before, bi), ("ac", x, i))[n]
                        pe.wait_ge(d.sem, d.at(prev[0] + prev[1], prev[2]))
                        unit(i * 6 + (U0["conv"] + c), c % 2, c % 2)

            a, d, z = enter(pe, "pe", "mix")
            with pe.Fori(0, KD // 2) as i:
                for mm_, x in enumerate("ab"):
                    u = i * 6 + (U0["mix"] + 3 * mm_)
                    s = mm_ % 2
                    pe.wait_ge(d.sem, d.at(f"mb{x}", i - 1))
                    unit(u, s, 4 * mm_)
                    unit(u + 1, 1 - s, 4 * mm_ + 1)
                    pe.wait_ge(split_ready, u + 3)
                    blocks(ps[4 * mm_ + 2][:, :], s, [(k, k) for k in range(4)], ya_hi, ya_lo)
                    blocks(ps[4 * mm_ + 3][:, :], s, [(4 + k, k) for k in range(4)], ob_hi, ob_lo).then_inc(unit_done, 1)

            a, d, z = enter(pe, "pe", "wo")
            with pe.Fori(0, KD // 2) as i:
                for m, x in enumerate("ab"):
                    pe.wait_ge(a.sem, a.at(f"sq{x}", i - 1))
                    unit(i * 2 + (U0["wo"] + m), m, m, mix_hi, mix_lo)

            def ple_proj(name, k):
                a, d, z = S[name]["act"], S[name]["dve"], S[name]["pe"]
                pe.wait_ge(d.sem, d.at("pl1"))
                for m in range(KD):
                    c = m // 4
                    if m % 4 == 0:
                        pe.wait_ge(split_ready, U0[name] + c + 1)
                    if m >= 4:
                        pe.wait_ge(a.sem, a.at(f"e{m - 4}"))
                    mm = blocks(ps[4 + m % 4][:, :], c % 2, [(2 * (m % 4) + n, n) for n in range(2)], p_hi, p_lo)
                    if m % 4 < 3:
                        z.done(mm, f"e{m}")
                    else:
                        mm.then_inc(unit_done, 1)

            def blockwise(u0, before):
                d = S[before]["dve"]
                for c in range(4):
                    pe.wait_ge(split_ready, u0 + c + 1)
                    for kk in range(2):
                        k = 2 * c + kk
                        pe.wait_ge(d.sem, d.at(f"lo{k}"))
                        for m in range(4):
                            mm = split_mm(ps[m][:, :], w_hi[:, c % 2, 4 * kk + m], w_lo[:, c % 2, 4 * kk + m],
                                          op_hi[:, k], op_lo[:, k], k == 0, k == KD - 1)
                    mm.then_inc(unit_done, 1)

            a, d, z = enter(pe, "pe", "res1")
            z.done(full_sum(2), "sum")
            ple_proj("res1", 1)
            blockwise(U0["up0"], "res1")
            pe.wait_ge(d.sem, d.at("acc7"))
            pe.wait_ge(a.sem, a.at("e7"))
            z.done(full_sum(7), "sum2")
            for half in (0, 1):
                name = f"up{half}"
                a, d, z = enter(pe, "pe", name, () if half == 0 else ("act", "dve", "pe"))
                if half == 0:
                    for n in range(2):
                        unit(U0[name] + 4 + n, n, 4 + n)
                with pe.Fori(0 if half else 3, HJ) as i:
                    for n, x in enumerate("gv"):
                        pe.wait_ge(d.sem, d.at(x, i - 1))
                        unit(i * 2 + (U0[name] + n), n, 4 + n)
                name = f"down{half}"
                a, d, z = enter(pe, "pe", name)
                reader, step = (a, "f") if half == 0 else (a, "sq")
                with pe.Fori(0, 2) as i:
                    for m2 in range(2):
                        for m in range(2):
                            reader_step = f"{step}{2 * m2 + m}"
                            pe.wait_ge(reader.sem, reader.at(reader_step, i - 1))
                        for v in range(3):
                            c = 3 * m2 + v
                            pe.wait_ge(split_ready, i * 6 + (U0[name] + c + 1))
                            for kb in range(8):
                                n = 8 * v + kb
                                if n >= 2 * HJ:
                                    break
                                m, k = n // HJ, n % HJ
                                mm = split_mm(ps[2 * m2 + m][:, :], w_hi[:, c % 2, kb], w_lo[:, c % 2, kb],
                                              f_hi[:, k], f_lo[:, k], k == 0, k == HJ - 1)
                            mm.then_inc(unit_done, 1)

            def ple_gate(k, before):
                name = f"ple{k}"
                a, d, z = enter(pe, "pe", name, ())
                blockwise(U0[name], before)
                pe.wait_ge(a.sem, a.credit)
                for m in range(4, KD):
                    unit(U0[name] + m, m % 2, m)

            a, d, z = enter(pe, "pe", "res2")
            z.done(full_sum(2), "sum")
            ple_gate(1, "res2")
            a, d, z = enter(pe, "pe", "res3")
            z.done(full_sum(2), "sum")

            a, d, z = enter(pe, "pe", "gla_a")
            u = U0["gla_a"]
            unit(u, 0, 0)
            pe.wait_ge(d.sem, d.at("al"))
            pe.wait_ge(split_ready, u + 2)
            for m in range(KD):
                if m >= 4:
                    pe.wait_ge(d.sem, d.at(f"mn{m - 4}"))
                mm = blocks(ps[1 + m % 4][:, :], 1, [(m, 0)], ga_hi, ga_lo)
                if m < KD - 1:
                    z.done(mm, f"a{m}")
                else:
                    mm.then_inc(unit_done, 1)

            a, d, z = enter(pe, "pe", "gla")
            qt_h, kt_h, ks_h = ga_hi[:, 0], ga_hi[:, 1], ga_hi[:, 2]
            qt_l, kt_l, ks_l = ga_lo[:, 0], ga_lo[:, 1], ga_lo[:, 2]
            qj_h, qj_l = ga_hi[:, 3:5].rearrange("p k t -> p (k t)"), ga_lo[:, 3:5].rearrange("p k t -> p (k t)")
            ath, atl = at_hi.rearrange("p k t -> p (k t)"), at_lo.rearrange("p k t -> p (k t)")
            with pe.Fori(0, GH) as i:
                base = i * 16 + U0["gla"]

                def products(b):
                    pe.wait_ge(d.sem, d.at(f"l{b}qj", i))
                    for j in range(QT):
                        t = slice(j * P, (j + 1) * P)
                        split_mm(ps[4][:, t], kt_h[:, t], kt_l[:, t], qt_h[:, t], qt_l[:, t],
                                 b == 0 and j == 0, b == 1, skip=True)
                        q0, n = q_span(j)
                        bank, o = GLA_BANK[j]
                        mm = split_mm(ps[bank][:, o:o + n], ks_h[:, t], ks_l[:, t], qj_h[:, q0:q0 + n], qj_l[:, q0:q0 + n],
                                      b == 0 and o == 0, b == 1, skip=True)
                    z.done(mm, f"A{b}")

                pe.wait_ge(d.sem, d.at("y7", i - 1))
                for c in range(4):
                    unit(base + c, c % 2, c)
                pe.wait_ge(a.sem, a.at("k1", i))
                for c in range(4, 8):
                    s = c % 2
                    pe.wait_ge(split_ready, base + (c + 1))
                    for t in range(QT):
                        for kk in range(2):
                            k = 2 * (c - 4) + kk
                            wh = w_hi[:, s, 4 * kk:4 * kk + 4].rearrange("p k n -> p (k n)")
                            wl = w_lo[:, s, 4 * kk:4 * kk + 4].rearrange("p k n -> p (k n)")
                            mm = split_mm(ps[t][:, :], op_hi[:, k, t * P:(t + 1) * P], op_lo[:, k, t * P:(t + 1) * P],
                                          wh, wl, k == 0, k == KD - 1)
                    mm.then_inc(unit_done, 1)
                products(0)
                for t in range(QT):
                    pe.wait_ge(d.sem, d.at(f"vl{t}", i))
                    unit(base + (8 + t), t % 2, t)
                products(1)
                pe.wait_ge(a.sem, a.at("z3", i))
                pe.wait_ge(d.sem, d.at("atl", i))
                for b in range(4):
                    for j in range(QT):
                        o = GLA_PACK[j]
                        mm = split_mm(ps[b][:, j * P:T], gv_hi[:, j, b * P:(b + 1) * P], gv_lo[:, j, b * P:(b + 1) * P],
                                      ath[:, o:o + T - j * P], atl[:, o:o + T - j * P], j == 0, j == QT - 1)
                    z.done(mm, f"o{b}")
                pe.wait_ge(d.sem, d.at("oacc3", i))
                z.done(full_sum(4), "osum")
                pe.wait_ge(d.sem, d.at("ol3", i))
                for m in range(KD):
                    c = 12 + m // 2
                    if m % 2 == 0:
                        pe.wait_ge(split_ready, base + (c + 1))
                    if m >= 4:
                        pe.wait_ge(d.sem, d.at(f"y{m - 4}", i))
                    mm = blocks(ps[4 + (m + 1) % 4][:, :], c % 2, [(4 * (m % 2) + k, k) for k in range(4)], go_hi, go_lo)
                    if m % 2 == 0:
                        z.done(mm, f"y{m}")
                    else:
                        mm.then_inc(unit_done, 1)

            def norm_sums(name, k):
                a, d, z = enter(pe, "pe", name)
                if name == "ln1":
                    pe.wait_ge(d.sem, d.at("acc7"))
                z.done(full_sum(2), "sum")
                ple_proj(name, k)
                pe.wait_ge(d.sem, d.at("v7"))
                z.done(full_sum(3), "sum2")

            norm_sums("ln1", 2)
            ple_gate(2, "ln1")

            before = S["ple2"]["dve"]
            a, d, z = enter(pe, "pe", "idx", ())
            u = U0["idx"]
            pe.wait_ge(split_ready, u + 1)
            pe.wait_ge(before.sem, before.at("loa", KD // 2 - 1))
            blocks(ps[0][:, :], u % 2, [(k, k) for k in range(KD - 1)], x2_hi, x2_lo, stop=False)
            pe.wait_ge(before.sem, before.at("lob", KD // 2 - 1))
            split_mm(ps[0][:, :], w_hi[:, u % 2, KD - 1], w_lo[:, u % 2, KD - 1], x2_hi[:, KD - 1], x2_lo[:, KD - 1],
                     False, True).then_inc(unit_done, 1)
            for n in range(1, 6):
                if n >= 2:
                    pe.wait_ge(a.sem, a.at(f"qf{n - 2}"))
                unit(u + n, (u + n) % 2, n % 2, x2_hi, x2_lo)
            for n, (name, width) in enumerate((("v", P), ("wi", IH))):
                c = u + 6 + n
                pe.wait_ge(split_ready, c + 1)
                for t in range(QT):
                    for k in range(KD):
                        mm = split_mm(ps[2 + n][:, t * width:(t + 1) * width], x2_hi[:, k, t * P:(t + 1) * P],
                                      x2_lo[:, k, t * P:(t + 1) * P], w_hi[:, c % 2, k, 0:width], w_lo[:, c % 2, k, 0:width],
                                      k == 0, k == KD - 1)
                mm.then_inc(unit_done, 1)
            pe.wait_ge(d.sem, d.at("kil1"))
            n = 0
            for q in range(1, QT):
                for x in range(IH):
                    if n >= 2:
                        last = divmod(n - 2, IH)
                        pe.wait_ge(a.sem, a.at(f"rel{last[0] + 1}{last[1]}"))
                    t = slice(q * P, (q + 1) * P)
                    w = P * (q + 1)
                    z.done(split_mm(ps[4 + n % 2][:, 0:w], qi_hi[:, x // 2, t], qi_lo[:, x // 2, t],
                                    ki_hi[:, x % 2, 0:w], ki_lo[:, x % 2, 0:w], True, True), f"s{q}{x}")
                    n += 1

            a, d, z = enter(pe, "pe", "dsa_z", ())
            with pe.Fori(0, DH // 2) as i:
                for n, x in enumerate("ab"):
                    pe.wait_ge(a.sem, a.at(f"z{x}", i - 1))
                    unit(i * 2 + (U0["dsa_z"] + n), (U0["dsa_z"] + n) % 2, n, x2_hi, x2_lo)
            def dsa_heads(name, u0, i, i0, last):
                a, d, z = S[name]["act"], S[name]["dve"], S[name]["pe"]
                for hh, x in enumerate("ab"):
                    before, bi = ("b", i - 1) if hh == 0 else ("a", i)

                    def project(piece):
                        if last:
                            return
                        if piece == 0:
                            pe.wait_ge(split_ready, i0 * 2 + (u0 + hh + 1))
                        first, end = ((0, 3), (3, 5), (5, 6), (6, 7), (7, 8))[piece]
                        mm = blocks(ps[hh][:, :], hh, [(k, k) for k in range(first, end)], x2_hi, x2_lo, end == 8, first == 0)
                        if piece == 4:
                            mm.then_inc(unit_done, 1)

                    pe.wait_ge(d.sem, split_before(d, hh, i))
                    attend(S[name], x, i, dk_hi[:, 0], dk_lo[:, 0], dq_hi[:, 0], dq_lo[:, 0], dv_hi[:, 0], dv_lo[:, 0],
                           dpt_hi, dpt_lo, dsa_probs, project, d.at(f"oz{before}", bi))

            enter(pe, "pe", "dsa_p")
            for n in range(2):
                unit(U0["dsa0"] + n, n, n, x2_hi, x2_lo)
            for half in (0, 1):
                name = f"dsa{half}"
                u0 = U0[name] + (0 if half else 2)
                rounds = DH // 4 - half
                enter(pe, "pe", name)
                with pe.Fori(0, rounds) as i:
                    dsa_heads(name, u0, i, i, False)
                if half:
                    enter(pe, "pe", "dsa1_end")
                    dsa_heads("dsa1_end", u0, 0, rounds, True)
                name = f"dout{half}"
                a, d, z = enter(pe, "pe", name)
                with pe.Fori(0, KD // 2) as i:
                    for m, x in enumerate("ab"):
                        pe.wait_ge(d.sem, d.at(f"f{x}", i - 1))
                        unit(i * 2 + (U0[name] + m), (U0[name] + m) % 2, 5 + m, oz_hi, oz_lo)
            norm_sums("ln2", 3)
            ple_gate(3, "ln2")

        def sweep(sqs):
            return lambda n: fx[:, sqs[n % 2], :]

        @block.scalar
        def _(act):
            def hi(steps, name, o, i_):
                steps.done(act.activation(o, i_, ACT.Copy), name)

            def root(steps, name, o, bank, n, eps):
                steps.done(act.activation(o, ps[bank][:, :], ACT.Sqrt, bias=const(eps), scale=1.0 / n), name)

            def load_p(src):
                for k in range(2):
                    act.dma_start(p_raw[k], src[k]).then_inc(p_in, 16)

            def split_p(a, k):
                act.wait_ge(p_in, 32 * k)
                for n in range(2):
                    hi(a, f"ph{n}", p_hi[:, n], p_raw[n])

            def proj_out(name, m):
                a, z = S[name]["act"], S[name]["pe"]
                if m % 4 < 3:
                    act.wait_ge(z.sem, z.at(f"e{m}"))
                else:
                    act.wait_ge(unit_done, U0[name] + m // 4 + 1)
                hi(a, f"e{m}", ebuf[:, m, :], ps[4 + m % 4][:, :])

            def exponentials(z, x, i, probs, tiles):
                a, d = z["act"], z["dve"]
                for q in tiles:
                    act.wait_ge(d.sem, d.at(f"m{q}{x}", i))
                    a.done(act.activation(probs(q), probs(q), ACT.Exp, bias=st[:, 40 + q:41 + q], scale=-1.0,
                                          accum_out=st[:, 44 + q:45 + q]), f"e{q}{x}")

            def turned_high(z, x, i, pth, tiles):
                a, e = z["act"], z["pe"]
                for q in tiles:
                    n = P * (q + 1)
                    act.wait_ge(e.sem, e.at(f"t{q}{x}", i))
                    if q >= 2:
                        act.wait_ge(e.sem, e.at(f"o{q - 2}{x}", i))
                    hi(a, f"h{q}{x}", pth[:, q % 2, 0:n], ps[5 + q % 2][:, 0:n])

            act.wait_ge(cst_in, 32)
            act.wait_ge(x_in, 16)
            a, d, z = enter(act, "act", "start")
            sqs = sweep((2, 11))
            for m in M8:
                a.done(act.activation(op_hi[:, m], h[:, m], ACT.Copy, scale=gcol("g_mix_pre", m)), f"hi{m}")
                if m >= 2:
                    act.wait_ge(d.sem, d.at(f"acc{m - 2}"))
                a.done(act.activation(sqs(m), h[:, m], ACT.Square), f"sq{m}")
            act.wait_ge(z.sem, z.at("sum"))
            root(a, "sqrt", rs, 2, D, "eps")
            act.wait_ge(d.sem, d.at("clip"))
            a.done(act.activation(rope_sin[:, :, :], fx[:, 3:6, :], ACT.Sin), "sin")
            a.done(act.activation(fx[:, 6:9, :], fx[:, 3:6, :], ACT.Abs), "abs")
            act.wait_ge(d.sem, d.at("quarter"))
            a.done(act.activation(rope_cos[:, :, :], fx[:, 6:9, :], ACT.Sin), "cos")

            a, d, z = enter(act, "act", "lat")
            for b in LB:
                act.wait_ge(d.sem, d.at(f"z{b}"))
                if b >= 2:
                    act.wait_ge(d.sem, d.at(f"acc{b - 2}"))
                a.done(act.activation(sqs(b), fx[:, 3 + b, :], ACT.Square), f"sq{b}")
            act.wait_ge(z.sem, z.at("sum_q"))
            root(a, "sqrt_q", fx[:, 8, :], 2, QL, "eps")
            act.wait_ge(z.sem, z.at("sum_kv"))
            root(a, "sqrt_kv", fx[:, 9, :], 3, KVL, "eps")
            for b in LB:
                act.wait_ge(d.sem, d.at(f"n{b}"))
                hi(a, f"hi{b}", qn_hi[:, b] if b < 3 else kvn_hi[:, b - 3], fx[:, 3 + b, :])
            act.wait_ge(d.sem, d.at("kr_rot"))
            hi(a, "k0h", ak_hi[0:64, 0], fx[0:64, 10, :])
            hi(a, "k1h", ak_hi[64:128, 1], fx[64:128, 10, :])

            krows = (slice(64, 128), slice(0, 64))
            orows = (slice(0, 64), slice(64, 128))

            def mla_evacuate(a, x, hh, i, what):
                if what == "qk":
                    hi(a, f"qf{x}", fx[:, 3, :], ps[0][:, :])
                    hi(a, f"kh{x}", ak_hi[krows[hh], hh], ps[1][krows[hh], :])
                else:
                    hi(a, f"vh{x}", av[hh][0][:, 0], ps[2][:, :])

            def mla_heads(name, i, i0, last):
                a, d, z = S[name]["act"], S[name]["dve"], S[name]["pe"]
                for hh, x in enumerate("ab"):
                    more = not (last and hh)
                    if more:
                        act.wait_ge(unit_done, i0 * 2 + (U0["mla"] + hh + 2))
                        mla_evacuate(a, x, 1 - hh, i, "qk")
                    exponentials(S[name], x, i, mla_probs, (0, 1))
                    if more:
                        mla_evacuate(a, x, 1 - hh, i, "v")
                    exponentials(S[name], x, i, mla_probs, (2, 3))
                    turned_high(S[name], x, i, apt_hi, (0, 1))
                    if more:
                        act.wait_ge(d.sem, d.at(f"qa{x}", i))
                        act.wait_ge(z.sem, z.at(f"s3{x}", i))
                        hi(a, f"qh{x}", aq_hi[:, 0], fx[:, 3, :])
                    turned_high(S[name], x, i, apt_hi, (2, 3))
                    act.wait_ge(z.sem, z.at(f"o3{x}", i))
                    hi(a, f"oh{x}", ob_hi[orows[hh], bass.ds(i0, 1), :].rearrange("p a t -> p (a t)"), ps[7][orows[hh], :])

            a, d, z = enter(act, "act", "mla0")
            act.wait_ge(unit_done, U0["mla"] + 1)
            mla_evacuate(a, "", 0, 0, "qk")
            mla_evacuate(a, "", 0, 0, "v")
            act.wait_ge(d.sem, d.at("qa"))
            hi(a, "qh", aq_hi[:, 0], fx[:, 3, :])
            enter(act, "act", "mla")
            with act.Fori(0, NH // 2 - 1) as i:
                mla_heads("mla", i, i, False)
            enter(act, "act", "mla_end")
            mla_heads("mla_end", 0, NH // 2 - 1, True)

            a, d, z = enter(act, "act", "conv")
            load_p(ins["p"])
            with act.Fori(0, JC // 2) as i:
                for jj, x in enumerate("ab"):
                    act.wait_ge(d.sem, d.at(f"ya{x}", i))
                    hi(a, f"hi{x}", ya_hi[:, bass.ds(i * 2 + jj, 1), :].rearrange("p a t -> p (a t)"), fx[:, 7, :])

            a, d, z = enter(act, "act", "mix")
            with act.Fori(0, KD // 2) as i:
                for m, x in enumerate("ab"):
                    for n, g in enumerate(("a", "b")):
                        act.wait_ge(d.sem, d.at(f"g{g}{x}", i))
                        t = fx[:, 3 + 2 * m + n, :]
                        a.done(act.activation(t, t, ACT.Sigmoid), f"s{g}{x}")
                    act.wait_ge(d.sem, d.at(f"mx{x}", i))
                    hi(a, f"hi{x}", mix_hi[:, bass.ds(i * 2 + m, 1), :].rearrange("p a t -> p (a t)"), fx[:, 3 + 2 * m, :])

            a, d, z = enter(act, "act", "wo")
            with act.Fori(0, KD // 2) as i:
                for m, x in enumerate("ab"):
                    act.wait_ge(unit_done, i * 2 + (U0["wo"] + m + 1))
                    a.done(act.activation(fbuf[:, bass.ds(i * 2 + m, 1), :].rearrange("p a t -> p (a t)"), ps[m][:, :], ACT.Copy), f"f{x}")
                    act.wait_ge(d.sem, d.at(f"acc{x}", i - 1))
                    a.done(act.activation(sqs(m), ps[m][:, :], ACT.Square), f"sq{x}")

            a, d, z = enter(act, "act", "res1")
            split_p(a, 1)
            act.wait_ge(z.sem, z.at("sum"))
            root(a, "sqrt", rs, 2, D, "eps")
            for m in range(4):
                proj_out("res1", m)
            for m in M8:
                act.wait_ge(d.sem, d.at(f"h{m}"))
                a.done(act.activation(op_hi[:, m], h[:, m], ACT.Copy, scale=gcol("g_ffn_pre", m)), f"hi{m}")
                if m >= 2:
                    act.wait_ge(d.sem, d.at(f"acc{m - 2}"))
                a.done(act.activation(sqs(m), h[:, m], ACT.Square), f"sq{m}")
                if m < 4:
                    proj_out("res1", m + 4)
            act.wait_ge(z.sem, z.at("sum2"))
            act.wait_ge(d.sem, d.at("rs"))
            root(a, "sqrt2", rs, 7, D, "eps")

            for half in (0, 1):
                name = f"up{half}"
                a, d, z = enter(act, "act", name)
                with act.Fori(0, HJ) as i:
                    act.wait_ge(d.sem, d.at("g2", i))
                    a.done(act.activation(fx[:, 5, :], fx[:, 5, :], ACT.Gelu_apprx_tanh), "ge")
                    act.wait_ge(d.sem, d.at("pr", i))
                    hi(a, "hi", f_hi[:, bass.ds(i, 1), :].rearrange("p a t -> p (a t)"), fx[:, 6, :])
                name = f"down{half}"
                a, d, z = enter(act, "act", name)
                with act.Fori(0, 2) as i:
                    for m in range(4):
                        fm = fbuf[:, bass.ds(i * 4 + m, 1), :].rearrange("p a t -> p (a t)")
                        if half == 0:
                            act.wait_ge(unit_done, i * 6 + (U0[name] + 3 * (m // 2) + 2 + m % 2))
                            a.done(act.activation(fm, ps[m][:, :], ACT.Copy), f"f{m}")
                        else:
                            act.wait_ge(d.sem, d.at(f"f{m}", i))
                            if m >= 2:
                                act.wait_ge(d.sem, d.at(f"acc{m - 2}", i))
                            else:
                                act.wait_ge(d.sem, d.at(f"acc{m + 2}", i - 1))
                            a.done(act.activation(sqs(m), fm, ACT.Square), f"sq{m}")

            def ple_gate(k):
                name = f"ple{k}"
                a, d, z = enter(act, "act", name, ())
                for m in M8:
                    i, x = m // 2, "ab"[m % 2]
                    act.wait_ge(unit_done, U0[name] + max(m, 3) + 1)
                    if m >= 2:
                        act.wait_ge(d.sem, d.at(f"e{x}", i - 1))
                    a.done(act.activation(fx[:, 3 + m % 2, :], ps[m][:, :], ACT.Sigmoid), f"g{x}")
                    if k == 1:
                        act.wait_ge(d.sem, d.at(f"e{x}", i))
                        act.wait_ge(d.sem, d.at(f"acc{x}", i - 1))
                        a.done(act.activation(sqs(m), ebuf[:, m], ACT.Square), f"sq{x}")
                    elif k == 2:
                        act.wait_ge(d.sem, d.at(f"h{x}", i))
                        hi(a, f"hi{x}", x2_hi[:, m], h[:, m])

            def residual(name):
                a, d, z = enter(act, "act", name)
                act.wait_ge(z.sem, z.at("sum"))
                root(a, "sqrt", rs, 2, D, "eps")
                for m in M8:
                    act.wait_ge(d.sem, d.at(f"h{m}"))
                    hi(a, f"hi{m}", op_hi[:, m], h[:, m])

            residual("res2")
            ple_gate(1)
            residual("res3")

            a, d, z = enter(act, "act", "gla_a")
            load_p(ins["p_2"][0:2])
            act.wait_ge(unit_done, U0["gla_a"] + 1)
            hi(a, "ah", ga_hi[:, 0], ps[0][:, :])
            for m in M8:
                if m < KD - 1:
                    act.wait_ge(z.sem, z.at(f"a{m}"))
                else:
                    act.wait_ge(unit_done, U0["gla_a"] + 2)
                if m >= 2:
                    act.wait_ge(d.sem, d.at(f"g{m - 2}"))
                t = fx[:, 3 + m % 2, :]
                a.done(act.activation(t, ps[1 + m % 4][:, :], ACT.Abs, bias=gcol("gla_b_a_2", m)), f"ab{m}")
                act.wait_ge(a.sem, a.at(f"ab{m}"))
                a.done(act.activation(t, t, ACT.Exp, scale=-1.0), f"ex{m}")
                act.wait_ge(a.sem, a.at(f"ex{m}"))
                a.done(act.activation(t, t, ACT.Ln, bias=const("one")), f"ln{m}")

            a, d, z = enter(act, "act", "gla")
            g64, gl = fx[:, 3, :], fx[:, 4, :]
            ex, tm = fx[:, 5:7, :].rearrange("p k t -> p (k t)"), fx[:, 7:9, :].rearrange("p k t -> p (k t)")
            atf = fx[:, 9:12, :].rearrange("p k t -> p (k t)")
            gsq = sweep((2, 7))
            inv = 1.0 / GATE_NORM
            with act.Fori(0, GH) as i:
                base = i * 16 + U0["gla"]
                for c, n in enumerate(("q0", "q1", "k0", "k1")):
                    act.wait_ge(unit_done, base + (c + 1))
                    a.done(act.activation(h[:, c], ps[c][:, :], ACT.Copy, scale=GDK ** -0.5 if c < 2 else 1.0), n)

                def prep(b):
                    act.wait_ge(d.sem, d.at(f"po{b}", i))
                    a.done(act.activation(ex[:, 0:T], g64, ACT.Exp, scale=inv), f"x{b}qt")
                    act.wait_ge(d.sem, d.at(f"m{b}qt", i))
                    if b:
                        act.wait_ge(z.sem, z.at("A0", i))
                    hi(a, f"h{b}qt", ga_hi[:, 0], tm[:, 0:T])
                    a.done(act.activation(ex[:, 0:T], g64, ACT.Exp, scale=-inv), f"x{b}kt")
                    act.wait_ge(d.sem, d.at(f"m{b}kt", i))
                    hi(a, f"h{b}kt", ga_hi[:, 1], tm[:, 0:T])
                    for j in range(QT):
                        t = slice(j * P, (j + 1) * P)
                        a.done(act.activation(ex[:, t], gl[:, t], ACT.Exp, scale=-inv, bias=st[:, 8 * b + 4 + j:8 * b + 5 + j]), f"x{b}s{j}")
                    act.wait_ge(d.sem, d.at(f"m{b}ks", i))
                    hi(a, f"h{b}ks", ga_hi[:, 2], tm[:, 0:T])
                    for j in range(QT):
                        q0, n = q_span(j)
                        a.done(act.activation(ex[:, q0:q0 + n], gl[:, T - n:T], ACT.Exp, scale=inv, bias=st[:, 8 * b + j:8 * b + j + 1]), f"x{b}j{j}")
                    act.wait_ge(d.sem, d.at(f"m{b}j{QT - 1}", i))
                    hi(a, f"h{b}qj", ga_hi[:, 3:5].rearrange("p k t -> p (k t)"), tm)

                prep(0)
                for t in range(QT):
                    act.wait_ge(unit_done, base + 8)
                    hi(a, f"vh{t}", gv_hi[:, t], ps[t][:, :])
                prep(1)
                for b in range(4):
                    act.wait_ge(unit_done, base + (9 + b))
                    a.done(act.activation(h[:, 4 + b], ps[b][:, :], ACT.Silu), f"z{b}")
                act.wait_ge(d.sem, d.at(f"ac{QT - 1}", i))
                hi(a, "ath", at_hi.rearrange("p k t -> p (k t)")[:, 0:GLA_AT], atf[:, 0:GLA_AT])
                for b in range(4):
                    act.wait_ge(z.sem, z.at(f"o{b}", i))
                    if b >= 2:
                        act.wait_ge(d.sem, d.at(f"oacc{b - 2}", i))
                    a.done(act.activation(gsq(b), ps[b][:, :], ACT.Square), f"osq{b}")
                act.wait_ge(z.sem, z.at("osum", i))
                root(a, "osqrt", rs, 4, GDV, "eps_ln")
                for b in range(4):
                    act.wait_ge(d.sem, d.at(f"oz{b}", i))
                    hi(a, f"oh{b}", go_hi[:, b], fx[:, 5 + b % 2, :])

            def layer_norm(name, k):
                a, d, z = enter(act, "act", name)
                split_p(a, k)
                act.wait_ge(z.sem, z.at("sum"))
                a.done(act.activation(fx[:, 3, :], ps[2][:, :], ACT.Copy, scale=1.0 / D), "mu")
                for m in M8:
                    act.wait_ge(d.sem, d.at(f"c{m}"))
                    if m >= 2:
                        act.wait_ge(d.sem, d.at(f"v{m - 2}"))
                    a.done(act.activation(sqs(m), fbuf[:, m], ACT.Square), f"sq{m}")
                    proj_out(name, m)
                act.wait_ge(z.sem, z.at("sum2"))
                root(a, "sqrt", rs, 3, D, "eps_ln")
                for m in M8:
                    act.wait_ge(d.sem, d.at(f"x{m}"))
                    hi(a, f"hi{m}", op_hi[:, m], h[:, m])

            layer_norm("ln1", 2)
            ple_gate(2)

            a, d, z = enter(act, "act", "idx")
            load_p(ins["p_2"][2:4])
            u = U0["idx"]

            def copy_out(b):
                act.wait_ge(unit_done, u + b + 1)
                if b >= 2:
                    act.wait_ge(d.sem, d.at(["lo0", "lo1", "lo2", "lo3"][b - 2]))
                hi(a, f"qf{b}", fx[:, 9 + b % 2, :], ps[b % 2][:, :])

            def high(b):
                act.wait_ge(d.sem, d.at(f"qa{b}"))
                hi(a, f"hi{b}", qi_hi[:, b], fx[:, 9 + b % 2, :])

            copy_out(0)
            copy_out(1)
            for b in range(4):
                high(b)
                copy_out(b + 2)
            act.wait_ge(d.sem, d.at("qa4"))
            act.wait_ge(d.sem, d.at("zero3"))
            hi(a, "kih0", ki_hi[0:64, 0], fx[0:64, 9, :])
            hi(a, "kih1", ki_hi[64:128, 1], fx[64:128, 9, :])
            act.wait_ge(d.sem, d.at("qa5"))
            hi(a, "kh", dk_hi[:, 0], fx[:, 10, :])
            act.wait_ge(unit_done, u + 7)
            hi(a, "vh", dv_hi[:, 0], ps[2][:, :])
            act.wait_ge(unit_done, u + 8)
            a.done(act.activation(st[:, 0:QT * IH], ps[3][:, 0:QT * IH], ACT.Copy, scale=INDEX_SCALE), "wi")
            for n, (q, x) in enumerate(pairs):
                w = P * (q + 1)
                act.wait_ge(z.sem, z.at(f"s{q}{x}"))
                if n >= 2:
                    act.wait_ge(d.sem, d.at("sc%d%d" % pairs[n - 2]))
                a.done(act.activation(fx[:, 7 + n % 2, 0:w], ps[4 + n % 2][:, 0:w], ACT.Relu), f"rel{q}{x}")

            a, d, z = enter(act, "act", "dsa_z", ())
            with act.Fori(0, DH // 2) as i:
                for n, x in enumerate("ab"):
                    act.wait_ge(unit_done, i * 2 + (U0["dsa_z"] + n + 1))
                    a.done(act.activation(fb[:, bass.ds(i * 2 + n, 1), :].rearrange("p a t -> p (a t)"), ps[n][:, :], ACT.Silu), f"z{x}")
            def dsa_heads(name, half, u0, i, i0, last):
                a, d, z = S[name]["act"], S[name]["dve"], S[name]["pe"]
                for hh, x in enumerate("ab"):
                    more = not (last and hh)
                    if more:
                        act.wait_ge(unit_done, i0 * 2 + (u0 + hh))
                        hi(a, f"qf{x}", fx[:, 10, :], ps[1 - hh][:, :])
                    exponentials(S[name], x, i, dsa_probs, (0, 1))
                    exponentials(S[name], x, i, dsa_probs, (2, 3))
                    turned_high(S[name], x, i, dpt_hi, (0, 1))
                    if more:
                        act.wait_ge(d.sem, d.at(f"qa{x}", i))
                        act.wait_ge(z.sem, z.at(f"s3{x}", i))
                        hi(a, f"qh{x}", dq_hi[:, 0], fx[:, 10, :])
                    turned_high(S[name], x, i, dpt_hi, (2, 3))
                    act.wait_ge(d.sem, d.at(f"oz{x}", i))
                    hi(a, f"oh{x}", oz_hi[:, bass.ds(i0 * 2 + hh, 1), :].rearrange("p a t -> p (a t)"), acc)

            a, d, z = enter(act, "act", "dsa_p")
            act.wait_ge(unit_done, U0["dsa0"] + 1)
            hi(a, "qf", fx[:, 10, :], ps[0][:, :])
            act.wait_ge(d.sem, d.at("qa"))
            hi(a, "qh", dq_hi[:, 0], fx[:, 10, :])
            for half in (0, 1):
                name = f"dsa{half}"
                u0 = U0[name] + (0 if half else 2)
                rounds = DH // 4 - half
                enter(act, "act", name)
                with act.Fori(0, rounds) as i:
                    dsa_heads(name, half, u0, i, i, False)
                if half:
                    enter(act, "act", "dsa1_end")
                    dsa_heads("dsa1_end", half, u0, 0, rounds, True)
                name = f"dout{half}"
                a, d, z = enter(act, "act", name)
            layer_norm("ln2", 3)
            ple_gate(3)

        @block.vector
        def _(dve):
            def lo(steps, name, o, src, high):
                steps.done(dve.tensor_tensor(o, src, high.bitcast(F32), ALU.subtract), name)

            def mul(steps, name, o, x, y):
                steps.done(dve.tensor_tensor(o, x, y, ALU.mult), name)

            def add(steps, name, o, x, y):
                steps.done(dve.tensor_tensor(o, x, y, ALU.add), name)

            def stt(steps, name, o, x, s, y, op0, op1):
                steps.done(dve.scalar_tensor_tensor(out=o, in0=x, scalar=s, in1=y, op0=op0, op1=op1), name)

            def sync(steps, name, i=0):
                dve.wait_ge(steps.sem, steps.at(name, i))

            def at(tile, i):
                return tile[:, bass.ds(i, 1), :].rearrange("p a t -> p (a t)")

            def accumulate(steps, name, first, s):
                if first:
                    steps.done(dve.tensor_copy(acc, s), name)
                else:
                    add(steps, name, acc, acc, s)

            zeroed = [0]

            def clear(x):
                dve.memset(x, 0.0).then_inc(cleared, 1)
                zeroed[0] += 1
                dve.wait_ge(cleared, zeroed[0])

            def rotate(steps, step, n, i, f, tmp, table, rows, half):
                size = 2 * half
                swap = [(r + half) % size + (r - r % size) if r % 32 < size else r for r in range(32)]
                if step == "sw":
                    dve.sem_inc(dve_held, 1)
                    steps.done(dve.stream_shuffle(tmp[rows, :], f[rows, :], swap), f"sw{n}")
                elif step == "qc":
                    sync(steps, f"sw{n}", i)
                    mul(steps, f"qc{n}", f[rows, :], f[rows, :], rope_cos[rows, table, :])
                elif step == "ss":
                    mul(steps, f"ss{n}", tmp[rows, :], tmp[rows, :], rope_sin[rows, table, :])
                else:
                    sync(steps, f"ss{n}", i)
                    add(steps, f"qa{n}", f[rows, :], f[rows, :], tmp[rows, :])

            def softmax(z, x, i, probs, pth, ptl, bias, scale, chore):
                a, d, e = z["act"], z["dve"], z["pe"]

                def mask(q):
                    sync(e, f"s{q}{x}", i)
                    dve.sem_inc(dve_held, 1)
                    d.done(dve.tensor_tensor_reduce(out=probs(q), in0=ps[3 + q % 2][:, 0:P * (q + 1)], in1=bias(q), scale=-scale,
                                                    scalar=3.0e38, op0=ALU.add, op1=ALU.min, accum_out=st[:, 40 + q:41 + q]), f"m{q}{x}")

                def normalise(q):
                    sync(a, f"e{q}{x}", i)
                    d.done(dve.reciprocal(st[:, 48 + q:49 + q], st[:, 44 + q:45 + q]), f"r{q}{x}")
                    sync(d, f"r{q}{x}", i)
                    d.done(dve.tensor_scalar(probs(q), probs(q), st[:, 48 + q:49 + q], None, ALU.mult), f"n{q}{x}")

                def low(q):
                    n = P * (q + 1)
                    sync(a, f"h{q}{x}", i)
                    lo(d, f"l{q}{x}", ptl[:, q % 2, 0:n], ps[5 + q % 2][:, 0:n], pth[:, q % 2, 0:n])

                mask(0)
                mask(1)
                chore(0)
                normalise(0)
                normalise(1)
                mask(2)
                mask(3)
                chore(1)
                normalise(2)
                normalise(3)
                low(0)
                low(1)
                chore(2)
                low(2)
                chore(3)
                low(3)

            dve.wait_ge(cst_in, 32)
            dve.wait_ge(x_in, 16)
            a, d, z = enter(dve, "dve", "start")
            sqs = sweep((2, 11))
            for m in M8:
                sync(a, f"hi{m}")
                stt(d, f"lo{m}", op_lo[:, m], h[:, m], gcol("g_mix_pre", m), op_hi[:, m].bitcast(F32), ALU.mult, ALU.subtract)
                sync(a, f"sq{m}")
                accumulate(d, f"acc{m}", m == 0, sqs(m))
                sync(d, f"acc{m}")
            sync(a, "sqrt")
            d.done(dve.reciprocal(rs, rs), "rs")
            dve.wait_ge(pos_in, 32)
            d.done(dve.tensor_copy(fx[:, 6:8, :], fx[:, 9:11, :].bitcast(I32)), "pos")
            sync(d, "pos")
            for t in range(3):
                d.done(dve.tensor_scalar(fx[:, 3 + t, :], fx[:, 6 + (t > 0), :], const("inv_freq")[:, t:t + 1], None, ALU.mult), f"ang{t}")
            sync(d, "ang2")
            ang, turns = fx[:, 3:6, :], fx[:, 6:9, :]
            magic = 1.5 * 2 ** 23
            d.done(dve.tensor_scalar(turns, ang, 1.0 / (2 * np.pi), magic, ALU.mult, ALU.add), "turn")
            sync(d, "turn")
            d.done(dve.tensor_scalar(turns, turns, magic, None, ALU.subtract), "whole")
            sync(d, "whole")
            for n, part in enumerate(TURN):
                stt(d, f"red{n + 1}", ang, turns, -part, ang, ALU.mult, ALU.add)
                sync(d, f"red{n + 1}")
            d.done(dve.tensor_scalar(ang, ang, PI, -PI, ALU.min, ALU.max), "clip")
            sync(a, "abs")
            d.done(dve.tensor_scalar(turns, turns, -1.0, np.pi / 2, ALU.mult, ALU.add), "quarter")
            sync(a, "sin")
            for t in range(3):
                d.done(dve.tensor_scalar(rope_sin[:, t, :], rope_sin[:, t, :], const("sign")[:, t:t + 1], None, ALU.mult), f"sin{t}")

            a, d, z = enter(dve, "dve", "lat")
            lat = fx[:, 3:8, :]

            def scaled(b):
                dve.wait_ge(unit_done, U0["lat"] + b + 1)
                mul(d, f"z{b}" if b < 5 else "kr", lat[:, b] if b < 5 else fx[:, 10, :], ps[b % 2][:, :], rs)

            def squares(b):
                sync(a, f"sq{b}")
                accumulate(d, f"acc{b}", b in (0, 3), sqs(b))
                sync(d, f"acc{b}")

            for b in range(3):
                scaled(b)
            for b in range(3):
                squares(b)
            for b in (3, 4, 5):
                scaled(b)
            sync(a, "sqrt_q")
            d.done(dve.reciprocal(fx[:, 8, :], fx[:, 8, :]), "rs_q")
            squares(3)
            squares(4)
            sync(a, "sqrt_kv")
            d.done(dve.reciprocal(fx[:, 9, :], fx[:, 9, :]), "rs_kv")
            sync(d, "rs_kv")
            for b in LB:
                g, o_hi, o_lo = ((gcol("g_q_lat", b), qn_hi[:, b], qn_lo[:, b]) if b < 3 else
                                 (gcol("g_kv_lat", b - 3), kvn_hi[:, b - 3], kvn_lo[:, b - 3]))
                stt(d, f"n{b}", lat[:, b], lat[:, b], g, fx[:, 8 + (b > 2), :], ALU.mult, ALU.mult)
                sync(a, f"hi{b}")
                lo(d, f"lo{b}", o_lo, lat[:, b], o_hi)
            kr, tmp = fx[:, 10, :], fx[:, 2, :]
            d.done(dve.stream_shuffle(tmp, kr, [(r + 16) % 32 for r in range(32)]), "swap")
            sync(d, "swap")
            mul(d, "swap_sin", tmp, tmp, rope_sin[:, 0, :])
            mul(d, "kr_cos", kr, kr, rope_cos[:, 0, :])
            sync(d, "kr_cos")
            add(d, "kr_rot", kr, kr, tmp)
            sync(a, "k0h")
            lo(d, "k0l", ak_lo[0:64, 0], kr[0:64, :], ak_hi[0:64, 0])
            sync(a, "k1h")
            lo(d, "k1l", ak_lo[64:128, 1], kr[64:128, :], ak_hi[64:128, 1])

            krows = (slice(64, 128), slice(0, 64))
            rrows = (slice(0, 32), slice(64, 96))
            orows = (slice(0, 64), slice(64, 128))

            def mla_chore(a, d, x, hh, i, k):
                def turn(step):
                    rotate(d, step, x, i, fx[:, 3, :], fx[:, 4, :], 0, rrows[hh], ROPE // 2)

                if k == 0:
                    sync(a, f"kh{x}", i)
                    lo(d, f"kl{x}", ak_lo[krows[hh], hh], ps[1][krows[hh], :], ak_hi[krows[hh], hh])
                    turn("sw")
                elif k == 1:
                    turn("qc")
                    turn("ss")
                    sync(a, f"vh{x}", i)
                    lo(d, f"vl{x}", av[hh][1][:, 0], ps[2][:, :], av[hh][0][:, 0])
                elif k == 2:
                    turn("qa")
                else:
                    sync(a, f"qh{x}", i)
                    lo(d, f"ql{x}", aq_lo[:, 0], fx[:, 3, :], aq_hi[:, 0])

            def mla_heads(name, i, i0, last):
                a, d, z = S[name]["act"], S[name]["dve"], S[name]["pe"]
                for hh, x in enumerate("ab"):
                    def chore(k):
                        if not (last and hh):
                            mla_chore(a, d, x, 1 - hh, i, k)

                    softmax(S[name], x, i, mla_probs, apt_hi, apt_lo, lambda q: const("mla_bias")[:, T - P * (q + 1):T],
                            MLA_SCALE, chore)
                    sync(a, f"oh{x}", i)
                    lo(d, f"ol{x}", ob_lo[orows[hh], bass.ds(i0, 1), :].rearrange("p a t -> p (a t)"), ps[7][orows[hh], :],
                       ob_hi[orows[hh], bass.ds(i0, 1), :].rearrange("p a t -> p (a t)"))

            a, d, z = enter(dve, "dve", "mla0")
            for k in range(4):
                mla_chore(a, d, "", 0, 0, k)
            enter(dve, "dve", "mla")
            with dve.Fori(0, NH // 2 - 1) as i:
                mla_heads("mla", i, i, False)
            enter(dve, "dve", "mla_end")
            mla_heads("mla_end", 0, NH // 2 - 1, True)

            a, d, z = enter(dve, "dve", "conv")
            tA, tB, cc, yy = fx[:, 3, :], fx[:, 4, :], fx[:, 5, :], fx[:, 7, :]
            with dve.Fori(0, JC // 2) as i:
                for jj, x in enumerate("ab"):
                    j = i * 2 + jj
                    u = i * 6 + (U0["conv"] + 3 * jj)
                    sync(d, "lob" if jj == 0 else "loa", i - 1 if jj == 0 else i)
                    for n, (name, o) in enumerate((("ac", tA), ("ax", tB))):
                        dve.wait_ge(unit_done, u + (n + 1))
                        mul(d, name + x, o, ps[(3 * jj + n) % 2][:, :], rs)
                    sync(d, f"ax{x}", i)
                    mul(d, f"c{x}", cc, tA, tB)
                    sync(d, f"c{x}", i)
                    dve.wait_ge(unit_done, u + 3)
                    mul(d, f"ab{x}", tA, ps[(3 * jj + 2) % 2][:, :], rs)
                    d.done(dve.tensor_scalar(yy, cc, gcol("conv_a_w", j + 2 * JC), None, ALU.mult), f"y0{x}")
                    sync(d, f"y0{x}", i)
                    stt(d, f"y1{x}", yy[:, 1:T], cc[:, 0:T - 1], gcol("conv_a_w", j + JC), yy[:, 1:T], ALU.mult, ALU.add)
                    sync(d, f"y1{x}", i)
                    stt(d, f"y2{x}", yy[:, 2:T], cc[:, 0:T - 2], gcol("conv_a_w", j), yy[:, 2:T], ALU.mult, ALU.add)
                    sync(d, f"y2{x}", i)
                    mul(d, f"ya{x}", yy, yy, tA)
                    sync(a, f"hi{x}", i)
                    lo(d, f"lo{x}", at(ya_lo, j), yy, at(ya_hi, j))

            a, d, z = enter(dve, "dve", "mix")
            with dve.Fori(0, KD // 2) as i:
                for m, x in enumerate("ab"):
                    u = i * 6 + (U0["mix"] + 3 * m)
                    ga, gb = fx[:, 3 + 2 * m, :], fx[:, 4 + 2 * m, :]
                    dve.wait_ge(unit_done, u + 1)
                    mul(d, f"ga{x}", ga, ps[4 * m][:, :], rs)
                    dve.wait_ge(unit_done, u + 2)
                    mul(d, f"gb{x}", gb, ps[4 * m + 1][:, :], rs)
                    dve.wait_ge(unit_done, u + 3)
                    sync(a, f"sa{x}", i)
                    mul(d, f"ma{x}", ga, ps[4 * m + 2][:, :], ga)
                    sync(a, f"sb{x}", i)
                    mul(d, f"mb{x}", gb, ps[4 * m + 3][:, :], gb)
                    sync(d, f"mb{x}", i)
                    add(d, f"mx{x}", ga, ga, gb)
                    sync(a, f"hi{x}", i)
                    lo(d, f"lo{x}", at(mix_lo, i * 2 + m), ga, at(mix_hi, i * 2 + m))

            a, d, z = enter(dve, "dve", "wo")
            clear(acc)
            with dve.Fori(0, KD // 2) as i:
                for m, x in enumerate("ab"):
                    sync(a, f"sq{x}", i)
                    add(d, f"acc{x}", acc, acc, sqs(m))
                    sync(d, f"acc{x}", i)

            def post_norm(a, d, f, g):
                sync(a, "sqrt")
                d.done(dve.reciprocal(rs, rs), "rs")
                sync(d, "rs")

                def update(m):
                    stt(d, f"sc{m}", f[:, m], f[:, m], gcol(g, m), rs, ALU.mult, ALU.mult)
                    sync(d, f"sc{m}")
                    add(d, f"h{m}", h[:, m], h[:, m], f[:, m])

                return update

            def split_p(a, d):
                for n in range(2):
                    sync(a, f"ph{n}")
                    lo(d, f"pl{n}", p_lo[:, n], p_raw[n], p_hi[:, n])

            a, d, z = enter(dve, "dve", "res1")
            split_p(a, d)
            update = post_norm(a, d, fbuf, "g_mix_post")
            for m in M8:
                update(m)
                sync(a, f"hi{m}")
                stt(d, f"lo{m}", op_lo[:, m], h[:, m], gcol("g_ffn_pre", m), op_hi[:, m].bitcast(F32), ALU.mult, ALU.subtract)
                sync(a, f"sq{m}")
                accumulate(d, f"acc{m}", m == 0, sqs(m))
                sync(d, f"acc{m}")
            sync(a, "sqrt2")
            d.done(dve.reciprocal(rs, rs), "rs2")

            for half in (0, 1):
                name = f"up{half}"
                a, d, z = enter(dve, "dve", name)

                def ffn_block(i, ready, banks):
                    for n, x in enumerate("gv"):
                        c, y = fx[:, 3 + n, :], fx[:, 5 + n, :]
                        blk = i + (half * HJ + n * JF)
                        dve.wait_ge(unit_done, ready[n])
                        mul(d, x, c, ps[banks + n][:, :], rs)
                        sync(d, x, i)
                        d.done(dve.tensor_scalar(y, c, gcol("conv_ffn_w", blk + 4 * JF), gcol("b_ffn_conv", blk), ALU.mult, ALU.add), f"{x}0")
                        sync(d, f"{x}0", i)
                        stt(d, f"{x}1", y[:, 1:T], c[:, 0:T - 1], gcol("conv_ffn_w", blk + 2 * JF), y[:, 1:T], ALU.mult, ALU.add)
                        sync(d, f"{x}1", i)
                        stt(d, f"{x}2", y[:, 2:T], c[:, 0:T - 2], gcol("conv_ffn_w", blk), y[:, 2:T], ALU.mult, ALU.add)
                    sync(d, "v2", i)
                    sync(a, "ge", i)
                    mul(d, "pr", fx[:, 6, :], fx[:, 5, :], fx[:, 6, :])
                    sync(a, "hi", i)
                    lo(d, "lo", at(f_lo, i), fx[:, 6, :], at(f_hi, i))

                if half == 0:
                    for i in range(2):
                        ffn_block(i, [U0[name] + 4] * 2, 2 * i)
                with dve.Fori(0 if half else 2, HJ) as i:
                    ffn_block(i, [i * 2 + (U0[name] + n + 1) for n in range(2)], 4)
                name = f"down{half}"
                a, d, z = enter(dve, "dve", name)
                if half:
                    clear(acc)
                    with dve.Fori(0, 2) as i:
                        for m in range(4):
                            dve.wait_ge(unit_done, i * 6 + (U0[name] + 3 * (m // 2) + 2 + m % 2))
                            fm = at(fbuf, i * 4 + m)
                            add(d, f"f{m}", fm, fm, ps[m][:, :])
                            sync(a, f"sq{m}", i)
                            add(d, f"acc{m}", acc, acc, sqs(m))
                            sync(d, f"acc{m}", i)

            def ple_gate(k):
                a, d, z = enter(dve, "dve", f"ple{k}")
                if k == 1:
                    clear(acc)
                for m in M8:
                    i, x = m // 2, "ab"[m % 2]
                    e = ebuf[:, m]
                    sync(a, f"g{x}", i)
                    mul(d, f"e{x}", e, e, fx[:, 3 + m % 2, :])
                    if k == 1:
                        sync(a, f"sq{x}", i)
                        add(d, f"acc{x}", acc, acc, sqs(m))
                        sync(d, f"acc{x}", i)
                    else:
                        sync(d, f"e{x}", i)
                        add(d, f"h{x}", h[:, m], h[:, m], e)
                    if k == 2:
                        sync(d, f"h{x}", i)
                        d.done(dve.tensor_scalar(fbuf[:, m], h[:, m], ALPHA, None, ALU.mult), f"t{x}")
                        sync(a, f"hi{x}", i)
                        lo(d, f"lo{x}", x2_lo[:, m], h[:, m], x2_hi[:, m])

            def residual(name, f, g):
                a, d, z = enter(dve, "dve", name)
                update = post_norm(a, d, f, g)
                for m in M8:
                    update(m)
                    sync(a, f"hi{m}")
                    lo(d, f"lo{m}", op_lo[:, m], h[:, m], op_hi[:, m])

            residual("res2", fbuf, "g_ffn_post")
            ple_gate(1)
            residual("res3", ebuf, "g_ple_post")

            a, d, z = enter(dve, "dve", "gla_a")
            d.done(dve.tensor_scalar(fbuf.rearrange("p k t -> p (k t)"), h.rearrange("p k t -> p (k t)"), ALPHA, None, ALU.mult), "zero_y")
            d.done(dve.memset(fx[:, 9:12, :], 0.0), "zero_at")
            sync(a, "ah")
            lo(d, "al", ga_lo[:, 0], ps[0][:, :], ga_hi[:, 0])
            for m in M8:
                sync(a, f"ab{m}")
                t = fx[:, 5 + m % 2, :]
                d.done(dve.tensor_scalar(t, ps[1 + m % 4][:, :], gcol("gla_b_a_2", m), 0.0, ALU.add, ALU.min), f"mn{m}")
                sync(a, f"ln{m}")
                sync(d, f"mn{m}")
                d.done(dve.tensor_tensor(ebuf[:, m], t, fx[:, 3 + m % 2, :], ALU.subtract), f"g{m}")

            a, d, z = enter(dve, "dve", "gla")
            g64, gl = fx[:, 3, :], fx[:, 4, :]
            ex, tm = fx[:, 5:7, :].rearrange("p k t -> p (k t)"), fx[:, 7:9, :].rearrange("p k t -> p (k t)")
            atf = fx[:, 9:12, :].rearrange("p k t -> p (k t)")
            gsq = sweep((2, 7))
            with dve.Fori(0, GH) as i:
                base = i * 16 + U0["gla"]

                def prep(b):
                    g = at(ebuf, i * 2 + b)
                    if b:
                        sync(a, "x0j3", i)
                    d.done(dve.tensor_tensor_scan(g64, const("reset"), g, 0.0, ALU.mult, ALU.add), f"s64{b}")
                    d.done(dve.tensor_tensor_scan(gl, const("ones"), g, 0.0, ALU.mult, ALU.add), f"sgl{b}")
                    sync(d, f"sgl{b}", i)
                    ends = gl.rearrange("p (j t) -> p j t", t=P)[:, :, P - 1]
                    d.done(dve.tensor_scalar(st[:, 8 * b:8 * b + 4], ends, -1.0 / GATE_NORM, None, ALU.mult), f"ne{b}")
                    d.done(dve.tensor_scalar(st[:, 8 * b + 4:8 * b + 8], ends, 1.0 / GATE_NORM, None, ALU.mult), f"po{b}")
                    for n, (name, src) in enumerate((("qt", h[:, b]), ("kt", h[:, 2 + b]), ("ks", h[:, 2 + b]))):
                        if n == 0:
                            sync(a, "k1", i)
                        sync(a, f"x{b}{name}" if n < 2 else f"x{b}s{QT - 1}", i)
                        if n:
                            sync(d, f"l{b}{('qt', 'kt')[n - 1]}", i)
                        mul(d, f"m{b}{name}", tm[:, 0:T], src, ex[:, 0:T])
                        sync(a, f"h{b}{name}", i)
                        lo(d, f"l{b}{name}", ga_lo[:, n], tm[:, 0:T], ga_hi[:, n])
                    for j in range(QT):
                        q0, n = q_span(j)
                        if j == 0:
                            sync(d, f"l{b}ks", i)
                        sync(a, f"x{b}j{j}", i)
                        mul(d, f"m{b}j{j}", tm[:, q0:q0 + n], h[:, b, T - n:T], ex[:, q0:q0 + n])
                    sync(a, f"h{b}qj", i)
                    lo(d, f"l{b}qj", ga_lo[:, 3:5].rearrange("p k t -> p (k t)"), tm, ga_hi[:, 3:5].rearrange("p k t -> p (k t)"))

                prep(0)
                for t in range(QT):
                    sync(a, f"vh{t}", i)
                    lo(d, f"vl{t}", gv_lo[:, t], ps[t][:, :], gv_hi[:, t])
                prep(1)
                sync(z, "A1", i)
                dve.sem_inc(dve_held, 1)
                for j in range(QT):
                    o = GLA_PACK[j]
                    d.done(dve.copy_predicated(atf[:, o:o + P], const("tri").bitcast(U32), ps[4][:, j * P:(j + 1) * P]), f"ad{j}")
                for j in range(QT):
                    o = GLA_PACK[j]
                    q0, n = q_span(j)
                    bank, c = GLA_BANK[j]
                    sync(d, f"ad{j}", i)
                    d.done(dve.tensor_copy(atf[0:CHUNK, o + CHUNK:o + P], ps[bank][0:CHUNK, c:c + CHUNK]), f"ac{j}")
                    if j < QT - 1:
                        d.done(dve.tensor_copy(atf[:, o + P:o + T - j * P], ps[bank][:, c + CHUNK:c + n]), f"ao{j}")
                sync(a, "ath", i)
                lo(d, "atl", at_lo.rearrange("p k t -> p (k t)")[:, 0:GLA_AT], atf[:, 0:GLA_AT],
                   at_hi.rearrange("p k t -> p (k t)")[:, 0:GLA_AT])
                for b in range(4):
                    sync(a, f"osq{b}", i)
                    accumulate(d, f"oacc{b}", b == 0, gsq(b))
                    sync(d, f"oacc{b}", i)
                sync(a, "osqrt", i)
                d.done(dve.reciprocal(rs, rs), "ors")
                sync(d, "ors", i)
                for b in range(4):
                    t = fx[:, 5 + b % 2, :]
                    mul(d, f"on{b}", t, ps[b][:, :], rs)
                    sync(d, f"on{b}", i)
                    stt(d, f"oz{b}", t, t, gcol("gla_gn_g_2", i * 4 + b), h[:, 4 + b], ALU.mult, ALU.mult)
                    sync(a, f"oh{b}", i)
                    lo(d, f"ol{b}", go_lo[:, b], t, go_hi[:, b])
                for m in M8:
                    if m % 2 == 0:
                        sync(z, f"y{m}", i)
                    else:
                        dve.wait_ge(unit_done, base + (12 + m // 2 + 1))
                    add(d, f"y{m}", fbuf[:, m], fbuf[:, m], ps[4 + (m + 1) % 4][:, :])

            def layer_norm(name, k):
                a, d, z = enter(dve, "dve", name)
                split_p(a, d)
                if name == "ln1":
                    for m in M8:
                        accumulate(d, f"acc{m}", m == 0, fbuf[:, m])
                        sync(d, f"acc{m}")
                sync(a, "mu")
                for m in M8:
                    d.done(dve.tensor_tensor(fbuf[:, m], fbuf[:, m], fx[:, 3, :], ALU.subtract), f"c{m}")
                    sync(a, f"sq{m}")
                    accumulate(d, f"v{m}", m == 0, sqs(m))
                    sync(d, f"v{m}")
                sync(a, "sqrt")
                d.done(dve.reciprocal(rs, rs), "rs")
                sync(d, "rs")
                for m in M8:
                    mul(d, f"n{m}", fbuf[:, m], fbuf[:, m], rs)
                    sync(d, f"n{m}")
                    d.done(dve.tensor_scalar(h[:, m], fbuf[:, m], gcol("ln_g_2", k * KD + m), gcol("ln_b_2", k * KD + m),
                                             ALU.mult, ALU.add), f"x{m}")
                    sync(a, f"hi{m}")
                    lo(d, f"lo{m}", op_lo[:, m], h[:, m], op_hi[:, m])

            layer_norm("ln1", 0)
            ple_gate(2)

            a, d, z = enter(dve, "dve", "idx")
            for n, tile in enumerate((ki_hi[:, 0], ki_hi[:, 1], ki_lo[:, 0], ki_lo[:, 1])):
                d.done(dve.tensor_scalar(tile, const("ones"), 0.0, None, ALU.mult), f"zero{n}")
            for b in range(6):
                f = fx[:, 9 + b % 2, :]
                sync(a, f"qf{b}")
                rows, table, half = (slice(0, P), 2, ID // 8) if b < 5 else (slice(0, 32), 1, DHD // 8)
                for step in ("sw", "qc", "ss", "qa"):
                    rotate(d, step, str(b), 0, f, fx[:, 11, :], table, rows, half)
                if b < 4:
                    sync(a, f"hi{b}")
                    lo(d, f"lo{b}", qi_lo[:, b], f, qi_hi[:, b])
                elif b == 4:
                    sync(a, "kih0")
                    lo(d, "kil0", ki_lo[0:64, 0], f[0:64, :], ki_hi[0:64, 0])
                    sync(a, "kih1")
                    lo(d, "kil1", ki_lo[64:128, 1], f[64:128, :], ki_hi[64:128, 1])
                else:
                    sync(a, "kh")
                    lo(d, "kl", dk_lo[:, 0], f, dk_hi[:, 0])
            sync(a, "vh")
            lo(d, "vl", dv_lo[:, 0], ps[2][:, :], dv_hi[:, 0])
            sync(a, "wi")
            for n, (q, x) in enumerate(pairs):
                w = P * (q + 1)
                sync(a, f"rel{q}{x}")
                s, rel, wt = fx[:, 3 + q, 0:w], fx[:, 7 + n % 2, 0:w], st[:, q * IH + x:q * IH + x + 1]
                if x == 0:
                    d.done(dve.tensor_scalar(s, rel, wt, None, ALU.mult), f"sc{q}{x}")
                else:
                    stt(d, f"sc{q}{x}", s, rel, wt, s, ALU.mult, ALU.add)
                sync(d, f"sc{q}{x}")
            for q in range(1, QT):
                s = fx[:, 3 + q, q * P:(q + 1) * P]
                add(d, f"ca{q}", s, s, const("causal")[:, T - P:T])
            for q in range(1, QT):
                s = fx[:, 3 + q, 0:P * (q + 1)]
                sync(d, f"ca{q}")
                for r in range(TOPK // 8):
                    d.done(dve.max(st[:, 32:40], s), f"mx{q}_{r}")
                    sync(d, f"mx{q}_{r}")
                    d.done(dve.match_replace(s, st[:, 32:40], s, TAKEN), f"mr{q}_{r}")
                    sync(d, f"mr{q}_{r}")
            for q in range(1, QT):
                s = fx[:, 3 + q, 0:P * (q + 1)]
                d.done(dve.tensor_scalar(s, s, 0.5 * TAKEN, MASKED, ALU.is_gt, ALU.mult), f"sel{q}")

            enter(dve, "dve", "dsa_z", ())
            def dsa_chore(a, d, x, i, k):
                def turn(step):
                    rotate(d, step, x, i, fx[:, 10, :], fx[:, 11, :], 1, slice(0, 32), DHD // 8)

                if k == 0:
                    sync(a, f"qf{x}", i)
                    turn("sw")
                elif k == 1:
                    turn("qc")
                    turn("ss")
                elif k == 2:
                    turn("qa")
                else:
                    sync(a, f"qh{x}", i)
                    lo(d, f"ql{x}", dq_lo[:, 0], fx[:, 10, :], dq_hi[:, 0])

            def dsa_heads(name, half, i, i0, last):
                a, d, z = S[name]["act"], S[name]["dve"], S[name]["pe"]
                for hh, x in enumerate("ab"):
                    def chore(k):
                        if not (last and hh):
                            dsa_chore(a, d, x, i, k)

                    softmax(S[name], x, i, dsa_probs, dpt_hi, dpt_lo,
                            lambda q: fx[:, 3 + q, 0:P * (q + 1)] if q else const("causal")[:, T - P:T], DSA_SCALE, chore)
                    sync(z, f"o3{x}", i)
                    mul(d, f"oz{x}", acc, ps[7][:, :], at(fb, i0 * 2 + (hh + half * DH // 2)))
                    sync(a, f"oh{x}", i)
                    lo(d, f"ol{x}", at(oz_lo, i0 * 2 + hh), acc, at(oz_hi, i0 * 2 + hh))

            a, d, z = enter(dve, "dve", "dsa_p")
            for k in range(4):
                dsa_chore(a, d, "", 0, k)
            for half in (0, 1):
                name = f"dsa{half}"
                rounds = DH // 4 - half
                enter(dve, "dve", name)
                with dve.Fori(0, rounds) as i:
                    dsa_heads(name, half, i, i, False)
                if half:
                    enter(dve, "dve", "dsa1_end")
                    dsa_heads("dsa1_end", half, 0, rounds, True)
                name = f"dout{half}"
                a, d, z = enter(dve, "dve", name)
                if half:
                    clear(acc)
                with dve.Fori(0, KD // 2) as i:
                    for m, x in enumerate("ab"):
                        dve.wait_ge(unit_done, i * 2 + (U0[name] + m + 1))
                        f = at(fbuf, i * 2 + m)
                        add(d, f"f{x}", f, f, ps[5 + m][:, :])
                        if half:
                            sync(d, f"f{x}", i)
                            add(d, f"acc{x}", acc, acc, f)
            layer_norm("ln2", 1)
            ple_gate(3)

    return nc


def blocks_of(w, rows, cols):
    return w[rows, cols].reshape(-1, P, w[rows, cols].shape[1]).transpose(1, 0, 2)


def weight_units(a):
    units = []

    def put(*parts):
        u = np.zeros((P, 8 * P), np.float32)
        at = 0
        for x in parts:
            x = x.reshape(P, -1)
            u[:, at:at + x.shape[1]] = x
            at += x.shape[1]
        units.append(u)

    def col(w, c, n=P):
        return blocks_of(w, slice(None), slice(c, c + n))

    def wide(w, pieces):
        x = np.zeros((w.shape[0], P), np.float32)
        for at, c, n in pieces:
            x[:, at:at + n] = w[:, c:c + n]
        return col(x, 0)

    def blockwise(four):
        for c in range(4):
            put(*[x[:, 2 * c + kk:2 * c + kk + 1] for kk in range(2) for x in four])

    def projection(proj):
        for m in range(0, KD, 4):
            put(*[col(proj, (m + n) * P) for n in range(4)])

    def gate(w):
        blockwise([col(w, m * P) for m in range(4)])
        for m in range(4, KD):
            put(col(w, m * P))

    w = a["w_in"][0]
    c_q = 3 * CONV
    c_kv = c_q + QL
    c_r = c_kv + KVL
    c_ga = c_r + ROPE
    for b in range((QL + KVL) // P):
        put(col(w, c_q + b * P))
    put(wide(w, [(0, c_r, ROPE), (64, c_r, ROPE)]))
    wq, wkv = a["w_q_up"][0], a["w_kv_up"][0]
    for n in range(NH):
        q, k = n * (NOPE + ROPE), n * (NOPE + VD)
        if n % 2 == 0:
            put(wide(wq, [(0, q + NOPE, ROPE), (64, q, NOPE)]), wide(wkv, [(0, k + NOPE, VD), (64, k, NOPE)]))
        else:
            put(wide(wq, [(0, q, NOPE), (64, q + NOPE, ROPE)]), wide(wkv, [(0, k, NOPE), (64, k + NOPE, VD)]))
    for j in range(JC):
        for part in (1, 2, 0):
            put(col(w, part * CONV + j * P))
    for m in range(KD):
        put(col(w, c_ga + m * P))
        put(col(w, c_ga + D + m * P))
        put(col(a["w_a_out"][0], m * P), col(a["w_b_out"][0], m * P))
    for m in range(KD):
        put(col(a["w_o"][0], m * P))
    projection(a["w_ple_proj"][0])
    w = a["w_ffn_up"][0]
    for half in range(2):
        first = half * HJ
        if half == 0:
            blockwise([col(w, c) for j in range(2) for c in (j * P, DFF + j * P)])
            first = 2
        for j in range(first, (half + 1) * HJ):
            put(col(w, j * P))
            put(col(w, DFF + j * P))
        down = a["w_ffn_down"][0][half * HJ * P:(half + 1) * HJ * P]
        for m in range(0, KD, 2):
            both = np.concatenate([col(down, m * P), col(down, (m + 1) * P)], axis=1)
            for v in range(3):
                put(both[:, 8 * v:8 * v + 8])

    gate(a["w_ple_gate"][0])
    w = a["gla_w_in_2"][0]
    qk = GH * GDK
    put(wide(w, [(0, 2 * qk + 2 * DI, GRANK)]))
    up = np.zeros((P, D), np.float32)
    up[:GRANK] = a["gla_w_a2_2"][0]
    put(up)
    for n in range(GH):
        for c in (n * GDK, n * GDK + P, qk + n * GDK, qk + n * GDK + P):
            put(col(w, c))
        v = col(w, 2 * qk + n * GDV, GDV)
        for c in range(4):
            put(v[:, 2 * c:2 * c + 2])
        for b in range(4):
            put(col(w, 2 * qk + DI + n * GDV + b * P))
        rows = a["gla_w_out_2"][0][n * GDV:(n + 1) * GDV]
        for m in range(0, KD, 2):
            put(col(rows, m * P), col(rows, (m + 1) * P))
    projection(a["ple_w_2"][0])
    gate(a["ple_gate_w_2"][0])
    w = a["dsa_w_in_2"][0]
    c_k, c_v, c_z = DI, DI + DHD, DI + 2 * DHD
    c_qi = c_z + DI
    c_ki = c_qi + IH * ID
    c_wi = c_ki + ID
    for b in range(4):
        put(col(w, c_qi + b * P))
    put(wide(w, [(0, c_ki, ID), (ID, c_ki, ID)]))
    put(col(w, c_k))
    put(col(w, c_v))
    put(wide(w, [(0, c_wi, IH)]))
    for n in range(DH):
        put(col(w, c_z + n * P))
    for half, heads in enumerate((range(DH // 2 + 2), range(DH // 2 + 2, DH))):
        for n in heads:
            put(col(w, n * P))
        rows = a["dsa_w_out_2"][0][half * D:(half + 1) * D]
        for m in range(KD):
            put(col(rows, m * P))
    projection(a["ple_w_2"][1])
    gate(a["ple_gate_w_2"][1])
    assert len(units) == UNITS, (len(units), UNITS)
    return np.stack(units)


def constants():
    c = np.zeros((P, CONSTS), np.float32)

    def put(name, x):
        c[:, C0[name]:C0[name] + x.shape[1]] = x

    r = np.arange(P)
    put("ident", np.eye(P, dtype=np.float32))
    put("ones", np.ones((P, T), np.float32))
    mla, causal = np.zeros((P, T), np.float32), np.zeros((P, T), np.float32)
    mla[:, T - P:] = np.where(r[None, :] // CHUNK <= r[:, None] // CHUNK, 0.0, MASKED)
    causal[:, T - P:] = np.where(r[None, :] <= r[:, None], 0.0, MASKED)
    put("mla_bias", mla)
    put("causal", causal)
    put("tri", ((r[:, None] <= r[None, :]) & (r[:, None] // CHUNK == r[None, :] // CHUNK)).astype(np.float32))
    put("reset", np.broadcast_to(np.arange(T) % CHUNK != 0, (P, T)).astype(np.float32))

    def frequencies(theta, rot, period):
        half = rot // 2
        inv = (np.float32(1.0) / np.float32(theta) ** (np.arange(half, dtype=np.float32) * np.float32(2.0 / rot))).astype(np.float32)
        f, s = np.zeros(P, np.float32), np.ones(P, np.float32)
        on = r % period < rot
        f[on] = inv[(r[on] % period) % half]
        s[on] = np.where(r[on] % period < half, -1.0, 1.0)
        return f, s

    tables = [frequencies(THETA_1, ROPE, 32), frequencies(THETA_2, DHD // 4, 32), frequencies(THETA_2, ID // 4, ID)]
    put("inv_freq", np.stack([f for f, _ in tables], axis=1))
    put("sign", np.stack([s for _, s in tables], axis=1))
    put("eps", np.full((P, 1), EPS, np.float32))
    put("eps_ln", np.full((P, 1), NORM_EPS, np.float32))
    put("one", np.ones((P, 1), np.float32))
    return c


def arrays_of(a):
    def columns(x):
        return x.reshape(-1, P).T

    def turned(x):
        return np.ascontiguousarray(np.swapaxes(x, -1, -2)).reshape(-1, P, T)

    gains = np.concatenate([columns(np.asarray(a[name])) for name, _ in GAIN_COLS], axis=1)
    return {"x": turned(a["x"][0]), "p": turned(a["p"][0, 0]), "p_2": turned(a["p_2"][:, 0]),
            "positions": np.ascontiguousarray(a["positions"]), "positions_2": np.ascontiguousarray(a["positions_2"]),
            "gains": np.ascontiguousarray(gains), "consts": constants(), "weights": weight_units(a)}


def kernel(**inputs):
    import concourse.bacc as bacc
    from concourse.bass_utils import run_bass_kernel_spmd

    arrays = arrays_of({n: np.asarray(x) for n, x in inputs.items()})
    nc = bacc.Bacc("TRN2", target_bir_lowering=False, num_devices=1, dynamic_dma_scratch_size=1024)
    ins = {n: nc.dram_tensor(f"in_{n}", x.shape, mybir.dt.from_np(x.dtype), kind="ExternalInput").ap() for n, x in arrays.items()}
    out = nc.dram_tensor("out_0", (KD, P, T), F32, kind="ExternalOutput").ap()
    build(nc, ins, out)
    r = run_bass_kernel_spmd(nc, [{f"in_{n}": x for n, x in arrays.items()}], core_ids=[0])
    return np.ascontiguousarray(r.results[0]["out_0"].reshape(D, T).T).reshape(1, T, D)
```

```python
import numpy as np
from contextlib import ExitStack

import concourse.bass as bass
from concourse import mybir

F32 = mybir.dt.float32
F32R = mybir.dt.float32r
I32 = mybir.dt.int32
U32 = mybir.dt.uint32
ACT = mybir.ActivationFunctionType
ALU = mybir.AluOpType

P = 128
T = 512
QT = T // P
D = 1024
KD = D // P
CONV = 512
JC = CONV // P
NH, NOPE, ROPE, VD = 8, 64, 32, 64
QL, KVL = 384, 256
DFF = 2816
JF = DFF // P
HJ = JF // 2
PLE = 256
EPS = 1e-6
MLA_SCALE = (NOPE + ROPE) ** -0.5
THETA_1, THETA_2 = 10000.0, 500000.0
DI = 2048
GH, GDK, GDV, GRANK = 4, 256, 512, 16
GATE_NORM = 16.0
CHUNK = 64
DH, DHD = 16, 128
IH, ID = 8, 64
TOPK = 128
DSA_SCALE = DHD ** -0.5
INDEX_SCALE = (IH ** -0.5) * (ID ** -0.5)
ALPHA = 4 ** 0.25
NORM_EPS = 1e-5
MASKED = -1.0e30
TAKEN = -3.0e38

STAGES = [("lat", 6), ("mla", NH), ("conv", 3 * JC), ("mix", 3 * KD), ("wo", KD), ("res1", 2),
          ("up0", 2 * HJ), ("down0", 12), ("up1", 2 * HJ), ("down1", 12),
          ("ple1", KD),
          ("gla_a", 6), ("gla", 16 * (GH - 1)), ("gla_end", 12), ("ln1", 2), ("ple2", KD),
          ("idx", 8), ("dsa_z", DH), ("dsa0", DH // 2 + 2), ("dout0", KD), ("dsa1", DH // 2 - 2), ("dout1", KD),
          ("ln2", 2), ("ple3", KD)]
U0 = {}
_n = 0
for _name, _count in STAGES:
    U0[_name] = _n
    _n += _count
UNITS = _n
RAW = 4
SLOTS = 2

GAIN_COLS = [("g_mix_pre", KD), ("g_q_lat", QL // P), ("g_kv_lat", KVL // P), ("g_mix_post", KD),
             ("g_ffn_pre", KD), ("g_ffn_post", KD), ("g_ple_post", KD), ("conv_a_w", 3 * JC),
             ("conv_ffn_w", 3 * 2 * JF), ("b_ffn_conv", 2 * JF), ("gla_b_a_2", KD), ("gla_gn_g_2", DI // P),
             ("ln_g_2", 2 * KD), ("ln_b_2", 2 * KD)]
G0 = {}
_n = 0
for _name, _count in GAIN_COLS:
    G0[_name] = _n
    _n += _count
GAINS = _n

CONST_COLS = [("ident", P), ("ones", T), ("mla_bias", T), ("causal", T), ("tri", P), ("reset", T),
              ("inv_freq", 3), ("sign", 3), ("eps", 1), ("eps_ln", 1), ("one", 1)]
C0 = {}
_n = 0
for _name, _count in CONST_COLS:
    C0[_name] = _n
    _n += _count
CONSTS = _n


PI = float(np.nextafter(np.float32(np.pi), np.float32(0)))
TURN = (6.28125, 0.001934051513671875, 2 * np.pi - 6.28125 - 0.001934051513671875)


class Steps:

    def __init__(self, sem, names, n=1):
        self.sem, self.names, self.n = sem, names, n
        self.per = len(names)
        self.credit = max(self.per, 1)
        self.total = self.credit + n * self.per
        self.next = 0

    def at(self, name, i=0):
        return i * self.per + (self.credit + self.names.index(name) + 1)

    def done(self, ins, name):
        assert self.names[self.next] == name, (self.names[self.next], name)
        self.next = (self.next + 1) % self.per
        ins.then_inc(self.sem, 1)


def q_span(j):
    start = sum(T - (P * m + CHUNK) for m in range(j))
    return start, T - (P * j + CHUNK)


GLA_BANK = [(5, 0), (6, 0), (6, q_span(1)[1]), (5, q_span(0)[1])]
GLA_PACK = [sum(T - P * m for m in range(j)) for j in range(QT)]
GLA_AT = sum(T - P * m for m in range(QT))


def build(nc, ins, out):
    ctx = ExitStack()
    with ctx:
        def sb(name, shape, dt):
            return ctx.enter_context(nc.sbuf_tensor(name, shape, dt))

        def sem(name):
            return ctx.enter_context(nc.semaphore(name))

        raw = sb("raw", [P, RAW, 8 * P], F32)
        w_hi = sb("w_hi", [P, SLOTS, 8, P], F32R)
        w_lo = sb("w_lo", [P, SLOTS, 8, P], F32R)
        op_hi = sb("op_hi", [P, KD, T], F32R)
        op_lo = sb("op_lo", [P, KD, T], F32R)
        fb = sb("fb", [P, 24, T], F32)
        h = fb[:, 0:8, :]
        ebuf = fb[:, 8:16, :]
        fbuf = fb[:, 16:24, :]
        r2 = sb("r2", [P, 32 * T], F32R)
        fx = sb("fx", [P, 12, T], F32)
        rope_cos = sb("rope_cos", [P, 3, T], F32)
        rope_sin = sb("rope_sin", [P, 3, T], F32)
        cst = sb("cst", [P, CONSTS], F32)
        gain = sb("gain", [P, GAINS], F32)
        st = sb("st", [P, 64], F32)
        ps = [ctx.enter_context(nc.psum_tensor(f"bank{b}", [P, T], F32)) for b in range(8)]

        def const(name):
            width = dict(CONST_COLS)[name]
            return cst[:, C0[name]:C0[name] + width]

        def gcol(name, i):
            return gain[:, bass.ds(G0[name] + i, 1)]

        ident, ones = const("ident"), const("ones")[:, 0:P]
        rs, acc, sq = fx[:, 0, :], fx[:, 1, :], fx[:, 2, :]

        def pair(at, n):
            a = r2[:, at * T:(at + n) * T].rearrange("p (k t) -> p k t", t=T)
            b = r2[:, (at + n) * T:(at + 2 * n) * T].rearrange("p (k t) -> p k t", t=T)
            return a, b

        ob_hi, ob_lo = pair(0, 4)
        qn_hi, qn_lo = pair(8, 3)
        kvn_hi, kvn_lo = pair(14, 2)
        aq_hi, aq_lo = pair(18, 1)
        ak_hi, ak_lo = pair(20, 2)
        av = [pair(24, 1), pair(30, 1)]
        apt_hi, apt_lo = pair(26, 2)
        ya_hi, ya_lo = pair(8, 4)
        mix_hi, mix_lo = pair(16, 8)
        f_hi, f_lo = pair(0, HJ)
        p_hi, p_lo = pair(24, 2)
        p_raw = [rope_cos[:, 0, :], rope_sin[:, 0, :]]
        go_hi, go_lo = pair(0, 4)
        gv_hi, gv_lo = pair(8, 4)
        at_hi, at_lo = pair(16, 3)
        ga_hi, ga_lo = pair(22, 5)
        x2_hi, x2_lo = pair(0, 8)
        oz_hi, oz_lo = op_hi, op_lo
        qi_hi, qi_lo = op_hi[:, 0:4], op_lo[:, 0:4]
        ki_hi, ki_lo = op_hi[:, 4:6], op_lo[:, 4:6]
        dq_hi, dq_lo = pair(16, 1)
        dk_hi, dk_lo = pair(18, 1)
        dv_hi, dv_lo = pair(20, 1)
        dpt_hi, dpt_lo = pair(22, 4)

        def packed(f):
            def tile(q):
                block, at = ((1, 3 * P), (2, 0), (1, 0), (0, 0))[q]
                return fx[:, f + block, at:at + P * (q + 1)]

            return tile

        mla_probs, dsa_probs = packed(5), packed(7)

        def mla_query_tile(hh):
            return fx[:, 8 if hh else 3, :]

        def dsa_query_tile(hh):
            return fx[:, 3 if hh else 10, :]

        landed = [sem(f"landed{r}") for r in range(RAW)]
        hi_ready = sem("hi_ready")
        split_ready = sem("split_ready")
        unit_done = sem("unit_done")
        gain_in, p_in, pos_in = sem("gain_in"), sem("p_in"), sem("pos_in")
        x_in = [sem(f"x_in{n}") for n in range(KD // 2)]
        cst_in, out_sem = sem("cst_in"), sem("out_sem")

        pool_held, dve_held = sem("pool_held"), sem("dve_held")
        cleared = sem("cleared")
        S = {}

        def stage(name, n, act, dve, pe):
            S[name] = {"act": Steps(sem(f"act_{name}"), act, n), "dve": Steps(sem(f"dve_{name}"), dve, n),
                       "pe": Steps(sem(f"pe_{name}"), pe, n)}

        M8 = range(KD)
        stage("start", 1,
              [f"{a}{m}" for m in M8 for a in ("hi", "sq")] + ["sin", "abs", "cos", "sqrt"],
              [f"{a}{m}" for m in M8 for a in ("lo", "acc")]
              + ["pos", "ang0", "ang1", "ang2", "turn", "whole", "red1", "red2", "red3", "clip", "quarter", "sin0", "sin1", "sin2", "rs"],
              ["sum"])
        LB = range(5)
        stage("lat", 1,
              [f"sq{b}" for b in LB] + ["sqrt_q", "sqrt_kv"] + [f"hi{b}" for b in LB] + ["k0h", "k1h"],
              [f"{a}{b}" for part in (LB[:3], LB[3:]) for a in ("z", "acc") for b in part] + ["rs_q", "n0", "n1", "lo0", "n2", "lo1", "lo2"]
              + ["kr", "rs_kv", "n3", "n4", "lo3", "lo4", "swap", "swap_sin", "kr_cos", "kr_rot", "k0l", "k1l"],
              ["sum_q", "sum_kv"])

        def soft_act(x, late):
            return [f"{a}{x}" for a in ["e0", "e1", "n0", "n1", "e2", "e3"] + ["n2", "n3"] * (late == "act")
                    + ["h0", "h1", "h2", "h3"]]

        def soft_dve(x, chores, late):
            c = [[f"{name}{x}" for name in chore] for chore in chores]
            return ([f"m0{x}", f"m1{x}"] + c[0] + [f"r0{x}", f"m2{x}", f"m3{x}", f"r2{x}"]
                    + ([] if late == "act" else [f"n2{x}", f"r3{x}", f"n3{x}"])
                    + c[1] + [f"l0{x}", f"l1{x}"] + c[2] + [f"l2{x}", f"l3{x}"] + c[3])

        def soft_pe(x):
            return [f"{a}{x}" for a in ("s0", "s1", "s2", "s3", "t0", "t1", "o0", "t2", "o1", "t3", "o2", "o3")]

        def dsa_pe(x):
            return [f"{a}{x}" for a in ("s0", "s1", "s2", "s3", "t0", "t1", "t2", "t3", "o")]

        NONE = [[]] * 4
        MLA_CHORES = [["kl", "sw"], ["vl"], ["qc", "ss"], ["qa", "ql"]]
        DSA_CHORES = [["sw"], [], ["qc"], ["ss", "qa", "ql"]]
        stage("mla0", 1, ["qf", "kh", "vh", "qh"], ["kl", "sw", "vl", "qc", "ss", "qa", "ql"], [])
        for name, n in (("mla", NH // 2 - 1), ("mla_end", 1)):
            more = [x for x in "ab" if (name, x) != ("mla_end", "b")]
            stage(name, n,
                  sum([([f"qf{x}", f"kh{x}"] if x in more else []) + soft_act(x, "act")[:4] + ([f"vh{x}"] if x in more else [])
                       + soft_act(x, "act")[4:] + ([f"qh{x}"] if x in more else []) + [f"oh{x}"] for x in "ab"], []),
                  sum([soft_dve(x, MLA_CHORES if x in more else NONE, "act") + [f"ol{x}"] for x in "ab"], []),
                  sum([soft_pe(x) for x in "ab"], []))
        stage("conv", JC // 2,
              sum([[f"hi{x}"] for x in "ab"], []),
              sum([[f"{a}{x}" for a in ("ac", "ax", "c", "ab", "y0", "y1", "y2", "ya", "lo")] for x in "ab"], []), [])
        stage("mix", KD // 2,
              sum([[f"sa{x}", f"sb{x}", f"hi{x}"] for x in "ab"], []),
              sum([[f"{a}{x}" for a in ("ga", "gb", "ma", "mb", "mx", "lo")] for x in "ab"], []), [])
        stage("wo", KD // 2, sum([[f"f{x}", f"sq{x}"] for x in "ab"], []), [f"acc{x}" for x in "ab"], [])
        stage("res1", 1, ["ph0", "ph1", "sqrt"] + [f"e{m}" for m in range(4)]
              + [x for m in M8 for x in [f"hi{m}", f"sq{m}"] + ([f"e{m + 4}"] if m < 4 else [])] + ["sqrt2"],
              ["pl0", "pl1", "rs", "sc0", "h0"]
              + [x for m in M8 for x in ([f"sc{m + 1}", f"h{m + 1}"] if m < KD - 1 else []) + [f"lo{m}", f"acc{m}"]] + ["rs2"], ["sum"] + [f"e{m}" for m in M8 if m % 4 < 3] + ["sum2"])
        for half in (0, 1):
            stage(f"up{half}", HJ, ["ge", "hi"],
                  ["g", "g0", "g1", "g2", "v", "v0", "v1", "v2", "pr", "lo"], [])
            if half == 0:
                stage("down0", 2, [f"f{m}" for m in range(4)], [], [])
            else:
                stage("down1", 2, [f"sq{m}" for m in range(4)], [f"{a}{m}" for m in range(4) for a in ("f", "acc")], [])
        stage("res2", 1, ["sqrt"] + [f"hi{m}" for m in M8],
              ["rs", "sc0", "h0"] + [x for m in M8 for x in ([f"sc{m + 1}", f"h{m + 1}"] if m < KD - 1 else []) + [f"lo{m}"]], ["sum"])
        stage("ple1", KD // 2, sum([[f"g{x}", f"sq{x}"] for x in "ab"], []),
              sum([[f"e{x}", f"acc{x}"] for x in "ab"], []), [])
        stage("res3", 1, ["sqrt"] + [f"hi{m}" for m in M8],
              ["rs", "sc0", "h0"] + [x for m in M8 for x in ([f"sc{m + 1}", f"h{m + 1}"] if m < KD - 1 else []) + [f"lo{m}"]], ["sum"])
        QK = ["q0", "q1", "k0", "k1"]
        stage("gla_a", 1, QK + ["ah"] + [f"{a}{m}" for a in ("ab", "ex", "ln") for m in M8],
              ["zero_y", "al"] + [f"{a}{m}" for a in ("mn", "g") for m in M8] + ["zero_at"], [f"a{m}" for m in range(KD - 1)])

        def gla_prep_act(b):
            return ([f"x{b}qt", f"h{b}qt", f"x{b}kt", f"h{b}kt"] + [f"x{b}s{j}" for j in range(QT)] + [f"h{b}ks"]
                    + [f"x{b}j{j}" for j in range(QT)] + [f"h{b}qj"])

        def gla_prep_dve(b):
            return ([f"s64{b}", f"sgl{b}", f"ne{b}", f"po{b}", f"m{b}qt", f"l{b}qt", f"m{b}kt", f"l{b}kt", f"m{b}ks", f"l{b}ks"]
                    + [f"m{b}j{j}" for j in range(QT)] + [f"l{b}qj"])

        for name, n in (("gla", GH - 1), ("gla_end", 1)):
            more = name == "gla"
            gla_act = gla_prep_act(0) + [f"vh{t}" for t in range(QT)] + gla_prep_act(1) + ["z0", "z1", "z2", "ath", "z3"]
            gla_act += ["q0"] * more + [f"osq{b}" for b in range(4)] + ["q1"] * more + ["osqrt"]
            gla_act += [f"oh{b}" for b in range(4)] + ["k0", "k1"] * more
            gla_dve = gla_prep_dve(0) + [f"vl{t}" for t in range(QT)] + gla_prep_dve(1)
            gla_dve += [f"ad{j}" for j in range(QT)] + [f"{a}{j}" for j in range(QT) for a in ("ac", "ao")][:-1] + ["atl"]
            gla_dve += [f"{a}{b}" for b in range(4) for a in ("oacc", "on")] + ["ors", "oz0"]
            gla_dve += [x for b in range(4) for x in ([f"oz{b + 1}"] if b < 3 else []) + [f"ol{b}"]]
            gla_dve += [x for m in M8 for x in [f"y{m}"] + ([] if more else [f"s{m}"])]
            stage(name, n, gla_act, gla_dve,
                  ["A0", "A1"] + [f"o{b}" for b in range(4)] + ["osum"] + [f"y{m}" for m in M8 if m % 2 == 0])

        def ln_stage(name):
            stage(name, 1, ["ph0", "ph1", "mu"] + [f"{a}{m}" for m in M8 for a in ("sq", "e")] + ["sqrt"] + [f"hi{m}" for m in M8],
                  ["pl0", "pl1"] + ["c0"] + [x for m in M8 for x in ([f"c{m + 1}"] if m < KD - 1 else []) + [f"v{m}"]] + ["rs"]
                  + ["n0", "x0"] + [x for m in M8 for x in ([f"n{m + 1}", f"x{m + 1}"] if m < KD - 1 else []) + [f"lo{m}"]],
                  ["sum"] + [f"e{m}" for m in M8 if m % 4 < 3] + ["sum2"])

        ln_stage("ln1")
        stage("ple2", KD // 2, [f"{a}{x}" for x in "ab" for a in ("g", "hi")],
              [f"{a}{x}" for x in "ab" for a in ("e", "h", "t", "lo")], [])
        idx_act = ["qf0", "qf1", "hi0", "qf2", "hi1", "qf3", "hi2", "qf4", "hi3", "qf5", "kih0", "kih1", "kh", "vh", "wi"]
        idx_dve = [f"zero{n}" for n in range(4)]
        for b in range(6):
            idx_dve += [f"sw{b}", f"qc{b}", f"ss{b}", f"qa{b}"] + ([f"lo{b}"] if b < 4 else [["kil0", "kil1"], ["kl"]][b - 4])
        pairs = [(q, x) for q in range(1, QT) for x in range(IH)]
        stage("idx", 1, idx_act + [f"rel{q}{x}" for q, x in pairs],
              idx_dve + ["vl"] + [f"sc{q}{x}" for q, x in pairs] + [f"ca{q}" for q in range(1, QT)]
              + [f"{a}{q}_{r}" for q in range(1, QT) for r in range(TOPK // 8) for a in ("mx", "mr")]
              + [f"sel{q}" for q in range(1, QT)],
              [f"s{q}{x}" for q, x in pairs])
        stage("dsa_z", DH // 2, ["za", "zb"], [], [])
        stage("dsa_p", 1, ["qf", "qh"], ["sw", "qc", "ss", "qa", "ql"], [])
        for name, n in (("dsa0", DH // 4), ("dsa1", DH // 4 - 1), ("dsa1_end", 1)):
            more = [x for x in "ab" if (name, x) != ("dsa1_end", "b")]
            stage(name, n,
                  sum([([f"qf{x}"] if x in more else []) + soft_act(x, "dve") + ([f"qh{x}"] if x in more else [])
                       for x in "ab"], []),
                  sum([soft_dve(x, DSA_CHORES if x in more else NONE, "dve") + [f"oz{x}", f"oh{x}", f"ol{x}"] for x in "ab"], []),
                  sum([dsa_pe(x) for x in "ab"], []))
        for half in (0, 1):
            stage(f"dout{half}", KD // 2, [], ["fa", "fb"] if half == 0 else ["fa", "acca", "fb", "accb"], [])
        ln_stage("ln2")
        stage("ple3", KD // 2, [f"g{x}" for x in "ab"], [f"{a}{x}" for x in "ab" for a in ("e", "h")], [])

        ORDER = ["start", "lat", "mla0", "mla", "mla_end", "conv", "mix", "wo", "res1", "up0", "down0", "up1", "down1", "res2",
                 "ple1", "res3", "gla_a", "gla", "gla_end", "ln1", "ple2", "idx", "dsa_z", "dsa_p", "dsa0", "dout0", "dsa1",
                 "dsa1_end", "dout1", "ln2", "ple3"]

        def enter(eng, who, name, others=("act", "dve", "pe")):
            k = ORDER.index(name)
            if k:
                before = S[ORDER[k - 1]][who]
                eng.wait_ge(before.sem, before.total)
            if who == "pe":
                used = U0[name] if name in U0 else 0
                if used:
                    eng.wait_ge(unit_done, used)
            mine = S[name][who]
            eng.sem_inc(mine.sem, mine.credit)
            for other in others:
                if other != who:
                    eng.wait_ge(S[name][other].sem, S[name][other].credit)
            return S[name]["act"], S[name]["dve"], S[name]["pe"]

        block = ctx.enter_context(nc.Block())

        @block.sync
        def _(sp):
            def load(u, r):
                sp.dma_start(raw[:, r, :], ins["weights"][bass.ds(u, 1)].rearrange("a p n -> (a p) n")).then_inc(landed[r], 16)

            n = UNITS
            load(0, 0)
            sp.dma_start(gain[:, :], ins["gains"]).then_inc(gain_in, 16)
            for k in range(KD // 2):
                sp.dma_start(h[:, 2 * k:2 * k + 2], ins["x"][2 * k:2 * k + 2].rearrange("k p t -> p k t")).then_inc(x_in[k], 16)
                if k == 0:
                    load(1, 1)
            sp.dma_start(cst[:, :], ins["consts"]).then_inc(cst_in, 16)
            for u in range(2, min(RAW, n)):
                load(u, u)
            for i, name in enumerate(("positions", "positions_2")):
                sp.dma_start(fbuf[:, i].bitcast(I32), ins[name].broadcast_to([P, T])).then_inc(pos_in, 16)
            rounds = n // RAW
            if rounds > 1:
                with sp.Fori(1, rounds) as k:
                    for r in range(RAW):
                        sp.wait_ge(split_ready, k * RAW + (r - RAW + 1))
                        load(k * RAW + r, r)
            for u in range(max(rounds, 1) * RAW, n):
                sp.wait_ge(split_ready, u - RAW + 1)
                load(u, u % RAW)
            end = S[ORDER[-1]]
            for who in ("act", "dve", "pe"):
                sp.wait_ge(end[who].sem, end[who].total)
            sp.dma_start(out.rearrange("k p t -> p k t"), h).then_inc(out_sem, 16)
            sp.wait_ge(out_sem, 16)

        @block.gpsimd
        def _(pool):
            def split(u, k, r, free):
                s = r % SLOTS
                pool.wait_ge(landed[r], (k + 1) * 16)
                if free:
                    pool.wait_ge(unit_done, u - (SLOTS - 1))
                hi = w_hi[:, s].rearrange("p k n -> p (k n)")
                lo = w_lo[:, s].rearrange("p k n -> p (k n)")
                pool.sem_inc(pool_held, 1)
                pool.tensor_scalar(hi, raw[:, r, :], 1.0, 0.0, ALU.mult, ALU.add).then_inc(hi_ready, 1)
                pool.wait_ge(hi_ready, u + 1)
                pool.tensor_tensor(lo, raw[:, r, :], hi.bitcast(F32), ALU.subtract).then_inc(split_ready, 1)

            n = UNITS
            for u in range(min(RAW, n)):
                split(u, 0, u, u >= SLOTS)
            rounds = n // RAW
            if rounds > 1:
                with pool.Fori(1, rounds) as k:
                    for r in range(RAW):
                        split(k * RAW + r, k, r, True)
            for u in range(max(rounds, 1) * RAW, n):
                split(u, u // RAW, u % RAW, True)

        @block.tensor
        def _(pe):
            def split_mm(o, ah, al, bh, bl, start, stop, skip=False):
                pe.matmul(o, ah, bh, start=start, stop=False, skip_group_check=skip)
                pe.matmul(o, ah, bl, start=False, stop=False, skip_group_check=skip)
                return pe.matmul(o, al, bh, start=False, stop=stop, skip_group_check=skip)

            def blocks(o, s, kbs, xh, xl, stop=True, start=True):
                for n, (kb, k) in enumerate(kbs):
                    mm = split_mm(o, w_hi[:, s, kb], w_lo[:, s, kb], xh[:, k], xl[:, k],
                                  start and n == 0, stop and n == len(kbs) - 1)
                return mm

            def unit(u, parity, bank, xh=op_hi, xl=op_lo):
                pe.wait_ge(split_ready, u + 1)
                blocks(ps[bank][:, :], parity, [(k, k) for k in range(8)], xh, xl).then_inc(unit_done, 1)

            def full_sum(bank, x=acc):
                return pe.matmul(ps[bank][:, :], ones, x, start=True, stop=True)

            def scores(z, q, x, i, kh, kl, qh, ql):
                if q >= 2:
                    pe.wait_ge(z["dve"].sem, z["dve"].at(f"m{q - 2}{x}", i))
                n = P * (q + 1)
                z["pe"].done(split_mm(ps[3 + q % 2][:, 0:n], qh[:, q * P:(q + 1) * P], ql[:, q * P:(q + 1) * P],
                                      kh[:, 0:n], kl[:, 0:n], True, True), f"s{q}{x}")

            def turn(z, q, x, i, p):
                normalised = z["act" if f"n{q}{x}" in z["act"].names else "dve"]
                pe.wait_ge(normalised.sem, normalised.at(f"n{q}{x}", i))
                if q >= 2:
                    pe.wait_ge(z["dve"].sem, z["dve"].at(f"l{q - 2}{x}", i))
                for kt in range(q + 1):
                    mm = pe.transpose(ps[5 + q % 2][:, kt * P:(kt + 1) * P], p[:, kt * P:(kt + 1) * P], ident)
                z["pe"].done(mm, f"t{q}{x}")

            def values(z, q, x, i, vh, vl, pth, ptl):
                pe.wait_ge(z["dve"].sem, z["dve"].at(f"l{q}{x}", i))
                for kt in range(q + 1):
                    mm = split_mm(ps[7][:, q * P:(q + 1) * P], vh[:, kt * P:(kt + 1) * P], vl[:, kt * P:(kt + 1) * P],
                                  pth[:, q % 2, kt * P:(kt + 1) * P], ptl[:, q % 2, kt * P:(kt + 1) * P], kt == 0, kt == q)
                z["pe"].done(mm, f"o{q}{x}")

            def attend(z, x, i, kh, kl, qh, ql, vh, vl, pth, ptl, probs, project, left):
                scores(z, 0, x, i, kh, kl, qh, ql)
                scores(z, 1, x, i, kh, kl, qh, ql)
                project(0)
                scores(z, 2, x, i, kh, kl, qh, ql)
                scores(z, 3, x, i, kh, kl, qh, ql)
                project(1)
                turn(z, 0, x, i, probs(0))
                turn(z, 1, x, i, probs(1))
                project(2)
                pe.wait_ge(z["dve"].sem, left)
                values(z, 0, x, i, vh, vl, pth, ptl)
                turn(z, 2, x, i, probs(2))
                project(3)
                values(z, 1, x, i, vh, vl, pth, ptl)
                turn(z, 3, x, i, probs(3))
                project(4)
                values(z, 2, x, i, vh, vl, pth, ptl)
                values(z, 3, x, i, vh, vl, pth, ptl)

            def blockwise(u0, before, units=range(4)):
                d = S[before]["dve"]
                for c in units:
                    pe.wait_ge(split_ready, u0 + c + 1)
                    for kk in range(2):
                        k = 2 * c + kk
                        pe.wait_ge(d.sem, d.at(f"lo{k}"))
                        for m in range(4):
                            mm = split_mm(ps[m][:, :], w_hi[:, c % 2, 4 * kk + m], w_lo[:, c % 2, 4 * kk + m],
                                          op_hi[:, k], op_lo[:, k], k == 0, k == KD - 1)
                    mm.then_inc(unit_done, 1)

            a, d, z = enter(pe, "pe", "start")
            blockwise(U0["lat"], "start", range(2))
            pe.wait_ge(cst_in, 16)
            pe.wait_ge(d.sem, d.at("acc7"))
            z.done(full_sum(4), "sum")
            blockwise(U0["lat"], "start", range(2, 4))

            a, d, z = enter(pe, "pe", "lat", ())
            u = U0["lat"]
            unit(u + 4, 0, 5)
            pe.wait_ge(d.sem, d.at("acc2"))
            z.done(full_sum(7), "sum_q")
            unit(u + 5, 1, 6)
            pe.wait_ge(d.sem, d.at("acc4"))
            z.done(full_sum(0, fx[:, 9, :]), "sum_kv")

            def split_before(d, hh, i):
                if hh:
                    return d.at("qla", i)
                return d.at("qlb", i - 1) if "qlb" in d.names else d.credit

            def mla_query(s):
                return blocks(ps[0][:, :], s, [(k, k) for k in range(3)], qn_hi, qn_lo)

            def mla_key(s):
                return blocks(ps[1][:, :], s, [(3 + k, k) for k in range(2)], kvn_hi, kvn_lo)

            def mla_value(s, tiles):
                for t in tiles:
                    for k in range(2):
                        mm = split_mm(ps[2][:, t * P:(t + 1) * P], kvn_hi[:, k, t * P:(t + 1) * P],
                                      kvn_lo[:, k, t * P:(t + 1) * P], w_hi[:, s, 3 + k], w_lo[:, s, 3 + k], k == 0, k == 1)
                return mm

            a, d, z = enter(pe, "pe", "mla0", ())
            for n in range(2):
                pe.wait_ge(split_ready, U0["mla"] + n + 1)
                if n:
                    pe.wait_ge(a.sem, a.at("qf"))
                    pe.wait_ge(d.sem, d.at("vl"))
                else:
                    pe.wait_ge(S["lat"]["dve"].sem, S["lat"]["dve"].at("lo2"))
                mla_query(n)
                if n == 0:
                    pe.wait_ge(S["lat"]["dve"].sem, S["lat"]["dve"].at("lo4"))
                mla_key(n)
                mla_value(n, range(QT)).then_inc(unit_done, 1)

            def mla_heads(name, i, i0, last):
                a, d, z = S[name]["act"], S[name]["dve"], S[name]["pe"]
                for hh, x in enumerate("ab"):
                    before, bi = ("b", i - 1) if hh == 0 else ("a", i)

                    def project(piece):
                        if last:
                            return
                        if piece == 0:
                            pe.wait_ge(split_ready, i0 * 2 + (U0["mla"] + hh + 3))
                            pe.wait_ge(a.sem, a.at(f"qf{x}", i))
                            mla_query(hh)
                        elif piece == 1:
                            pe.wait_ge(d.sem, d.at(f"kl{x}", i))
                            mla_key(hh)
                        elif piece == 2:
                            pe.wait_ge(d.sem, d.at(f"vl{x}", i))
                            mla_value(hh, [0, 1])
                        elif piece == 3:
                            mla_value(hh, [2])
                        else:
                            mla_value(hh, [3]).then_inc(unit_done, 1)

                    pe.wait_ge(d.sem, split_before(d, hh, i))
                    attend(S[name], x, i, ak_hi[:, hh], ak_lo[:, hh], aq_hi[:, 0], aq_lo[:, 0], av[hh][0][:, 0], av[hh][1][:, 0],
                           apt_hi, apt_lo, mla_probs, project, d.at(f"ol{before}", bi))

            enter(pe, "pe", "mla")
            with pe.Fori(0, NH // 2 - 1) as i:
                mla_heads("mla", i, i, False)
            enter(pe, "pe", "mla_end")
            mla_heads("mla_end", 0, NH // 2 - 1, True)

            a, d, z = enter(pe, "pe", "conv")
            with pe.Fori(0, JC // 2) as i:
                for jj, x in enumerate("ab"):
                    before, bi = ("b", i - 1) if jj == 0 else ("a", i)
                    for n, s in enumerate(("ac", "ax", "ab")):
                        c = 3 * jj + n
                        prev = (("ax", before, bi), ("ab", before, bi), ("ac", x, i))[n]
                        pe.wait_ge(d.sem, d.at(prev[0] + prev[1], prev[2]))
                        unit(i * 6 + (U0["conv"] + c), c % 2, c % 2)

            conv_d = S["conv"]["dve"]
            pe.wait_ge(conv_d.sem, conv_d.at("abb", JC // 2 - 1))
            a, d, z = enter(pe, "pe", "mix", ())
            with pe.Fori(0, KD // 2) as i:
                for mm_, x in enumerate("ab"):
                    u = i * 6 + (U0["mix"] + 3 * mm_)
                    s = mm_ % 2
                    if mm_:
                        pe.wait_ge(d.sem, d.at("mbb", i - 1))
                    unit(u, s, 4 * mm_)
                    unit(u + 1, 1 - s, 4 * mm_ + 1)
                    pe.wait_ge(split_ready, u + 3)
                    if mm_ == 0:
                        pe.wait_ge(conv_d.sem, conv_d.at("lob", JC // 2 - 1))
                    blocks(ps[4 * mm_ + 2][:, :], s, [(k, k) for k in range(4)], ya_hi, ya_lo)
                    blocks(ps[4 * mm_ + 3][:, :], s, [(4 + k, k) for k in range(4)], ob_hi, ob_lo).then_inc(unit_done, 1)
                pe.wait_ge(d.sem, d.at("mba", i))

            mix_d = S["mix"]["dve"]
            mix_last = KD // 2 - 1
            pe.wait_ge(mix_d.sem, mix_d.at("loa", mix_last))
            a, d, z = enter(pe, "pe", "wo", ())
            with pe.Fori(0, KD // 2) as i:
                u = i * 2 + U0["wo"]
                pe.wait_ge(split_ready, u + 1)
                blocks(ps[0][:, :], 0, [(k, k) for k in range(KD - 1)], mix_hi, mix_lo, stop=False)
                pe.wait_ge(mix_d.sem, mix_d.at("lob", mix_last))
                blocks(ps[0][:, :], 0, [(KD - 1, KD - 1)], mix_hi, mix_lo, start=False).then_inc(unit_done, 1)
                pe.wait_ge(a.sem, a.at("sqb", i - 1))
                unit(u + 1, 1, 1, mix_hi, mix_lo)
                pe.wait_ge(a.sem, a.at("sqa", i))

            def ple_proj(name, k):
                a, d, z = S[name]["act"], S[name]["dve"], S[name]["pe"]
                pe.wait_ge(d.sem, d.at("pl1"))
                for m in range(KD):
                    c = m // 4
                    if m % 4 == 0:
                        pe.wait_ge(split_ready, U0[name] + c + 1)
                    if m >= 4:
                        pe.wait_ge(a.sem, a.at(f"e{m - 4}"))
                    mm = blocks(ps[4 + m % 4][:, :], c % 2, [(2 * (m % 4) + n, n) for n in range(2)], p_hi, p_lo)
                    if m % 4 < 3:
                        z.done(mm, f"e{m}")
                    else:
                        mm.then_inc(unit_done, 1)

            a, d, z = enter(pe, "pe", "res1")
            z.done(full_sum(2), "sum")
            ple_proj("res1", 1)
            blockwise(U0["up0"], "res1")
            pe.wait_ge(d.sem, d.at("acc7"))
            pe.wait_ge(a.sem, a.at("e7"))
            z.done(full_sum(7), "sum2")
            for half in (0, 1):
                name = f"up{half}"
                a, d, z = enter(pe, "pe", name, () if half == 0 else ("act", "dve", "pe"))
                first = 1 if half else 3
                for n in range(2):
                    unit(U0[name] + 2 * (first - 1) + n, n, 4 + n)
                with pe.Fori(0, (HJ - first) // 2) as i:
                    for e in range(2):
                        blk = i * 2 + (first + e)
                        for n, x in enumerate("gv"):
                            pe.wait_ge(d.sem, d.at(x, blk - 2))
                            unit(blk * 2 + (U0[name] + n), n, (4 if e else 6) + n)
                name = f"down{half}"
                up_d = S[f"up{half}"]["dve"]
                pe.wait_ge(up_d.sem, up_d.at("lo", HJ - 2))
                a, d, z = enter(pe, "pe", name, ())
                reader, step = (a, "f") if half == 0 else (a, "sq")
                with pe.Fori(0, 2) as i:
                    for m2 in range(2):
                        if m2:
                            for m in (2, 3):
                                pe.wait_ge(reader.sem, reader.at(f"{step}{m}", i - 1))
                        for v in range(3):
                            c = 3 * m2 + v
                            pe.wait_ge(split_ready, i * 6 + (U0[name] + c + 1))
                            for kb in range(8):
                                n = 8 * v + kb
                                if n >= 2 * HJ:
                                    break
                                m, k = n // HJ, n % HJ
                                if m2 == 0 and n == HJ - 1:
                                    pe.wait_ge(up_d.sem, up_d.at("lo", HJ - 1))
                                mm = split_mm(ps[2 * m2 + m][:, :], w_hi[:, c % 2, kb], w_lo[:, c % 2, kb],
                                              f_hi[:, k], f_lo[:, k], k == 0, k == HJ - 1)
                            mm.then_inc(unit_done, 1)
                    for m in (0, 1):
                        pe.wait_ge(reader.sem, reader.at(f"{step}{m}", i))

            def ple_gate(k, before):
                name = f"ple{k}"
                a, d, z = enter(pe, "pe", name, ())
                blockwise(U0[name], before)
                pe.wait_ge(a.sem, a.credit)
                for m in range(4, KD):
                    unit(U0[name] + m, m % 2, m)

            a, d, z = enter(pe, "pe", "res2")
            z.done(full_sum(2), "sum")
            ple_gate(1, "res2")
            a, d, z = enter(pe, "pe", "res3")
            z.done(full_sum(2), "sum")

            a, d, z = enter(pe, "pe", "gla_a", ())
            u = U0["gla_a"]
            blockwise(u, "res3")
            unit(u + 4, 0, 4)
            pe.wait_ge(d.sem, d.at("al"))
            pe.wait_ge(split_ready, u + 6)
            for m in range(KD):
                if m >= 4:
                    pe.wait_ge(d.sem, d.at(f"mn{m - 4}"))
                mm = blocks(ps[4 + (m + 1) % 4][:, :], 1, [(m, 0)], ga_hi, ga_lo)
                if m < KD - 1:
                    z.done(mm, f"a{m}")
                else:
                    mm.then_inc(unit_done, 1)

            qt_h, kt_h, ks_h = ga_hi[:, 0], ga_hi[:, 1], ga_hi[:, 2]
            qt_l, kt_l, ks_l = ga_lo[:, 0], ga_lo[:, 1], ga_lo[:, 2]
            qj_h, qj_l = ga_hi[:, 3:5].rearrange("p k t -> p (k t)"), ga_lo[:, 3:5].rearrange("p k t -> p (k t)")
            ath, atl = at_hi.rearrange("p k t -> p (k t)"), at_lo.rearrange("p k t -> p (k t)")

            def gla_head(name, i, last):
                a, d, z = S[name]["act"], S[name]["dve"], S[name]["pe"]
                base = i * 16 + U0[name]

                def products(b):
                    for j in range(QT):
                        t = slice(j * P, (j + 1) * P)
                        split_mm(ps[4][:, t], kt_h[:, t], kt_l[:, t], qt_h[:, t], qt_l[:, t],
                                 b == 0 and j == 0, b == 1, skip=True)
                        q0, n = q_span(j)
                        bank, o = GLA_BANK[j]
                        mm = split_mm(ps[bank][:, o:o + n], ks_h[:, t], ks_l[:, t], qj_h[:, q0:q0 + n], qj_l[:, q0:q0 + n],
                                      b == 0 and o == 0, b == 1, skip=True)
                    z.done(mm, f"A{b}")

                def gate(b):
                    unit(base + (4 + b), b % 2, b)

                for c in range(4):
                    s = c % 2
                    pe.wait_ge(split_ready, base + (c + 1))
                    for t in range(QT):
                        for kk in range(2):
                            k = 2 * c + kk
                            wh = w_hi[:, s, 4 * kk:4 * kk + 4].rearrange("p k n -> p (k n)")
                            wl = w_lo[:, s, 4 * kk:4 * kk + 4].rearrange("p k n -> p (k n)")
                            mm = split_mm(ps[4 + t][:, :], op_hi[:, k, t * P:(t + 1) * P], op_lo[:, k, t * P:(t + 1) * P],
                                          wh, wl, k == 0, k == KD - 1)
                    mm.then_inc(unit_done, 1)
                pe.wait_ge(d.sem, d.credit if last else d.at("y7", i - 1))
                gate(0)
                pe.wait_ge(d.sem, d.at("vl2", i))
                products(0)
                gate(1)
                gate(2)
                pe.wait_ge(d.sem, d.at("l1qj", i))
                products(1)
                gate(3)
                if not last:
                    unit(base + 8, 0, 7)
                pe.wait_ge(a.sem, a.at("z3", i))
                pe.wait_ge(d.sem, d.at("atl", i))
                for b in range(4):
                    for j in range(QT):
                        o = GLA_PACK[j]
                        mm = split_mm(ps[b][:, j * P:T], gv_hi[:, j, b * P:(b + 1) * P], gv_lo[:, j, b * P:(b + 1) * P],
                                      ath[:, o:o + T - j * P], atl[:, o:o + T - j * P], j == 0, j == QT - 1)
                    z.done(mm, f"o{b}")
                if not last:
                    unit(base + 9, 1, 5)
                pe.wait_ge(d.sem, d.at("oacc3", i))
                z.done(full_sum(4), "osum")
                if not last:
                    unit(base + 10, 0, 6)
                    pe.wait_ge(a.sem, a.at("osqrt", i))
                    unit(base + 11, 1, 4)
                first = 8 if last else 12
                for m in range(KD):
                    c = first + m // 2
                    if m % 2 == 0:
                        pe.wait_ge(split_ready, base + (c + 1))
                    if m >= 4:
                        pe.wait_ge(d.sem, d.at(f"y{m - 4}", i))
                    for k in range(4):
                        if m == 0:
                            pe.wait_ge(d.sem, d.at(f"ol{k}", i))
                        mm = blocks(ps[m % 4][:, :], c % 2, [(4 * (m % 2) + k, k)], go_hi, go_lo, k == 3, k == 0)
                    if m % 2 == 0:
                        z.done(mm, f"y{m}")
                    else:
                        mm.then_inc(unit_done, 1)
                if not last:
                    pe.wait_ge(a.sem, a.at("k1", i))

            pe.wait_ge(a.sem, a.at("ab7"))
            pe.wait_ge(d.sem, d.at("mn7"))
            enter(pe, "pe", "gla", ())
            with pe.Fori(0, GH - 1) as i:
                gla_head("gla", i, False)
            enter(pe, "pe", "gla_end", ())
            gla_head("gla_end", 0, True)

            def norm_sums(name, k):
                a, d, z = enter(pe, "pe", name)
                z.done(full_sum(2), "sum")
                ple_proj(name, k)
                pe.wait_ge(d.sem, d.at("v7"))
                z.done(full_sum(3), "sum2")

            norm_sums("ln1", 2)
            ple_gate(2, "ln1")

            before = S["ple2"]["dve"]
            a, d, z = enter(pe, "pe", "idx", ())
            u = U0["idx"]
            pe.wait_ge(split_ready, u + 1)
            pe.wait_ge(before.sem, before.at("loa", KD // 2 - 1))
            blocks(ps[0][:, :], u % 2, [(k, k) for k in range(KD - 1)], x2_hi, x2_lo, stop=False)
            pe.wait_ge(before.sem, before.at("lob", KD // 2 - 1))
            split_mm(ps[0][:, :], w_hi[:, u % 2, KD - 1], w_lo[:, u % 2, KD - 1], x2_hi[:, KD - 1], x2_lo[:, KD - 1],
                     False, True).then_inc(unit_done, 1)
            for n in range(1, 6):
                if n >= 2:
                    pe.wait_ge(a.sem, a.at(f"qf{n - 2}"))
                unit(u + n, (u + n) % 2, n % 2, x2_hi, x2_lo)
            for n, (name, width) in enumerate((("v", P), ("wi", IH))):
                c = u + 6 + n
                pe.wait_ge(split_ready, c + 1)
                for t in range(QT):
                    for k in range(KD):
                        mm = split_mm(ps[2 + n][:, t * width:(t + 1) * width], x2_hi[:, k, t * P:(t + 1) * P],
                                      x2_lo[:, k, t * P:(t + 1) * P], w_hi[:, c % 2, k, 0:width], w_lo[:, c % 2, k, 0:width],
                                      k == 0, k == KD - 1)
                mm.then_inc(unit_done, 1)
            pe.wait_ge(d.sem, d.at("kil1"))
            n = 0
            for q in range(1, QT):
                for x in range(IH):
                    if n >= 2:
                        last = divmod(n - 2, IH)
                        pe.wait_ge(a.sem, a.at(f"rel{last[0] + 1}{last[1]}"))
                    t = slice(q * P, (q + 1) * P)
                    w = P * (q + 1)
                    z.done(split_mm(ps[4 + n % 2][:, 0:w], qi_hi[:, x // 2, t], qi_lo[:, x // 2, t],
                                    ki_hi[:, x % 2, 0:w], ki_lo[:, x % 2, 0:w], True, True), f"s{q}{x}")
                    n += 1

            a, d, z = enter(pe, "pe", "dsa_z", ())
            with pe.Fori(0, DH // 2) as i:
                for n, x in enumerate("ab"):
                    pe.wait_ge(a.sem, a.at(f"z{x}", i - 1))
                    unit(i * 2 + (U0["dsa_z"] + n), (U0["dsa_z"] + n) % 2, n, x2_hi, x2_lo)
            def dsa_heads(name, u0, i, i0, last):
                a, d, z = S[name]["act"], S[name]["dve"], S[name]["pe"]
                for hh, x in enumerate("ab"):
                    before, bi = ("b", i - 1) if hh == 0 else ("a", i)

                    def project(piece):
                        if last:
                            return
                        if piece == 0:
                            pe.wait_ge(split_ready, i0 * 2 + (u0 + hh + 1))
                        first, end = ((0, 3), (3, 4), (4, 5), (5, 6), (6, 8))[piece]
                        mm = blocks(ps[hh][:, :], hh, [(k, k) for k in range(first, end)], x2_hi, x2_lo, end == 8, first == 0)
                        if piece == 4:
                            mm.then_inc(unit_done, 1)

                    pe.wait_ge(d.sem, split_before(d, hh, i))
                    z = S[name]
                    q_hi, q_lo, k_hi, k_lo = dq_hi[:, 0], dq_lo[:, 0], dk_hi[:, 0], dk_lo[:, 0]
                    scores(z, 0, x, i, k_hi, k_lo, q_hi, q_lo)
                    scores(z, 1, x, i, k_hi, k_lo, q_hi, q_lo)
                    project(0)
                    scores(z, 2, x, i, k_hi, k_lo, q_hi, q_lo)
                    scores(z, 3, x, i, k_hi, k_lo, q_hi, q_lo)
                    project(1)
                    turn(z, 0, x, i, dsa_probs(0))
                    turn(z, 1, x, i, dsa_probs(1))
                    project(2)
                    turn(z, 2, x, i, dsa_probs(2))
                    project(3)
                    turn(z, 3, x, i, dsa_probs(3))
                    project(4)
                    pe.wait_ge(d.sem, d.at(f"oz{before}", bi))
                    pe.wait_ge(d.sem, d.at(f"l3{x}", i))
                    for kt in range(QT):
                        c = kt * P
                        mm = split_mm(ps[7][:, c:T], dv_hi[:, 0, c:c + P], dv_lo[:, 0, c:c + P], dpt_hi[:, kt, c:T], dpt_lo[:, kt, c:T],
                                      kt == 0, kt == QT - 1)
                    z["pe"].done(mm, f"o{x}")

            enter(pe, "pe", "dsa_p")
            for n in range(2):
                unit(U0["dsa0"] + n, n, n, x2_hi, x2_lo)
            for half in (0, 1):
                name = f"dsa{half}"
                u0 = U0[name] + (0 if half else 2)
                rounds = DH // 4 - half
                enter(pe, "pe", name)
                with pe.Fori(0, rounds) as i:
                    dsa_heads(name, u0, i, i, False)
                if half:
                    enter(pe, "pe", "dsa1_end")
                    dsa_heads("dsa1_end", u0, 0, rounds, True)
                name = f"dout{half}"
                a, d, z = enter(pe, "pe", name)
                with pe.Fori(0, KD // 2) as i:
                    for m, x in enumerate("ab"):
                        pe.wait_ge(d.sem, d.at(f"f{x}", i - 1))
                        unit(i * 2 + (U0[name] + m), (U0[name] + m) % 2, 5 + m, oz_hi, oz_lo)
            norm_sums("ln2", 3)
            ple_gate(3, "ln2")

        def sweep(sqs):
            return lambda n: fx[:, sqs[n % 2], :]

        @block.scalar
        def _(act):
            def hi(steps, name, o, i_):
                steps.done(act.activation(o, i_, ACT.Copy), name)

            def root(steps, name, o, bank, n, eps):
                steps.done(act.activation(o, ps[bank][:, :], ACT.Sqrt, bias=const(eps), scale=1.0 / n), name)

            spare = [0]

            def load_roots():
                act.activation(st[:, 52 + spare[0]:53 + spare[0]], const("one"), ACT.Sqrt, bias=const("eps"))
                spare[0] += 1

            def load_p(src):
                for k in range(2):
                    act.dma_start(p_raw[k], src[k]).then_inc(p_in, 16)

            def split_p(a, k):
                act.wait_ge(p_in, 32 * k)
                for n in range(2):
                    hi(a, f"ph{n}", p_hi[:, n], p_raw[n])

            def proj_out(name, m):
                a, z = S[name]["act"], S[name]["pe"]
                if m % 4 < 3:
                    act.wait_ge(z.sem, z.at(f"e{m}"))
                else:
                    act.wait_ge(unit_done, U0[name] + m // 4 + 1)
                hi(a, f"e{m}", ebuf[:, m, :], ps[4 + m % 4][:, :])

            def exponentials(z, x, i, probs, tiles):
                a, d = z["act"], z["dve"]
                for q in tiles:
                    act.wait_ge(d.sem, d.at(f"m{q}{x}", i))
                    a.done(act.activation(probs(q), probs(q), ACT.Exp, bias=st[:, 40 + q:41 + q], scale=-1.0,
                                          accum_out=st[:, 44 + q:45 + q]), f"e{q}{x}")
                if f"n{tiles[0]}{x}" not in a.names:
                    return
                act.wait_ge(d.sem, d.at(f"r{tiles[0]}{x}", i))
                for q in tiles:
                    a.done(act.activation(probs(q), probs(q), ACT.Copy, scale=st[:, 48 + q:49 + q]), f"n{q}{x}")

            def turned_high(z, x, i, pth, tiles):
                a, e = z["act"], z["pe"]
                for q in tiles:
                    n = P * (q + 1)
                    act.wait_ge(e.sem, e.at(f"t{q}{x}", i))
                    if q >= 2:
                        act.wait_ge(e.sem, e.at(f"o{q - 2}{x}", i))
                    hi(a, f"h{q}{x}", pth[:, q % 2, 0:n], ps[5 + q % 2][:, 0:n])

            def dsa_turned_high(z, x, i):
                a, e = z["act"], z["pe"]
                for q in range(QT):
                    act.wait_ge(e.sem, e.at(f"t{q}{x}", i))
                    hi(a, f"h{q}{x}", dpt_hi[:, 0:q + 1, q * P:(q + 1) * P],
                       ps[5 + q % 2][:, 0:P * (q + 1)].rearrange("p (k t) -> p k t", t=P))

            act.wait_ge(gain_in, 16)
            a, d, z = enter(act, "act", "start")
            sqs = sweep((2, 11))
            for m in M8:
                act.wait_ge(x_in[m // 2], 16)
                a.done(act.activation(op_hi[:, m], h[:, m], ACT.Copy, scale=gcol("g_mix_pre", m)), f"hi{m}")
                if m >= 2:
                    act.wait_ge(d.sem, d.at(f"acc{m - 2}"))
                a.done(act.activation(sqs(m), h[:, m], ACT.Square), f"sq{m}")
            act.wait_ge(d.sem, d.at("clip"))
            a.done(act.activation(rope_sin[:, :, :], fx[:, 3:6, :], ACT.Sin), "sin")
            a.done(act.activation(fx[:, 6:9, :], fx[:, 3:6, :], ACT.Abs), "abs")
            act.wait_ge(d.sem, d.at("quarter"))
            a.done(act.activation(rope_cos[:, :, :], fx[:, 6:9, :], ACT.Sin), "cos")
            act.wait_ge(cst_in, 16)
            act.wait_ge(z.sem, z.at("sum"))
            root(a, "sqrt", rs, 4, D, "eps")

            a, d, z = enter(act, "act", "lat", ())
            for b in LB:
                act.wait_ge(d.sem, d.at(f"z{b}"))
                if b >= 2:
                    act.wait_ge(d.sem, d.at(f"acc{b - 2}"))
                a.done(act.activation(sqs(b), fx[:, 3 + b, :], ACT.Square), f"sq{b}")
            act.wait_ge(z.sem, z.at("sum_q"))
            root(a, "sqrt_q", fx[:, 8, :], 7, QL, "eps")
            act.wait_ge(z.sem, z.at("sum_kv"))
            root(a, "sqrt_kv", fx[:, 9, :], 0, KVL, "eps")
            for b in LB:
                act.wait_ge(d.sem, d.at(f"n{b}"))
                hi(a, f"hi{b}", qn_hi[:, b] if b < 3 else kvn_hi[:, b - 3], fx[:, 3 + b, :])
            act.wait_ge(d.sem, d.at("kr_rot"))
            hi(a, "k0h", ak_hi[0:64, 0], fx[0:64, 10, :])
            hi(a, "k1h", ak_hi[64:128, 1], fx[64:128, 10, :])

            krows = (slice(64, 128), slice(0, 64))
            orows = (slice(0, 64), slice(64, 128))

            def mla_evacuate(a, x, hh, i, what):
                if what == "qk":
                    hi(a, f"qf{x}", mla_query_tile(hh), ps[0][:, :])
                    hi(a, f"kh{x}", ak_hi[krows[hh], hh], ps[1][krows[hh], :])
                else:
                    hi(a, f"vh{x}", av[hh][0][:, 0], ps[2][:, :])

            def mla_heads(name, i, i0, last):
                a, d, z = S[name]["act"], S[name]["dve"], S[name]["pe"]
                for hh, x in enumerate("ab"):
                    more = not (last and hh)
                    if more:
                        act.wait_ge(unit_done, i0 * 2 + (U0["mla"] + hh + 2))
                        mla_evacuate(a, x, 1 - hh, i, "qk")
                    exponentials(S[name], x, i, mla_probs, (0, 1))
                    if more:
                        mla_evacuate(a, x, 1 - hh, i, "v")
                    exponentials(S[name], x, i, mla_probs, (2, 3))
                    turned_high(S[name], x, i, apt_hi, range(QT))
                    if more:
                        act.wait_ge(d.sem, d.at(f"qa{x}", i))
                        act.wait_ge(z.sem, z.at(f"s3{x}", i))
                        hi(a, f"qh{x}", aq_hi[:, 0], mla_query_tile(1 - hh))
                    act.wait_ge(z.sem, z.at(f"o3{x}", i))
                    hi(a, f"oh{x}", ob_hi[orows[hh], bass.ds(i0, 1), :].rearrange("p a t -> p (a t)"), ps[7][orows[hh], :])

            a, d, z = enter(act, "act", "mla0", ())
            act.wait_ge(unit_done, U0["mla"] + 1)
            mla_evacuate(a, "", 0, 0, "qk")
            mla_evacuate(a, "", 0, 0, "v")
            act.wait_ge(d.sem, d.at("qa"))
            hi(a, "qh", aq_hi[:, 0], mla_query_tile(0))
            enter(act, "act", "mla")
            with act.Fori(0, NH // 2 - 1) as i:
                mla_heads("mla", i, i, False)
            enter(act, "act", "mla_end")
            mla_heads("mla_end", 0, NH // 2 - 1, True)

            a, d, z = enter(act, "act", "conv")
            load_p(ins["p"])
            with act.Fori(0, JC // 2) as i:
                for jj, x in enumerate("ab"):
                    act.wait_ge(d.sem, d.at(f"ya{x}", i))
                    hi(a, f"hi{x}", ya_hi[:, bass.ds(i * 2 + jj, 1), :].rearrange("p a t -> p (a t)"), fx[:, 7, :])

            a, d, z = enter(act, "act", "mix")
            with act.Fori(0, KD // 2) as i:
                for m, x in enumerate("ab"):
                    for n, g in enumerate(("a", "b")):
                        act.wait_ge(d.sem, d.at(f"g{g}{x}", i))
                        t = fx[:, 3 + 2 * m + n, :]
                        a.done(act.activation(t, t, ACT.Sigmoid), f"s{g}{x}")
                    act.wait_ge(d.sem, d.at(f"mx{x}", i))
                    hi(a, f"hi{x}", mix_hi[:, bass.ds(i * 2 + m, 1), :].rearrange("p a t -> p (a t)"), fx[:, 3 + 2 * m, :])

            a, d, z = enter(act, "act", "wo")
            with act.Fori(0, KD // 2) as i:
                for m, x in enumerate("ab"):
                    act.wait_ge(unit_done, i * 2 + (U0["wo"] + m + 1))
                    a.done(act.activation(fbuf[:, bass.ds(i * 2 + m, 1), :].rearrange("p a t -> p (a t)"), ps[m][:, :], ACT.Copy), f"f{x}")
                    act.wait_ge(d.sem, d.at(f"acc{x}", i - 1))
                    a.done(act.activation(sqs(m), ps[m][:, :], ACT.Square), f"sq{x}")

            a, d, z = enter(act, "act", "res1")
            split_p(a, 1)
            act.wait_ge(z.sem, z.at("sum"))
            root(a, "sqrt", rs, 2, D, "eps")
            for m in range(4):
                proj_out("res1", m)
            for m in M8:
                act.wait_ge(d.sem, d.at(f"h{m}"))
                a.done(act.activation(op_hi[:, m], h[:, m], ACT.Copy, scale=gcol("g_ffn_pre", m)), f"hi{m}")
                if m >= 2:
                    act.wait_ge(d.sem, d.at(f"acc{m - 2}"))
                a.done(act.activation(sqs(m), h[:, m], ACT.Square), f"sq{m}")
                if m < 4:
                    proj_out("res1", m + 4)
            act.wait_ge(z.sem, z.at("sum2"))
            act.wait_ge(d.sem, d.at("rs"))
            root(a, "sqrt2", rs, 7, D, "eps")

            for half in (0, 1):
                name = f"up{half}"
                a, d, z = enter(act, "act", name)
                with act.Fori(0, HJ) as i:
                    act.wait_ge(d.sem, d.at("g2", i))
                    a.done(act.activation(fx[:, 5, :], fx[:, 5, :], ACT.Gelu_apprx_tanh), "ge")
                    act.wait_ge(d.sem, d.at("pr", i))
                    hi(a, "hi", f_hi[:, bass.ds(i, 1), :].rearrange("p a t -> p (a t)"), fx[:, 6, :])
                name = f"down{half}"
                a, d, z = enter(act, "act", name)
                with act.Fori(0, 2) as i:
                    for m in range(4):
                        fm = fbuf[:, bass.ds(i * 4 + m, 1), :].rearrange("p a t -> p (a t)")
                        if half == 0:
                            act.wait_ge(unit_done, i * 6 + (U0[name] + 3 * (m // 2) + 2 + m % 2))
                            a.done(act.activation(fm, ps[m][:, :], ACT.Copy), f"f{m}")
                        else:
                            act.wait_ge(d.sem, d.at(f"f{m}", i))
                            if m >= 2:
                                act.wait_ge(d.sem, d.at(f"acc{m - 2}", i))
                            else:
                                act.wait_ge(d.sem, d.at(f"acc{m + 2}", i - 1))
                            a.done(act.activation(sqs(m), fm, ACT.Square), f"sq{m}")

            def ple_gate(k):
                name = f"ple{k}"
                a, d, z = enter(act, "act", name, ())
                for m in M8:
                    i, x = m // 2, "ab"[m % 2]
                    act.wait_ge(unit_done, U0[name] + max(m, 3) + 1)
                    if m >= 2:
                        act.wait_ge(d.sem, d.at(f"e{x}", i - 1))
                    a.done(act.activation(fx[:, 3 + m % 2, :], ps[m][:, :], ACT.Sigmoid), f"g{x}")
                    if k == 1:
                        act.wait_ge(d.sem, d.at(f"e{x}", i))
                        act.wait_ge(d.sem, d.at(f"acc{x}", i - 1))
                        a.done(act.activation(sqs(m), ebuf[:, m], ACT.Square), f"sq{x}")
                    elif k == 2:
                        act.wait_ge(d.sem, d.at(f"h{x}", i))
                        hi(a, f"hi{x}", x2_hi[:, m], h[:, m])

            def residual(name):
                a, d, z = enter(act, "act", name)
                load_roots()
                act.wait_ge(z.sem, z.at("sum"))
                root(a, "sqrt", rs, 2, D, "eps")
                for m in M8:
                    act.wait_ge(d.sem, d.at(f"h{m}"))
                    hi(a, f"hi{m}", op_hi[:, m], h[:, m])

            residual("res2")
            ple_gate(1)
            residual("res3")

            a, d, z = enter(act, "act", "gla_a")
            load_p(ins["p_2"][0:2])
            act.wait_ge(d.sem, d.at("zero_y"))
            act.wait_ge(unit_done, U0["gla_a"] + 4)
            for c, n in enumerate(QK):
                a.done(act.activation(h[:, c], ps[c][:, :], ACT.Copy, scale=GDK ** -0.5 if c < 2 else 1.0), n)
            act.wait_ge(unit_done, U0["gla_a"] + 5)
            hi(a, "ah", ga_hi[:, 0], ps[4][:, :])
            for m in M8:
                if m < KD - 1:
                    act.wait_ge(z.sem, z.at(f"a{m}"))
                else:
                    act.wait_ge(unit_done, U0["gla_a"] + 6)
                a.done(act.activation(ebuf[:, m], ps[4 + (m + 1) % 4][:, :], ACT.Abs, bias=gcol("gla_b_a_2", m)), f"ab{m}")
            for m in M8:
                act.wait_ge(a.sem, a.at(f"ab{m}"))
                a.done(act.activation(ebuf[:, m], ebuf[:, m], ACT.Exp, scale=-1.0), f"ex{m}")
            for m in M8:
                act.wait_ge(a.sem, a.at(f"ex{m}"))
                a.done(act.activation(ebuf[:, m], ebuf[:, m], ACT.Ln, bias=const("one")), f"ln{m}")

            g64, gl = fx[:, 3, :], fx[:, 4, :]
            ex, tm = fx[:, 5:7, :].rearrange("p k t -> p (k t)"), fx[:, 7:9, :].rearrange("p k t -> p (k t)")
            atf = fx[:, 9:12, :].rearrange("p k t -> p (k t)")
            gsq = sweep((2, 0))
            inv = 1.0 / GATE_NORM

            def gla_head(name, i, last):
                a, d, z = S[name]["act"], S[name]["dve"], S[name]["pe"]
                base = i * 16 + U0[name]

                def copy_out(n):
                    c = QK.index(n)
                    act.wait_ge(unit_done, base + (9 + c))
                    a.done(act.activation(h[:, c], ps[(7, 5, 6, 4)[c]][:, :], ACT.Copy, scale=GDK ** -0.5 if c < 2 else 1.0), n)

                def gate(b):
                    act.wait_ge(unit_done, base + (5 + b))
                    a.done(act.activation(h[:, 4 + b], ps[b][:, :], ACT.Silu), f"z{b}")

                def prep(b):
                    act.wait_ge(d.sem, d.at(f"po{b}", i))
                    a.done(act.activation(ex[:, 0:T], g64, ACT.Exp, scale=inv), f"x{b}qt")
                    act.wait_ge(d.sem, d.at(f"m{b}qt", i))
                    if b:
                        act.wait_ge(z.sem, z.at("A0", i))
                    hi(a, f"h{b}qt", ga_hi[:, 0], tm[:, 0:T])
                    a.done(act.activation(ex[:, 0:T], g64, ACT.Exp, scale=-inv), f"x{b}kt")
                    act.wait_ge(d.sem, d.at(f"m{b}kt", i))
                    hi(a, f"h{b}kt", ga_hi[:, 1], tm[:, 0:T])
                    for j in range(QT):
                        t = slice(j * P, (j + 1) * P)
                        a.done(act.activation(ex[:, t], gl[:, t], ACT.Exp, scale=-inv, bias=st[:, 8 * b + 4 + j:8 * b + 5 + j]), f"x{b}s{j}")
                    act.wait_ge(d.sem, d.at(f"m{b}ks", i))
                    hi(a, f"h{b}ks", ga_hi[:, 2], tm[:, 0:T])
                    for j in range(QT):
                        q0, n = q_span(j)
                        a.done(act.activation(ex[:, q0:q0 + n], gl[:, T - n:T], ACT.Exp, scale=inv, bias=st[:, 8 * b + j:8 * b + j + 1]), f"x{b}j{j}")
                    act.wait_ge(d.sem, d.at(f"m{b}j{QT - 1}", i))
                    hi(a, f"h{b}qj", ga_hi[:, 3:5].rearrange("p k t -> p (k t)"), tm)

                prep(0)
                for t in range(QT):
                    act.wait_ge(unit_done, base + 4)
                    hi(a, f"vh{t}", gv_hi[:, t], ps[4 + t][:, :])
                prep(1)
                for b in range(3):
                    gate(b)
                act.wait_ge(d.sem, d.at(f"ac{QT - 1}", i))
                hi(a, "ath", at_hi.rearrange("p k t -> p (k t)")[:, 0:GLA_AT], atf[:, 0:GLA_AT])
                gate(3)
                if not last:
                    copy_out("q0")
                for b in range(4):
                    act.wait_ge(z.sem, z.at(f"o{b}", i))
                    if b >= 2:
                        act.wait_ge(d.sem, d.at(f"oacc{b - 2}", i))
                    a.done(act.activation(gsq(b), ps[b][:, :], ACT.Square), f"osq{b}")
                if not last:
                    copy_out("q1")
                act.wait_ge(z.sem, z.at("osum", i))
                root(a, "osqrt", rs, 4, GDV, "eps_ln")
                for b in range(4):
                    act.wait_ge(d.sem, d.at(f"oz{b}", i))
                    hi(a, f"oh{b}", go_hi[:, b], h[:, 4 + b])
                if not last:
                    copy_out("k0")
                    copy_out("k1")

            enter(act, "act", "gla", ())
            with act.Fori(0, GH - 1) as i:
                gla_head("gla", i, False)
            enter(act, "act", "gla_end", ())
            gla_head("gla_end", 0, True)

            def layer_norm(name, k):
                a, d, z = enter(act, "act", name)
                split_p(a, k)
                act.wait_ge(z.sem, z.at("sum"))
                a.done(act.activation(fx[:, 3, :], ps[2][:, :], ACT.Copy, scale=1.0 / D), "mu")
                for m in M8:
                    act.wait_ge(d.sem, d.at(f"c{m}"))
                    if m >= 2:
                        act.wait_ge(d.sem, d.at(f"v{m - 2}"))
                    a.done(act.activation(sqs(m), fbuf[:, m], ACT.Square), f"sq{m}")
                    proj_out(name, m)
                load_roots()
                act.wait_ge(z.sem, z.at("sum2"))
                root(a, "sqrt", rs, 3, D, "eps_ln")
                for m in M8:
                    act.wait_ge(d.sem, d.at(f"x{m}"))
                    hi(a, f"hi{m}", op_hi[:, m], h[:, m])

            layer_norm("ln1", 2)
            ple_gate(2)

            a, d, z = enter(act, "act", "idx")
            load_p(ins["p_2"][2:4])
            u = U0["idx"]

            def copy_out(b):
                act.wait_ge(unit_done, u + b + 1)
                if b >= 2:
                    act.wait_ge(d.sem, d.at(["lo0", "lo1", "lo2", "lo3"][b - 2]))
                hi(a, f"qf{b}", fx[:, 9 + b % 2, :], ps[b % 2][:, :])

            def high(b):
                act.wait_ge(d.sem, d.at(f"qa{b}"))
                hi(a, f"hi{b}", qi_hi[:, b], fx[:, 9 + b % 2, :])

            copy_out(0)
            copy_out(1)
            for b in range(4):
                high(b)
                copy_out(b + 2)
            act.wait_ge(d.sem, d.at("qa4"))
            act.wait_ge(d.sem, d.at("zero3"))
            hi(a, "kih0", ki_hi[0:64, 0], fx[0:64, 9, :])
            hi(a, "kih1", ki_hi[64:128, 1], fx[64:128, 9, :])
            act.wait_ge(d.sem, d.at("qa5"))
            hi(a, "kh", dk_hi[:, 0], fx[:, 10, :])
            act.wait_ge(unit_done, u + 7)
            hi(a, "vh", dv_hi[:, 0], ps[2][:, :])
            act.wait_ge(unit_done, u + 8)
            a.done(act.activation(st[:, 0:QT * IH], ps[3][:, 0:QT * IH], ACT.Copy, scale=INDEX_SCALE), "wi")
            for n, (q, x) in enumerate(pairs):
                w = P * (q + 1)
                act.wait_ge(z.sem, z.at(f"s{q}{x}"))
                if n >= 2:
                    act.wait_ge(d.sem, d.at("sc%d%d" % pairs[n - 2]))
                a.done(act.activation(fx[:, 7 + n % 2, 0:w], ps[4 + n % 2][:, 0:w], ACT.Relu), f"rel{q}{x}")

            a, d, z = enter(act, "act", "dsa_z", ())
            with act.Fori(0, DH // 2) as i:
                for n, x in enumerate("ab"):
                    act.wait_ge(unit_done, i * 2 + (U0["dsa_z"] + n + 1))
                    a.done(act.activation(fb[:, bass.ds(i * 2 + n, 1), :].rearrange("p a t -> p (a t)"), ps[n][:, :], ACT.Silu), f"z{x}")
            def dsa_heads(name, half, u0, i, i0, last):
                a, d, z = S[name]["act"], S[name]["dve"], S[name]["pe"]
                for hh, x in enumerate("ab"):
                    more = not (last and hh)
                    if more:
                        act.wait_ge(unit_done, i0 * 2 + (u0 + hh))
                        hi(a, f"qf{x}", dsa_query_tile(1 - hh), ps[1 - hh][:, :])
                    exponentials(S[name], x, i, dsa_probs, (0, 1))
                    exponentials(S[name], x, i, dsa_probs, (2, 3))
                    dsa_turned_high(S[name], x, i)
                    if more:
                        act.wait_ge(d.sem, d.at(f"qa{x}", i))
                        act.wait_ge(z.sem, z.at(f"s3{x}", i))
                        hi(a, f"qh{x}", dq_hi[:, 0], dsa_query_tile(1 - hh))

            a, d, z = enter(act, "act", "dsa_p")
            act.wait_ge(unit_done, U0["dsa0"] + 1)
            hi(a, "qf", dsa_query_tile(0), ps[0][:, :])
            act.wait_ge(d.sem, d.at("qa"))
            hi(a, "qh", dq_hi[:, 0], dsa_query_tile(0))
            for half in (0, 1):
                name = f"dsa{half}"
                u0 = U0[name] + (0 if half else 2)
                rounds = DH // 4 - half
                enter(act, "act", name)
                with act.Fori(0, rounds) as i:
                    dsa_heads(name, half, u0, i, i, False)
                if half:
                    enter(act, "act", "dsa1_end")
                    dsa_heads("dsa1_end", half, u0, 0, rounds, True)
                name = f"dout{half}"
                a, d, z = enter(act, "act", name)
            layer_norm("ln2", 3)
            ple_gate(3)

        @block.vector
        def _(dve):
            def lo(steps, name, o, src, high):
                steps.done(dve.tensor_tensor(o, src, high.bitcast(F32), ALU.subtract), name)

            def mul(steps, name, o, x, y):
                steps.done(dve.tensor_tensor(o, x, y, ALU.mult), name)

            def add(steps, name, o, x, y):
                steps.done(dve.tensor_tensor(o, x, y, ALU.add), name)

            def stt(steps, name, o, x, s, y, op0, op1):
                steps.done(dve.scalar_tensor_tensor(out=o, in0=x, scalar=s, in1=y, op0=op0, op1=op1), name)

            def sync(steps, name, i=0):
                dve.wait_ge(steps.sem, steps.at(name, i))

            def at(tile, i):
                return tile[:, bass.ds(i, 1), :].rearrange("p a t -> p (a t)")

            def accumulate(steps, name, first, s, total=acc):
                if first:
                    steps.done(dve.tensor_copy(total, s), name)
                else:
                    add(steps, name, total, total, s)

            zeroed = [0]

            def clear(x):
                dve.memset(x, 0.0).then_inc(cleared, 1)
                zeroed[0] += 1
                dve.wait_ge(cleared, zeroed[0])

            def rotate(steps, step, n, i, f, tmp, table, rows, half):
                size = 2 * half
                swap = [(r + half) % size + (r - r % size) if r % 32 < size else r for r in range(32)]
                if step == "sw":
                    dve.sem_inc(dve_held, 1)
                    steps.done(dve.stream_shuffle(tmp[rows, :], f[rows, :], swap), f"sw{n}")
                elif step == "qc":
                    sync(steps, f"sw{n}", i)
                    mul(steps, f"qc{n}", f[rows, :], f[rows, :], rope_cos[rows, table, :])
                elif step == "ss":
                    mul(steps, f"ss{n}", tmp[rows, :], tmp[rows, :], rope_sin[rows, table, :])
                else:
                    sync(steps, f"ss{n}", i)
                    add(steps, f"qa{n}", f[rows, :], f[rows, :], tmp[rows, :])

            def softmax(z, x, i, probs, parts, bias, scale, chore):
                a, d, e = z["act"], z["dve"], z["pe"]

                def mask(q):
                    sync(e, f"s{q}{x}", i)
                    dve.sem_inc(dve_held, 1)
                    d.done(dve.tensor_tensor_reduce(out=probs(q), in0=ps[3 + q % 2][:, 0:P * (q + 1)], in1=bias(q), scale=-scale,
                                                    scalar=3.0e38, op0=ALU.add, op1=ALU.min, accum_out=st[:, 40 + q:41 + q]), f"m{q}{x}")

                def invert(q, n=1):
                    sync(a, f"e{q + n - 1}{x}", i)
                    d.done(dve.reciprocal(st[:, 48 + q:48 + q + n], st[:, 44 + q:44 + q + n]), f"r{q}{x}")

                def normalise(q):
                    invert(q)
                    sync(d, f"r{q}{x}", i)
                    d.done(dve.tensor_scalar(probs(q), probs(q), st[:, 48 + q:49 + q], None, ALU.mult), f"n{q}{x}")

                def low(q):
                    sync(a, f"h{q}{x}", i)
                    lo(d, f"l{q}{x}", *parts(q))

                mask(0)
                mask(1)
                chore(0)
                invert(0, 2)
                mask(2)
                mask(3)
                if f"n2{x}" in d.names:
                    normalise(2)
                    normalise(3)
                else:
                    invert(2, 2)
                chore(1)
                low(0)
                low(1)
                chore(2)
                low(2)
                low(3)
                chore(3)

            dve.wait_ge(gain_in, 16)
            a, d, z = enter(dve, "dve", "start")
            sqs = sweep((2, 11))
            for m in M8:
                sync(a, f"hi{m}")
                stt(d, f"lo{m}", op_lo[:, m], h[:, m], gcol("g_mix_pre", m), op_hi[:, m].bitcast(F32), ALU.mult, ALU.subtract)
                sync(a, f"sq{m}")
                accumulate(d, f"acc{m}", m == 0, sqs(m))
                sync(d, f"acc{m}")
            dve.wait_ge(cst_in, 16)
            dve.wait_ge(pos_in, 32)
            d.done(dve.tensor_copy(fx[:, 6:8, :], fbuf[:, 0:2].bitcast(I32)), "pos")
            sync(d, "pos")
            for t in range(3):
                d.done(dve.tensor_scalar(fx[:, 3 + t, :], fx[:, 6 + (t > 0), :], const("inv_freq")[:, t:t + 1], None, ALU.mult), f"ang{t}")
            sync(d, "ang2")
            ang, turns = fx[:, 3:6, :], fx[:, 6:9, :]
            magic = 1.5 * 2 ** 23
            d.done(dve.tensor_scalar(turns, ang, 1.0 / (2 * np.pi), magic, ALU.mult, ALU.add), "turn")
            sync(d, "turn")
            d.done(dve.tensor_scalar(turns, turns, magic, None, ALU.subtract), "whole")
            sync(d, "whole")
            for n, part in enumerate(TURN):
                stt(d, f"red{n + 1}", ang, turns, -part, ang, ALU.mult, ALU.add)
                sync(d, f"red{n + 1}")
            d.done(dve.tensor_scalar(ang, ang, PI, -PI, ALU.min, ALU.max), "clip")
            sync(a, "abs")
            d.done(dve.tensor_scalar(turns, turns, -1.0, np.pi / 2, ALU.mult, ALU.add), "quarter")
            sync(a, "sin")
            for t in range(3):
                d.done(dve.tensor_scalar(rope_sin[:, t, :], rope_sin[:, t, :], const("sign")[:, t:t + 1], None, ALU.mult), f"sin{t}")
            sync(a, "sqrt")
            d.done(dve.reciprocal(rs, rs), "rs")

            a, d, z = enter(dve, "dve", "lat", ())
            lat = fx[:, 3:8, :]

            def scaled(b):
                dve.wait_ge(unit_done, U0["lat"] + max(b, 3) + 1)
                mul(d, f"z{b}" if b < 5 else "kr", lat[:, b] if b < 5 else fx[:, 10, :], ps[b if b < 4 else b + 1][:, :], rs)

            def squares(b):
                sync(a, f"sq{b}")
                accumulate(d, f"acc{b}", b in (0, 3), sqs(b), acc if b < 3 else fx[:, 9, :])
                sync(d, f"acc{b}")

            sync(S["start"]["dve"], "rs")
            for part in (LB[:3], LB[3:]):
                for b in part:
                    scaled(b)
                for b in part:
                    squares(b)
            def normalised(b):
                stt(d, f"n{b}", lat[:, b], lat[:, b], gcol("g_q_lat", b) if b < 3 else gcol("g_kv_lat", b - 3),
                    fx[:, 8 + (b > 2), :], ALU.mult, ALU.mult)

            def low_part(b):
                sync(a, f"hi{b}")
                o_hi, o_lo = (qn_hi[:, b], qn_lo[:, b]) if b < 3 else (kvn_hi[:, b - 3], kvn_lo[:, b - 3])
                lo(d, f"lo{b}", o_lo, lat[:, b], o_hi)

            sync(a, "sqrt_q")
            d.done(dve.reciprocal(fx[:, 8, :], fx[:, 8, :]), "rs_q")
            sync(d, "rs_q")
            normalised(0)
            normalised(1)
            low_part(0)
            normalised(2)
            low_part(1)
            low_part(2)
            scaled(5)
            sync(a, "sqrt_kv")
            d.done(dve.reciprocal(fx[:, 9, :], fx[:, 9, :]), "rs_kv")
            sync(d, "rs_kv")
            normalised(3)
            normalised(4)
            low_part(3)
            low_part(4)
            kr, tmp = fx[:, 10, :], fx[:, 2, :]
            d.done(dve.stream_shuffle(tmp, kr, [(r + 16) % 32 for r in range(32)]), "swap")
            sync(d, "swap")
            mul(d, "swap_sin", tmp, tmp, rope_sin[:, 0, :])
            mul(d, "kr_cos", kr, kr, rope_cos[:, 0, :])
            sync(d, "kr_cos")
            add(d, "kr_rot", kr, kr, tmp)
            sync(a, "k0h")
            lo(d, "k0l", ak_lo[0:64, 0], kr[0:64, :], ak_hi[0:64, 0])
            sync(a, "k1h")
            lo(d, "k1l", ak_lo[64:128, 1], kr[64:128, :], ak_hi[64:128, 1])

            krows = (slice(64, 128), slice(0, 64))
            rrows = (slice(0, 32), slice(64, 96))
            orows = (slice(0, 64), slice(64, 128))

            def mla_chore(a, d, x, hh, i, k):
                def turn(step):
                    rotate(d, step, x, i, mla_query_tile(hh), fx[:, 4, :], 0, rrows[hh], ROPE // 2)

                if k == 0:
                    sync(a, f"kh{x}", i)
                    lo(d, f"kl{x}", ak_lo[krows[hh], hh], ps[1][krows[hh], :], ak_hi[krows[hh], hh])
                    turn("sw")
                elif k == 1:
                    sync(a, f"vh{x}", i)
                    lo(d, f"vl{x}", av[hh][1][:, 0], ps[2][:, :], av[hh][0][:, 0])
                elif k == 2:
                    turn("qc")
                    turn("ss")
                else:
                    turn("qa")
                    sync(a, f"qh{x}", i)
                    lo(d, f"ql{x}", aq_lo[:, 0], mla_query_tile(hh), aq_hi[:, 0])

            def mla_heads(name, i, i0, last):
                a, d, z = S[name]["act"], S[name]["dve"], S[name]["pe"]
                for hh, x in enumerate("ab"):
                    def chore(k):
                        if not (last and hh):
                            mla_chore(a, d, x, 1 - hh, i, k)

                    def parts(q):
                        n = P * (q + 1)
                        return apt_lo[:, q % 2, 0:n], ps[5 + q % 2][:, 0:n], apt_hi[:, q % 2, 0:n]

                    softmax(S[name], x, i, mla_probs, parts, lambda q: const("mla_bias")[:, T - P * (q + 1):T],
                            MLA_SCALE, chore)
                    sync(a, f"oh{x}", i)
                    lo(d, f"ol{x}", ob_lo[orows[hh], bass.ds(i0, 1), :].rearrange("p a t -> p (a t)"), ps[7][orows[hh], :],
                       ob_hi[orows[hh], bass.ds(i0, 1), :].rearrange("p a t -> p (a t)"))

            a, d, z = enter(dve, "dve", "mla0", ())
            for k in range(4):
                mla_chore(a, d, "", 0, 0, k)
            enter(dve, "dve", "mla")
            with dve.Fori(0, NH // 2 - 1) as i:
                mla_heads("mla", i, i, False)
            enter(dve, "dve", "mla_end")
            mla_heads("mla_end", 0, NH // 2 - 1, True)

            a, d, z = enter(dve, "dve", "conv")
            tA, tB, cc, yy = fx[:, 3, :], fx[:, 4, :], fx[:, 5, :], fx[:, 7, :]
            with dve.Fori(0, JC // 2) as i:
                for jj, x in enumerate("ab"):
                    j = i * 2 + jj
                    u = i * 6 + (U0["conv"] + 3 * jj)
                    sync(d, "lob" if jj == 0 else "loa", i - 1 if jj == 0 else i)
                    for n, (name, o) in enumerate((("ac", tA), ("ax", tB))):
                        dve.wait_ge(unit_done, u + (n + 1))
                        mul(d, name + x, o, ps[(3 * jj + n) % 2][:, :], rs)
                    sync(d, f"ax{x}", i)
                    mul(d, f"c{x}", cc, tA, tB)
                    sync(d, f"c{x}", i)
                    dve.wait_ge(unit_done, u + 3)
                    mul(d, f"ab{x}", tA, ps[(3 * jj + 2) % 2][:, :], rs)
                    d.done(dve.tensor_scalar(yy, cc, gcol("conv_a_w", j + 2 * JC), None, ALU.mult), f"y0{x}")
                    sync(d, f"y0{x}", i)
                    stt(d, f"y1{x}", yy[:, 1:T], cc[:, 0:T - 1], gcol("conv_a_w", j + JC), yy[:, 1:T], ALU.mult, ALU.add)
                    sync(d, f"y1{x}", i)
                    stt(d, f"y2{x}", yy[:, 2:T], cc[:, 0:T - 2], gcol("conv_a_w", j), yy[:, 2:T], ALU.mult, ALU.add)
                    sync(d, f"y2{x}", i)
                    mul(d, f"ya{x}", yy, yy, tA)
                    sync(a, f"hi{x}", i)
                    lo(d, f"lo{x}", at(ya_lo, j), yy, at(ya_hi, j))

            a, d, z = enter(dve, "dve", "mix")
            with dve.Fori(0, KD // 2) as i:
                for m, x in enumerate("ab"):
                    u = i * 6 + (U0["mix"] + 3 * m)
                    ga, gb = fx[:, 3 + 2 * m, :], fx[:, 4 + 2 * m, :]
                    dve.wait_ge(unit_done, u + 1)
                    mul(d, f"ga{x}", ga, ps[4 * m][:, :], rs)
                    dve.wait_ge(unit_done, u + 2)
                    mul(d, f"gb{x}", gb, ps[4 * m + 1][:, :], rs)
                    dve.wait_ge(unit_done, u + 3)
                    sync(a, f"sa{x}", i)
                    mul(d, f"ma{x}", ga, ps[4 * m + 2][:, :], ga)
                    sync(a, f"sb{x}", i)
                    mul(d, f"mb{x}", gb, ps[4 * m + 3][:, :], gb)
                    sync(d, f"mb{x}", i)
                    add(d, f"mx{x}", ga, ga, gb)
                    sync(a, f"hi{x}", i)
                    lo(d, f"lo{x}", at(mix_lo, i * 2 + m), ga, at(mix_hi, i * 2 + m))

            a, d, z = enter(dve, "dve", "wo")
            clear(acc)
            with dve.Fori(0, KD // 2) as i:
                for m, x in enumerate("ab"):
                    sync(a, f"sq{x}", i)
                    add(d, f"acc{x}", acc, acc, sqs(m))
                    sync(d, f"acc{x}", i)

            def post_norm(a, d, f, g):
                sync(a, "sqrt")
                d.done(dve.reciprocal(rs, rs), "rs")
                sync(d, "rs")

                def update(m):
                    stt(d, f"sc{m}", f[:, m], f[:, m], gcol(g, m), rs, ALU.mult, ALU.mult)
                    sync(d, f"sc{m}")
                    add(d, f"h{m}", h[:, m], h[:, m], f[:, m])

                update(0)
                return update

            def split_p(a, d):
                for n in range(2):
                    sync(a, f"ph{n}")
                    lo(d, f"pl{n}", p_lo[:, n], p_raw[n], p_hi[:, n])

            a, d, z = enter(dve, "dve", "res1")
            split_p(a, d)
            update = post_norm(a, d, fbuf, "g_mix_post")
            for m in M8:
                if m < KD - 1:
                    update(m + 1)
                sync(a, f"hi{m}")
                stt(d, f"lo{m}", op_lo[:, m], h[:, m], gcol("g_ffn_pre", m), op_hi[:, m].bitcast(F32), ALU.mult, ALU.subtract)
                sync(a, f"sq{m}")
                accumulate(d, f"acc{m}", m == 0, sqs(m))
                sync(d, f"acc{m}")
            sync(a, "sqrt2")
            d.done(dve.reciprocal(rs, rs), "rs2")

            for half in (0, 1):
                name = f"up{half}"
                a, d, z = enter(dve, "dve", name)

                def ffn_block(i, ready, banks):
                    for n, x in enumerate("gv"):
                        c, y = fx[:, 3 + n, :], fx[:, 5 + n, :]
                        blk = i + (half * HJ + n * JF)
                        dve.wait_ge(unit_done, ready[n])
                        mul(d, x, c, ps[banks + n][:, :], rs)
                        sync(d, x, i)
                        d.done(dve.tensor_scalar(y, c, gcol("conv_ffn_w", blk + 4 * JF), gcol("b_ffn_conv", blk), ALU.mult, ALU.add), f"{x}0")
                        sync(d, f"{x}0", i)
                        stt(d, f"{x}1", y[:, 1:T], c[:, 0:T - 1], gcol("conv_ffn_w", blk + 2 * JF), y[:, 1:T], ALU.mult, ALU.add)
                        sync(d, f"{x}1", i)
                        stt(d, f"{x}2", y[:, 2:T], c[:, 0:T - 2], gcol("conv_ffn_w", blk), y[:, 2:T], ALU.mult, ALU.add)
                    sync(d, "v2", i)
                    sync(a, "ge", i)
                    mul(d, "pr", fx[:, 6, :], fx[:, 5, :], fx[:, 6, :])
                    sync(a, "hi", i)
                    lo(d, "lo", at(f_lo, i), fx[:, 6, :], at(f_hi, i))

                if half == 0:
                    for i in range(2):
                        ffn_block(i, [U0[name] + 4] * 2, 2 * i)
                first = 1 if half else 3
                ffn_block(first - 1, [U0[name] + 2 * (first - 1) + n + 1 for n in range(2)], 4)
                with dve.Fori(0, (HJ - first) // 2) as i:
                    for e in range(2):
                        blk = i * 2 + (first + e)
                        ffn_block(blk, [blk * 2 + (U0[name] + n + 1) for n in range(2)], 4 if e else 6)
                name = f"down{half}"
                a, d, z = enter(dve, "dve", name)
                if half:
                    clear(acc)
                    with dve.Fori(0, 2) as i:
                        for m in range(4):
                            dve.wait_ge(unit_done, i * 6 + (U0[name] + 3 * (m // 2) + 2 + m % 2))
                            fm = at(fbuf, i * 4 + m)
                            add(d, f"f{m}", fm, fm, ps[m][:, :])
                            sync(a, f"sq{m}", i)
                            add(d, f"acc{m}", acc, acc, sqs(m))
                            sync(d, f"acc{m}", i)

            def ple_gate(k):
                a, d, z = enter(dve, "dve", f"ple{k}")
                if k == 1:
                    clear(acc)
                for m in M8:
                    i, x = m // 2, "ab"[m % 2]
                    e = ebuf[:, m]
                    sync(a, f"g{x}", i)
                    mul(d, f"e{x}", e, e, fx[:, 3 + m % 2, :])
                    if k == 1:
                        sync(a, f"sq{x}", i)
                        add(d, f"acc{x}", acc, acc, sqs(m))
                        sync(d, f"acc{x}", i)
                    else:
                        sync(d, f"e{x}", i)
                        add(d, f"h{x}", h[:, m], h[:, m], e)
                    if k == 2:
                        sync(d, f"h{x}", i)
                        d.done(dve.tensor_scalar(fbuf[:, m], h[:, m], ALPHA, None, ALU.mult), f"t{x}")
                        sync(a, f"hi{x}", i)
                        lo(d, f"lo{x}", x2_lo[:, m], h[:, m], x2_hi[:, m])

            def residual(name, f, g):
                a, d, z = enter(dve, "dve", name)
                update = post_norm(a, d, f, g)
                for m in M8:
                    if m < KD - 1:
                        update(m + 1)
                    sync(a, f"hi{m}")
                    lo(d, f"lo{m}", op_lo[:, m], h[:, m], op_hi[:, m])

            residual("res2", fbuf, "g_ffn_post")
            ple_gate(1)
            residual("res3", ebuf, "g_ple_post")

            a, d, z = enter(dve, "dve", "gla_a")
            d.done(dve.tensor_scalar(fbuf.rearrange("p k t -> p (k t)"), h.rearrange("p k t -> p (k t)"), ALPHA, None, ALU.mult), "zero_y")
            sync(a, "ah")
            lo(d, "al", ga_lo[:, 0], ps[4][:, :], ga_hi[:, 0])
            for m in M8:
                sync(a, f"ab{m}")
                d.done(dve.tensor_scalar(fx[:, 3 + m, :], ps[4 + (m + 1) % 4][:, :], gcol("gla_b_a_2", m), 0.0, ALU.add, ALU.min), f"mn{m}")
            for m in M8:
                sync(a, f"ln{m}")
                sync(d, f"mn{m}")
                d.done(dve.tensor_tensor(ebuf[:, m], fx[:, 3 + m, :], ebuf[:, m], ALU.subtract), f"g{m}")
            sync(d, "g7")
            d.done(dve.memset(fx[:, 9:12, :], 0.0), "zero_at")

            g64, gl = fx[:, 3, :], fx[:, 4, :]
            ex, tm = fx[:, 5:7, :].rearrange("p k t -> p (k t)"), fx[:, 7:9, :].rearrange("p k t -> p (k t)")
            atf = fx[:, 9:12, :].rearrange("p k t -> p (k t)")
            gsq = sweep((2, 0))

            def gla_head(name, i, i0, last):
                a, d, z = S[name]["act"], S[name]["dve"], S[name]["pe"]
                base = i * 16 + U0[name]

                def prep(b):
                    g = at(ebuf, i0 * 2 + b)
                    if b:
                        sync(a, "x0j3", i)
                    d.done(dve.tensor_tensor_scan(g64, const("reset"), g, 0.0, ALU.mult, ALU.add), f"s64{b}")
                    d.done(dve.tensor_tensor_scan(gl, const("ones"), g, 0.0, ALU.mult, ALU.add), f"sgl{b}")
                    sync(d, f"sgl{b}", i)
                    ends = gl.rearrange("p (j t) -> p j t", t=P)[:, :, P - 1]
                    d.done(dve.tensor_scalar(st[:, 8 * b:8 * b + 4], ends, -1.0 / GATE_NORM, None, ALU.mult), f"ne{b}")
                    d.done(dve.tensor_scalar(st[:, 8 * b + 4:8 * b + 8], ends, 1.0 / GATE_NORM, None, ALU.mult), f"po{b}")
                    for n, (name, src) in enumerate((("qt", h[:, b]), ("kt", h[:, 2 + b]), ("ks", h[:, 2 + b]))):
                        if n == 0:
                            dve.wait_ge(a.sem, a.credit if last else a.at("k1", i - 1))
                        sync(a, f"x{b}{name}" if n < 2 else f"x{b}s{QT - 1}", i)
                        if n:
                            sync(d, f"l{b}{('qt', 'kt')[n - 1]}", i)
                        mul(d, f"m{b}{name}", tm[:, 0:T], src, ex[:, 0:T])
                        sync(a, f"h{b}{name}", i)
                        lo(d, f"l{b}{name}", ga_lo[:, n], tm[:, 0:T], ga_hi[:, n])
                    for j in range(QT):
                        q0, n = q_span(j)
                        if j == 0:
                            sync(d, f"l{b}ks", i)
                        sync(a, f"x{b}j{j}", i)
                        mul(d, f"m{b}j{j}", tm[:, q0:q0 + n], h[:, b, T - n:T], ex[:, q0:q0 + n])
                    sync(a, f"h{b}qj", i)
                    lo(d, f"l{b}qj", ga_lo[:, 3:5].rearrange("p k t -> p (k t)"), tm, ga_hi[:, 3:5].rearrange("p k t -> p (k t)"))

                prep(0)
                for t in range(QT):
                    sync(a, f"vh{t}", i)
                    lo(d, f"vl{t}", gv_lo[:, t], ps[4 + t][:, :], gv_hi[:, t])
                prep(1)
                sync(z, "A1", i)
                dve.sem_inc(dve_held, 1)
                for j in range(QT):
                    o = GLA_PACK[j]
                    d.done(dve.copy_predicated(atf[:, o:o + P], const("tri").bitcast(U32), ps[4][:, j * P:(j + 1) * P]), f"ad{j}")
                for j in range(QT):
                    o = GLA_PACK[j]
                    q0, n = q_span(j)
                    bank, c = GLA_BANK[j]
                    sync(d, f"ad{j}", i)
                    d.done(dve.tensor_copy(atf[0:CHUNK, o + CHUNK:o + P], ps[bank][0:CHUNK, c:c + CHUNK]), f"ac{j}")
                    if j < QT - 1:
                        d.done(dve.tensor_copy(atf[:, o + P:o + T - j * P], ps[bank][:, c + CHUNK:c + n]), f"ao{j}")
                sync(a, "ath", i)
                lo(d, "atl", at_lo.rearrange("p k t -> p (k t)")[:, 0:GLA_AT], atf[:, 0:GLA_AT],
                   at_hi.rearrange("p k t -> p (k t)")[:, 0:GLA_AT])
                for b in range(4):
                    sync(a, f"osq{b}", i)
                    accumulate(d, f"oacc{b}", b == 0, gsq(b))
                    sync(d, f"oacc{b}", i)
                    t = h[:, 4 + b]
                    stt(d, f"on{b}", t, t, gcol("gla_gn_g_2", i0 * 4 + b), ps[b][:, :], ALU.mult, ALU.mult)
                sync(a, "osqrt", i)
                d.done(dve.reciprocal(rs, rs), "ors")
                sync(d, "ors", i)

                def normalise(b):
                    mul(d, f"oz{b}", h[:, 4 + b], h[:, 4 + b], rs)

                normalise(0)
                for b in range(4):
                    if b < 3:
                        normalise(b + 1)
                    sync(a, f"oh{b}", i)
                    lo(d, f"ol{b}", go_lo[:, b], h[:, 4 + b], go_hi[:, b])
                first = 8 if last else 12
                for m in M8:
                    if m % 2 == 0:
                        sync(z, f"y{m}", i)
                    else:
                        dve.wait_ge(unit_done, base + (first + m // 2 + 1))
                    add(d, f"y{m}", fbuf[:, m], fbuf[:, m], ps[m % 4][:, :])
                    if last:
                        sync(d, f"y{m}", i)
                        accumulate(d, f"s{m}", m == 0, fbuf[:, m])
                        sync(d, f"s{m}", i)

            enter(dve, "dve", "gla", ())
            with dve.Fori(0, GH - 1) as i:
                gla_head("gla", i, i, False)
            enter(dve, "dve", "gla_end", ())
            gla_head("gla_end", 0, GH - 1, True)

            def layer_norm(name, k):
                a, d, z = enter(dve, "dve", name)
                split_p(a, d)
                sync(a, "mu")

                def centre(m):
                    d.done(dve.tensor_tensor(fbuf[:, m], fbuf[:, m], fx[:, 3, :], ALU.subtract), f"c{m}")

                centre(0)
                for m in M8:
                    if m < KD - 1:
                        centre(m + 1)
                    sync(a, f"sq{m}")
                    accumulate(d, f"v{m}", m == 0, sqs(m))
                    sync(d, f"v{m}")
                sync(a, "sqrt")
                d.done(dve.reciprocal(rs, rs), "rs")
                sync(d, "rs")

                def normalise(m):
                    mul(d, f"n{m}", fbuf[:, m], fbuf[:, m], rs)
                    sync(d, f"n{m}")
                    d.done(dve.tensor_scalar(h[:, m], fbuf[:, m], gcol("ln_g_2", k * KD + m), gcol("ln_b_2", k * KD + m),
                                             ALU.mult, ALU.add), f"x{m}")

                normalise(0)
                for m in M8:
                    if m < KD - 1:
                        normalise(m + 1)
                    sync(a, f"hi{m}")
                    lo(d, f"lo{m}", op_lo[:, m], h[:, m], op_hi[:, m])

            layer_norm("ln1", 0)
            ple_gate(2)

            a, d, z = enter(dve, "dve", "idx")
            for n, tile in enumerate((ki_hi[:, 0], ki_hi[:, 1], ki_lo[:, 0], ki_lo[:, 1])):
                d.done(dve.tensor_scalar(tile, const("ones"), 0.0, None, ALU.mult), f"zero{n}")
            for b in range(6):
                f = fx[:, 9 + b % 2, :]
                sync(a, f"qf{b}")
                rows, table, half = (slice(0, P), 2, ID // 8) if b < 5 else (slice(0, 32), 1, DHD // 8)
                for step in ("sw", "qc", "ss", "qa"):
                    rotate(d, step, str(b), 0, f, fx[:, 11, :], table, rows, half)
                if b < 4:
                    sync(a, f"hi{b}")
                    lo(d, f"lo{b}", qi_lo[:, b], f, qi_hi[:, b])
                elif b == 4:
                    sync(a, "kih0")
                    lo(d, "kil0", ki_lo[0:64, 0], f[0:64, :], ki_hi[0:64, 0])
                    sync(a, "kih1")
                    lo(d, "kil1", ki_lo[64:128, 1], f[64:128, :], ki_hi[64:128, 1])
                else:
                    sync(a, "kh")
                    lo(d, "kl", dk_lo[:, 0], f, dk_hi[:, 0])
            sync(a, "vh")
            lo(d, "vl", dv_lo[:, 0], ps[2][:, :], dv_hi[:, 0])
            sync(a, "wi")
            for n, (q, x) in enumerate(pairs):
                w = P * (q + 1)
                sync(a, f"rel{q}{x}")
                s, rel, wt = fx[:, 3 + q, 0:w], fx[:, 7 + n % 2, 0:w], st[:, q * IH + x:q * IH + x + 1]
                if x == 0:
                    d.done(dve.tensor_scalar(s, rel, wt, None, ALU.mult), f"sc{q}{x}")
                else:
                    stt(d, f"sc{q}{x}", s, rel, wt, s, ALU.mult, ALU.add)
                sync(d, f"sc{q}{x}")
            for q in range(1, QT):
                s = fx[:, 3 + q, q * P:(q + 1) * P]
                add(d, f"ca{q}", s, s, const("causal")[:, T - P:T])
            for q in range(1, QT):
                s = fx[:, 3 + q, 0:P * (q + 1)]
                sync(d, f"ca{q}")
                for r in range(TOPK // 8):
                    d.done(dve.max(st[:, 32:40], s), f"mx{q}_{r}")
                    sync(d, f"mx{q}_{r}")
                    d.done(dve.match_replace(s, st[:, 32:40], s, TAKEN), f"mr{q}_{r}")
                    sync(d, f"mr{q}_{r}")
            for q in range(1, QT):
                s = fx[:, 3 + q, 0:P * (q + 1)]
                d.done(dve.tensor_scalar(s, s, 0.5 * TAKEN, MASKED, ALU.is_gt, ALU.mult), f"sel{q}")

            enter(dve, "dve", "dsa_z", ())
            def dsa_chore(a, d, x, hh, i, k):
                def turn(step):
                    rotate(d, step, x, i, dsa_query_tile(hh), fx[:, 11, :], 1, slice(0, 32), DHD // 8)

                if k == 0:
                    sync(a, f"qf{x}", i)
                    turn("sw")
                elif k == 2:
                    turn("qc")
                elif k == 3:
                    turn("ss")
                    turn("qa")
                    sync(a, f"qh{x}", i)
                    lo(d, f"ql{x}", dq_lo[:, 0], dsa_query_tile(hh), dq_hi[:, 0])

            def dsa_heads(name, half, i, i0, last):
                a, d, z = S[name]["act"], S[name]["dve"], S[name]["pe"]
                for hh, x in enumerate("ab"):
                    def chore(k):
                        if not (last and hh):
                            dsa_chore(a, d, x, 1 - hh, i, k)

                    def parts(q):
                        t = slice(q * P, (q + 1) * P)
                        turned = ps[5 + q % 2][:, 0:P * (q + 1)].rearrange("p (k t) -> p k t", t=P)
                        return dpt_lo[:, 0:q + 1, t], turned, dpt_hi[:, 0:q + 1, t]

                    softmax(S[name], x, i, dsa_probs, parts,
                            lambda q: fx[:, 3 + q, 0:P * (q + 1)] if q else const("causal")[:, T - P:T], DSA_SCALE, chore)
                    sync(z, f"o{x}", i)
                    mul(d, f"oz{x}", acc, ps[7][:, :], at(fb, i0 * 2 + (hh + half * DH // 2)))
                    sync(d, f"oz{x}", i)
                    d.done(dve.tensor_scalar(at(oz_hi, i0 * 2 + hh), acc, 1.0, None, ALU.mult), f"oh{x}")
                    sync(d, f"oh{x}", i)
                    lo(d, f"ol{x}", at(oz_lo, i0 * 2 + hh), acc, at(oz_hi, i0 * 2 + hh))

            a, d, z = enter(dve, "dve", "dsa_p")
            for k in range(4):
                dsa_chore(a, d, "", 0, 0, k)
            for half in (0, 1):
                name = f"dsa{half}"
                rounds = DH // 4 - half
                enter(dve, "dve", name)
                with dve.Fori(0, rounds) as i:
                    dsa_heads(name, half, i, i, False)
                if half:
                    enter(dve, "dve", "dsa1_end")
                    dsa_heads("dsa1_end", half, 0, rounds, True)
                name = f"dout{half}"
                a, d, z = enter(dve, "dve", name)
                if half:
                    clear(acc)
                with dve.Fori(0, KD // 2) as i:
                    for m, x in enumerate("ab"):
                        dve.wait_ge(unit_done, i * 2 + (U0[name] + m + 1))
                        f = at(fbuf, i * 2 + m)
                        add(d, f"f{x}", f, f, ps[5 + m][:, :])
                        if half:
                            sync(d, f"f{x}", i)
                            add(d, f"acc{x}", acc, acc, f)
            layer_norm("ln2", 1)
            ple_gate(3)

    return nc


def blocks_of(w, rows, cols):
    return w[rows, cols].reshape(-1, P, w[rows, cols].shape[1]).transpose(1, 0, 2)


def weight_units(a):
    units = []

    def put(*parts):
        u = np.zeros((P, 8 * P), np.float32)
        at = 0
        for x in parts:
            x = x.reshape(P, -1)
            u[:, at:at + x.shape[1]] = x
            at += x.shape[1]
        units.append(u)

    def col(w, c, n=P):
        return blocks_of(w, slice(None), slice(c, c + n))

    def wide(w, pieces):
        x = np.zeros((w.shape[0], P), np.float32)
        for at, c, n in pieces:
            x[:, at:at + n] = w[:, c:c + n]
        return col(x, 0)

    def blockwise(four):
        for c in range(4):
            put(*[x[:, 2 * c + kk:2 * c + kk + 1] for kk in range(2) for x in four])

    def projection(proj):
        for m in range(0, KD, 4):
            put(*[col(proj, (m + n) * P) for n in range(4)])

    def gate(w):
        blockwise([col(w, m * P) for m in range(4)])
        for m in range(4, KD):
            put(col(w, m * P))

    w = a["w_in"][0]
    c_q = 3 * CONV
    c_kv = c_q + QL
    c_r = c_kv + KVL
    c_ga = c_r + ROPE
    blockwise([col(w, c_q + b * P) for b in range(4)])
    for b in range(4, (QL + KVL) // P):
        put(col(w, c_q + b * P))
    put(wide(w, [(0, c_r, ROPE), (64, c_r, ROPE)]))
    wq, wkv = a["w_q_up"][0], a["w_kv_up"][0]
    for n in range(NH):
        q, k = n * (NOPE + ROPE), n * (NOPE + VD)
        if n % 2 == 0:
            put(wide(wq, [(0, q + NOPE, ROPE), (64, q, NOPE)]), wide(wkv, [(0, k + NOPE, VD), (64, k, NOPE)]))
        else:
            put(wide(wq, [(0, q, NOPE), (64, q + NOPE, ROPE)]), wide(wkv, [(0, k, NOPE), (64, k + NOPE, VD)]))
    for j in range(JC):
        for part in (1, 2, 0):
            put(col(w, part * CONV + j * P))
    for m in range(KD):
        put(col(w, c_ga + m * P))
        put(col(w, c_ga + D + m * P))
        put(col(a["w_a_out"][0], m * P), col(a["w_b_out"][0], m * P))
    for m in range(KD):
        put(col(a["w_o"][0], m * P))
    projection(a["w_ple_proj"][0])
    w = a["w_ffn_up"][0]
    for half in range(2):
        first = half * HJ
        if half == 0:
            blockwise([col(w, c) for j in range(2) for c in (j * P, DFF + j * P)])
            first = 2
        for j in range(first, (half + 1) * HJ):
            put(col(w, j * P))
            put(col(w, DFF + j * P))
        down = a["w_ffn_down"][0][half * HJ * P:(half + 1) * HJ * P]
        for m in range(0, KD, 2):
            both = np.concatenate([col(down, m * P), col(down, (m + 1) * P)], axis=1)
            for v in range(3):
                put(both[:, 8 * v:8 * v + 8])

    gate(a["w_ple_gate"][0])
    w = a["gla_w_in_2"][0]
    qk = GH * GDK

    def queries_keys(n):
        return [col(w, c) for c in (n * GDK, n * GDK + P, qk + n * GDK, qk + n * GDK + P)]

    blockwise(queries_keys(0))
    put(wide(w, [(0, 2 * qk + 2 * DI, GRANK)]))
    up = np.zeros((P, D), np.float32)
    up[:GRANK] = a["gla_w_a2_2"][0]
    put(up)
    for n in range(GH):
        v = col(w, 2 * qk + n * GDV, GDV)
        for c in range(4):
            put(v[:, 2 * c:2 * c + 2])
        for b in range(4):
            put(col(w, 2 * qk + DI + n * GDV + b * P))
        if n < GH - 1:
            for x in queries_keys(n + 1):
                put(x)
        rows = a["gla_w_out_2"][0][n * GDV:(n + 1) * GDV]
        for m in range(0, KD, 2):
            put(col(rows, m * P), col(rows, (m + 1) * P))
    projection(a["ple_w_2"][0])
    gate(a["ple_gate_w_2"][0])
    w = a["dsa_w_in_2"][0]
    c_k, c_v, c_z = DI, DI + DHD, DI + 2 * DHD
    c_qi = c_z + DI
    c_ki = c_qi + IH * ID
    c_wi = c_ki + ID
    for b in range(4):
        put(col(w, c_qi + b * P))
    put(wide(w, [(0, c_ki, ID), (ID, c_ki, ID)]))
    put(col(w, c_k))
    put(col(w, c_v))
    put(wide(w, [(0, c_wi, IH)]))
    for n in range(DH):
        put(col(w, c_z + n * P))
    for half, heads in enumerate((range(DH // 2 + 2), range(DH // 2 + 2, DH))):
        for n in heads:
            put(col(w, n * P))
        rows = a["dsa_w_out_2"][0][half * D:(half + 1) * D]
        for m in range(KD):
            put(col(rows, m * P))
    projection(a["ple_w_2"][1])
    gate(a["ple_gate_w_2"][1])
    assert len(units) == UNITS, (len(units), UNITS)
    return np.stack(units)


def constants():
    c = np.zeros((P, CONSTS), np.float32)

    def put(name, x):
        c[:, C0[name]:C0[name] + x.shape[1]] = x

    r = np.arange(P)
    put("ident", np.eye(P, dtype=np.float32))
    put("ones", np.ones((P, T), np.float32))
    mla, causal = np.zeros((P, T), np.float32), np.zeros((P, T), np.float32)
    mla[:, T - P:] = np.where(r[None, :] // CHUNK <= r[:, None] // CHUNK, 0.0, MASKED)
    causal[:, T - P:] = np.where(r[None, :] <= r[:, None], 0.0, MASKED)
    put("mla_bias", mla)
    put("causal", causal)
    put("tri", ((r[:, None] <= r[None, :]) & (r[:, None] // CHUNK == r[None, :] // CHUNK)).astype(np.float32))
    put("reset", np.broadcast_to(np.arange(T) % CHUNK != 0, (P, T)).astype(np.float32))

    def frequencies(theta, rot, period):
        half = rot // 2
        inv = (np.float32(1.0) / np.float32(theta) ** (np.arange(half, dtype=np.float32) * np.float32(2.0 / rot))).astype(np.float32)
        f, s = np.zeros(P, np.float32), np.ones(P, np.float32)
        on = r % period < rot
        f[on] = inv[(r[on] % period) % half]
        s[on] = np.where(r[on] % period < half, -1.0, 1.0)
        return f, s

    tables = [frequencies(THETA_1, ROPE, 32), frequencies(THETA_2, DHD // 4, 32), frequencies(THETA_2, ID // 4, ID)]
    put("inv_freq", np.stack([f for f, _ in tables], axis=1))
    put("sign", np.stack([s for _, s in tables], axis=1))
    put("eps", np.full((P, 1), EPS, np.float32))
    put("eps_ln", np.full((P, 1), NORM_EPS, np.float32))
    put("one", np.ones((P, 1), np.float32))
    return c


def arrays_of(a):
    def columns(x):
        return x.reshape(-1, P).T

    def turned(x):
        return np.ascontiguousarray(np.swapaxes(x, -1, -2)).reshape(-1, P, T)

    gains = np.concatenate([columns(np.asarray(a[name])) for name, _ in GAIN_COLS], axis=1)
    return {"x": turned(a["x"][0]), "p": turned(a["p"][0, 0]), "p_2": turned(a["p_2"][:, 0]),
            "positions": np.ascontiguousarray(a["positions"]), "positions_2": np.ascontiguousarray(a["positions_2"]),
            "gains": np.ascontiguousarray(gains), "consts": constants(), "weights": weight_units(a)}


def kernel(**inputs):
    import concourse.bacc as bacc
    from concourse.bass_utils import run_bass_kernel_spmd

    arrays = arrays_of({n: np.asarray(x) for n, x in inputs.items()})
    nc = bacc.Bacc("TRN2", target_bir_lowering=False, num_devices=1, dynamic_dma_scratch_size=1024)
    ins = {n: nc.dram_tensor(f"in_{n}", x.shape, mybir.dt.from_np(x.dtype), kind="ExternalInput").ap() for n, x in arrays.items()}
    out = nc.dram_tensor("out_0", (KD, P, T), F32, kind="ExternalOutput").ap()
    build(nc, ins, out)
    r = run_bass_kernel_spmd(nc, [{f"in_{n}": x for n, x in arrays.items()}], core_ids=[0])
    return np.ascontiguousarray(r.results[0]["out_0"].reshape(D, T).T).reshape(1, T, D)
```
